# Optimizing a Trainium2 kernel written in Bass

```python
import math
import jax, jax.numpy as jnp
from jax import lax
import numpy as np

D_MODEL = 1024
BATCH = 1
SEQ = 1024
DEPTH = 1

D_RNN = 1024
LRU_BLOCKS = 8
LRU_BW = D_RNN // LRU_BLOCKS
CONV_W = 4
LRU_C = 8.0
N_HEADS = 8
HEAD_DIM = 64
ATT_QK = N_HEADS * 2 * HEAD_DIM
ATT_V = N_HEADS * 2 * HEAD_DIM
Q_BLOCK = 128
N_EXPERTS = 64
TOP_K = 8
N_GROUPS = 8
TOPK_GROUPS = 4
D_EXPERT = 256
D_SHARED = 256
ROUTED_SCALE = 2.5
MOE_BLOCK = 128
EPS = 1e-6
W_IN = 2 * D_RNN + 2 * ATT_QK + ATT_V + 2 * D_MODEL

kernel_name = "hybrid_rglru_diffattn_moe_block"

def rms_norm(x, g):
    xf = x.astype(jnp.float32)
    y = xf * lax.rsqrt(jnp.mean(xf * xf, axis=-1, keepdims=True) + EPS)
    return (y * g).astype(x.dtype)

def modulate(h, shift, scale):
    return h * (1.0 + scale) + shift

def lambda_init(layer):
    return 0.8 - 0.6 * math.exp(-0.3 * layer)

def causal_dwconv(x, w, b):
    y = lax.conv_general_dilated(
        x, w[:, None, :].astype(x.dtype), window_strides=(1,),
        padding=[(CONV_W - 1, 0)], dimension_numbers=("NWC", "WIO", "NWC"),
        feature_group_count=x.shape[-1])
    return y + b

def rg_lru(x, wa, ba, wx, bx, lam):
    B, S, C = x.shape
    xb = x.reshape(B, S, LRU_BLOCKS, LRU_BW)
    r = jax.nn.sigmoid(jnp.einsum("bsnc,ncd->bsnd", xb, wa) + ba).reshape(B, S, C)
    i = jax.nn.sigmoid(jnp.einsum("bsnc,ncd->bsnd", xb, wx) + bx).reshape(B, S, C)
    log_a = (-LRU_C * jax.nn.softplus(-lam) * r).astype(jnp.float32)
    a = jnp.exp(log_a)
    mult = jnp.sqrt(-jnp.expm1(2.0 * log_a))
    first = (jnp.arange(S) == 0)[None, :, None]
    mult = jnp.where(first, 1.0, mult)
    u = mult * (i * x).astype(jnp.float32)

    def combine(lhs, rhs):
        a1, b1 = lhs
        a2, b2 = rhs
        return a1 * a2, a2 * b1 + b2

    _, h = lax.associative_scan(combine, (a, u), axis=1)
    return h.astype(x.dtype)

def diff_attention(q, k, v, lam):
    B, S = q.shape[0], q.shape[1]
    n_blk = S // Q_BLOCK
    scale = HEAD_DIM ** -0.5
    slopes = jnp.exp2(-8.0 * jnp.arange(1, N_HEADS + 1, dtype=jnp.float32) / N_HEADS)
    qb = q.reshape(B, n_blk, Q_BLOCK, N_HEADS, 2, HEAD_DIM).transpose(1, 0, 2, 3, 4, 5)
    pos_k = jnp.arange(S)

    def one_block(args):
        qi, bi = args
        pos_q = bi * Q_BLOCK + jnp.arange(Q_BLOCK)
        s = jnp.einsum("bqhmd,bkhmd->bhmqk", qi, k).astype(jnp.float32) * scale
        dist = (pos_q[:, None] - pos_k[None, :]).astype(jnp.float32)
        bias = -slopes[:, None, None, None] * dist
        s = jnp.where(dist >= 0, s + bias, -jnp.inf)
        p = jax.nn.softmax(s, axis=-1)
        attn = p[:, :, 0] - lam * p[:, :, 1]
        return jnp.einsum("bhqk,bkhe->bqhe", attn.astype(v.dtype), v)

    o = lax.map(one_block, (qb, jnp.arange(n_blk)))
    return o.transpose(1, 0, 2, 3, 4).reshape(B, S, N_HEADS, 2 * HEAD_DIM)

def hybrid_mixer(h, w_in, conv_w, conv_b, lru_wa, lru_ba, lru_wx, lru_bx, lru_lambda,
                 lam_q1, lam_k1, lam_q2, lam_k2, g_subln, w_proj_rnn, w_proj_att, w_out,
                 lam_init):
    B, S, _ = h.shape
    proj = h @ w_in
    cuts = [int(s) for s in np.cumsum([D_RNN, D_RNN, ATT_QK, ATT_QK, ATT_V, D_MODEL])]
    xr, gr, q, k, v, ga, gb = jnp.split(proj, cuts, axis=-1)
    xr = causal_dwconv(xr, conv_w, conv_b)
    yr = rg_lru(xr, lru_wa, lru_ba, lru_wx, lru_bx, lru_lambda) * jax.nn.gelu(gr)
    ya = yr @ w_proj_rnn
    q = q.reshape(B, S, N_HEADS, 2, HEAD_DIM)
    k = k.reshape(B, S, N_HEADS, 2, HEAD_DIM)
    v = v.reshape(B, S, N_HEADS, 2 * HEAD_DIM)
    lam = (jnp.exp(jnp.sum(lam_q1 * lam_k1)) - jnp.exp(jnp.sum(lam_q2 * lam_k2)) + lam_init)
    o = diff_attention(q, k, v, lam.astype(jnp.float32))
    o = rms_norm(o, g_subln) * (1.0 - lam_init)
    yb = o.reshape(B, S, ATT_V) @ w_proj_att
    merged = jax.nn.sigmoid(ga) * ya + jax.nn.sigmoid(gb) * yb
    return merged @ w_out

def moe_ffn(xf, w_router, e_bias, w1_e, w3_e, w2_e, w1_s, w3_s, w2_s):
    T, D = xf.shape
    scores = jax.nn.sigmoid((xf @ w_router).astype(jnp.float32))
    choice = scores + e_bias.astype(jnp.float32)
    per_g = N_EXPERTS // N_GROUPS
    grp_score = lax.top_k(choice.reshape(T, N_GROUPS, per_g), 2)[0].sum(-1)
    _, top_g = lax.top_k(grp_score, TOPK_GROUPS)
    gmask = jax.nn.one_hot(top_g, N_GROUPS, dtype=jnp.float32).sum(1) > 0
    choice = jnp.where(jnp.repeat(gmask, per_g, axis=1), choice, -jnp.inf)
    _, top_e = lax.top_k(choice, TOP_K)
    wts = jnp.take_along_axis(scores, top_e, axis=1)
    wts = wts / (wts.sum(-1, keepdims=True) + 1e-20) * ROUTED_SCALE

    A = T * TOP_K
    flat_e = top_e.reshape(A)
    order = jnp.argsort(flat_e)
    sorted_e = flat_e[order]
    counts = jnp.bincount(flat_e, length=N_EXPERTS)
    padded = (counts + MOE_BLOCK - 1) // MOE_BLOCK * MOE_BLOCK
    p_end = jnp.cumsum(padded)
    p_start = p_end - padded
    s_start = jnp.cumsum(counts) - counts
    dest = p_start[sorted_e] + (jnp.arange(A) - s_start[sorted_e])
    P = A + N_EXPERTS * MOE_BLOCK
    n_blocks = P // MOE_BLOCK
    slot_tok = jnp.full((P,), T, dtype=jnp.int32).at[dest].set((order // TOP_K).astype(jnp.int32))
    slot_w = jnp.zeros((P,), jnp.float32).at[dest].set(wts.reshape(A)[order])
    block_e = jnp.minimum(jnp.searchsorted(p_end, jnp.arange(n_blocks) * MOE_BLOCK, side="right"),
                          N_EXPERTS - 1)
    x_pad = jnp.concatenate([xf, jnp.zeros((1, D), xf.dtype)], axis=0)

    def body(acc, blk):
        tok, wt, e = blk
        xb = x_pad[tok]
        hb = jax.nn.silu(xb @ w1_e[e]) * (xb @ w3_e[e])
        yb = (hb @ w2_e[e]) * wt[:, None].astype(xb.dtype)
        return acc.at[tok].add(yb.astype(acc.dtype)), None

    acc0 = jnp.zeros((T + 1, D), xf.dtype)
    acc, _ = lax.scan(body, acc0, (slot_tok.reshape(n_blocks, MOE_BLOCK),
                                   slot_w.reshape(n_blocks, MOE_BLOCK), block_e))
    shared = (jax.nn.silu(xf @ w1_s) * (xf @ w3_s)) @ w2_s
    return acc[:T] + shared

def setup_inputs(seed: int = 0) -> dict:
    key = jax.random.key(seed)
    ks = iter(jax.random.split(key, 48))
    L, D = DEPTH, D_MODEL

    def nrm(shape, fan_in):
        return jax.random.normal(next(ks), shape, jnp.float32) * fan_in ** -0.5

    def gain(shape):
        return 1.0 + 0.05 * jax.random.normal(next(ks), shape, jnp.float32)

    def small(shape, s=0.02):
        return s * jax.random.normal(next(ks), shape, jnp.float32)

    x = jax.random.normal(next(ks), (BATCH, SEQ, D), jnp.float32)
    c = jax.random.normal(next(ks), (BATCH, D), jnp.float32)
    w_ada = nrm((L, D, 6 * D), D)
    b_ada = small((L, 6 * D))
    g_pre_mix = gain((L, D))
    w_in = nrm((L, D, W_IN), D)
    conv_w = nrm((L, CONV_W, D_RNN), CONV_W)
    conv_b = small((L, D_RNN))
    lru_wa = nrm((L, LRU_BLOCKS, LRU_BW, LRU_BW), LRU_BW)
    lru_ba = small((L, LRU_BLOCKS, LRU_BW))
    lru_wx = nrm((L, LRU_BLOCKS, LRU_BW, LRU_BW), LRU_BW)
    lru_bx = small((L, LRU_BLOCKS, LRU_BW))
    a0 = jax.random.uniform(next(ks), (L, D_RNN), jnp.float32, minval=0.9, maxval=0.999)
    lru_lambda = jnp.log(a0) - jnp.log1p(-a0)
    lam_q1 = small((L, HEAD_DIM), 0.1)
    lam_k1 = small((L, HEAD_DIM), 0.1)
    lam_q2 = small((L, HEAD_DIM), 0.1)
    lam_k2 = small((L, HEAD_DIM), 0.1)
    g_subln = gain((L, 2 * HEAD_DIM))
    w_proj_rnn = nrm((L, D_RNN, D), D_RNN)
    w_proj_att = nrm((L, ATT_V, D), ATT_V)
    w_out = nrm((L, D, D), D)
    g_post_mix = gain((L, D))
    g_pre_ffn = gain((L, D))
    w_router = nrm((L, D, N_EXPERTS), D)
    e_bias = small((L, N_EXPERTS), 0.01)
    w1_e = nrm((L, N_EXPERTS, D, D_EXPERT), D)
    w3_e = nrm((L, N_EXPERTS, D, D_EXPERT), D)
    w2_e = nrm((L, N_EXPERTS, D_EXPERT, D), D_EXPERT)
    w1_s = nrm((L, D, D_SHARED), D)
    w3_s = nrm((L, D, D_SHARED), D)
    w2_s = nrm((L, D_SHARED, D), D_SHARED)
    g_post_ffn = gain((L, D))
    return {"x": x, "c": c, "w_ada": w_ada, "b_ada": b_ada, "g_pre_mix": g_pre_mix,
            "w_in": w_in, "conv_w": conv_w, "conv_b": conv_b, "lru_wa": lru_wa,
            "lru_ba": lru_ba, "lru_wx": lru_wx, "lru_bx": lru_bx, "lru_lambda": lru_lambda,
            "lam_q1": lam_q1, "lam_k1": lam_k1, "lam_q2": lam_q2, "lam_k2": lam_k2,
            "g_subln": g_subln, "w_proj_rnn": w_proj_rnn, "w_proj_att": w_proj_att,
            "w_out": w_out, "g_post_mix": g_post_mix, "g_pre_ffn": g_pre_ffn,
            "w_router": w_router, "e_bias": e_bias, "w1_e": w1_e, "w3_e": w3_e,
            "w2_e": w2_e, "w1_s": w1_s, "w3_s": w3_s, "w2_s": w2_s, "g_post_ffn": g_post_ffn}

def reference(x, c, w_ada, b_ada, g_pre_mix, w_in, conv_w, conv_b, lru_wa, lru_ba, lru_wx,
              lru_bx, lru_lambda, lam_q1, lam_k1, lam_q2, lam_k2, g_subln, w_proj_rnn,
              w_proj_att, w_out, g_post_mix, g_pre_ffn, w_router, e_bias, w1_e, w3_e, w2_e,
              w1_s, w3_s, w2_s, g_post_ffn):
    B, S, D = x.shape
    cond = jax.nn.silu(c)
    for l in range(DEPTH):
        mod = cond @ w_ada[l] + b_ada[l]
        sh1, sc1, gt1, sh2, sc2, gt2 = [m[:, None, :] for m in jnp.split(mod, 6, axis=-1)]
        h = modulate(rms_norm(x, g_pre_mix[l]), sh1, sc1)
        y = hybrid_mixer(h, w_in[l], conv_w[l], conv_b[l], lru_wa[l], lru_ba[l], lru_wx[l],
                         lru_bx[l], lru_lambda[l], lam_q1[l], lam_k1[l], lam_q2[l], lam_k2[l],
                         g_subln[l], w_proj_rnn[l], w_proj_att[l], w_out[l], lambda_init(l))
        x = x + gt1 * rms_norm(y, g_post_mix[l])
        h = modulate(rms_norm(x, g_pre_ffn[l]), sh2, sc2)
        y = moe_ffn(h.reshape(B * S, D), w_router[l], e_bias[l], w1_e[l], w3_e[l], w2_e[l],
                    w1_s[l], w3_s[l], w2_s[l]).reshape(B, S, D)
        x = x + gt2 * rms_norm(y, g_post_ffn[l])
    return x


_drawn_inputs = setup_inputs


def setup_inputs(seed=0):
    import zlib

    import numpy as np

    out = dict(_drawn_inputs(seed))
    spreads = {}
    factors = {'lru_ba': 4.196, 'lru_bx': 3.729}
    for name, (base, spread) in spreads.items():
        noise = np.random.default_rng([zlib.crc32(name.encode()), seed]).standard_normal(out[name].shape)
        drawn = base * np.exp(spread * noise) if base else spread * noise
        out[name] = __import__('jax').numpy.asarray(drawn.astype(out[name].dtype))
    for name, factor in factors.items():
        out[name] = (out[name] * factor).astype(out[name].dtype)
    return out
```

```python
import math
import concourse.bass as bass
from concourse import mybir
from contextlib import ExitStack

P = 128
D = 1024
T = 1024
KT = D // P
TT = T // P
NH = 8
HD = 64
HALF = 512
EPS = 1e-6
LRU_C = 8.0
LAM_INIT = 0.8 - 0.6 * math.exp(-0.3 * 0)
MASKED = -1e30
NE = 64
TOP = 8
NG = 8
TOPG = 4
FE = 256
FT = FE // P
ROUTED_SCALE = 2.5
NBLK = T * TOP // P + NE
COL_XR, COL_GR, COL_Q, COL_K, COL_V, COL_GA, COL_GB = (i * D for i in range(7))
STAGE = "full"


def layer(nc, a, out):
    fp32 = mybir.dt.float32
    ACT = mybir.ActivationFunctionType
    ALU = mybir.AluOpType
    AX = mybir.AxisListType
    ds = bass.ds
    ctx = ExitStack()
    with ctx:
        base = 17 * 1024

        def at(name, kb, shape, dt=fp32):
            return nc.alloc_sbuf_tensor_at(name, shape, dt, offset=base + int(kb * 1024))

        def sem(name):
            return ctx.enter_context(nc.semaphore(name))

        hT = at("hT", 0, [P, KT, T])
        xcT = at("xcT", 32, [P, KT, T])
        V = at("V", 32, [P, TT, D])
        oT = at("oT", 32, [P, KT, T])
        ON = at("ON", 64, [P, TT, D])
        Y = at("Y", 64, [P, TT, D])
        gT = at("gateT", 96, [P, KT, T])
        WT = at("WT", 128, [P, 4, KT, P])
        TMP = 144
        xin = at("xin", TMP + 32, [P, 2, D])
        junk = at("junk", TMP + 40, [P, D])
        AW = at("AW", TMP, [P, 2, KT, HALF])
        xpad = at("xpad", TMP, [P, 2, 4 + T])
        rT = at("rT", TMP + 9, [P, T])
        iT = at("iT", TMP + 13, [P, T])
        tT = at("tT", TMP + 17, [P, T])
        aT = at("aT", TMP + 21, [P, T])
        mT = at("mT", TMP + 25, [P, T])
        geT = at("geT", TMP + 29, [P, T])
        hsT = at("hsT", TMP + 33, [P, T])
        ixT = at("ixT", TMP + 37, [P, T])
        GW = at("GW", TMP + 41, [P, 4, 2, P])
        SM = at("SM", TMP, [P, 2, 2, T])
        PT = at("PT", TMP + 16, [P, 2, TT, P])
        qT = at("qT", TMP + 24, [P, 2, T])
        kT = at("kT", TMP + 32, [P, 2, T])
        sq = at("sq", TMP + 32, [P, D])
        sg = at("sg", TMP + 32, [P, 2, T])
        on2 = at("on2", TMP + 16, [P, 2, D])
        ty = at("ty", TMP + 40, [P, T])
        ROWS = at("ROWS", TMP, [P, 4, D])
        h2t = at("h2t", TMP + 16, [P, 2, D])
        dg = at("dg", TMP + 24, [P, 2, P])
        W13 = at("W13", 32, [P, 2, KT, 2 * FE])
        W2 = at("W2", 96, [P, 2, FT, D])
        W2s = at("W2s", 112, [P, FT, D])
        sgm = at("sgm", 120, [P, 2, FE])
        hb = at("hb", 122, [P, 2, FE])
        hbT = at("hbT", 124, [P, 2, FT, P])
        xg = at("xg", TMP + 16, [P, 2, D])
        xT = at("xT", TMP + 24, [P, 2, KT, P])
        yo = at("yo", TMP + 32, [P, 2, D])
        wr = at("wr", TMP + 40, [P, KT, NE])
        M = at("M", TMP + 42, [P, TT, NE])
        oh = at("oh", TMP + 44, [P, TOP, NE])
        oh2 = at("oh2", TMP + 46, [P, TOP, NE])
        i32 = mybir.dt.int32
        u32 = mybir.dt.uint32
        tab = at("tab", 128, [P, P, 2])
        tokT = at("tokT", 129, [P, P], i32)
        wtT = at("wtT", 129.5, [P, P])
        junk2 = at("junk2", 96, [P, D])
        fin = at("fin", TMP + 24, [P, 2, D])
        vr0 = at("vr0", TMP + 44, [P, P])
        vr1 = at("vr1", TMP + 44.5, [3 * KT + 1, P])
        CON = 192
        ident = at("ident", CON, [P, P])
        ones = at("ones", CON + .5, [P, P])
        MASK = at("MASK", CON + 1, [P, P])
        R = at("R", CON + 2, [P, T])
        B8 = at("B8", CON + 6, [P, T])
        sm0 = CON + 10
        small_at = [int(sm0 * 256)]

        def small(name, n, dt=fp32, parts=P):
            t = at(name, small_at[0] / 256, [parts, n], dt)
            small_at[0] += -(-n // 8) * 8
            assert small_at[0] <= 207 * 256 - 64, small_at
            return t

        vc0 = small("vc0", P)
        vc1 = small("vc1", 3 * KT + 1)
        ccol, bada = vc0[:, 0:8], vc0[:, 8:56]
        gpm, gpo, gpf, gpo2, cb = (vc0[:, 56 + 8 * j:64 + 8 * j] for j in range(5))
        cw = vc0[:, 96:128]
        ba, bx, lamc, gsub = vc1[:, 0:8], vc1[:, 8:16], vc1[:, 16:24], vc1[:, 24:25]
        cond = small("cond", KT)
        mod = small("mod", 48)
        rows_c = small("rows_c", 4 * KT)
        a1 = small("a1", KT)
        sp8 = small("sp8", KT)
        nsp8 = small("nsp8", KT)
        spt = small("spt", 4 * KT)
        gsub8 = small("gsub8", 1)
        lqk = small("lqk", 4 * HD, parts=1)
        lpr = small("lpr", HD, parts=1)
        ls = small("ls", 8, parts=1)
        nlam = small("nlam", 1)
        SL = small("SL", NH)
        ss = small("ss", TT)
        rms = small("rms", TT)
        rstd = small("rstd", TT)
        ssn = small("ssn", 2 * NH)
        rmn = small("rmn", 2 * NH)
        rsn = small("rsn", 2 * NH)
        mn = small("mn", 4)
        lsum = small("lsum", 4)
        rl = small("rl", 4)
        c1 = small("c1", 2)
        eps = small("eps", 1)
        small_at[0] = int((CON + 2) * 256)
        tri = small("tri", P)
        ebias = small("ebias", NE)
        io64 = small("io64", NE)
        ioP = small("ioP", 1)
        thr = small("thr", 8)
        sco = small("sco", NE)
        cho = small("cho", NE)
        g8 = small("g8", NE)
        gs = small("gs", NG)
        gv = small("gv", 8)
        gi = small("gi", 8, u32)
        gif = small("gif", 8)
        gm4 = small("gm4", TOPG * NG)
        gmk = small("gmk", NG)
        v8 = small("v8", 8)
        i8 = small("i8", 8, u32)
        idxf = small("idxf", TT * TOP)
        w8 = small("w8", TOP)
        wsm = small("wsm", 1)
        pairs = small("pairs", TT * TOP * 2)
        slotf = small("slotf", TT * TOP)
        slots = small("slots", TT * TOP, i32)
        posab = small("posab", NE)
        nbk = small("nbk", NE)
        pend = small("pend", NE)
        pst = small("pst", NE)
        eidf = small("eidf", 1)
        ehi = small("ehi", 1, i32)
        ehf = small("ehf", 1)
        tbf = small("tbf", 4)
        tbi = small("tbi", 4, i32)
        pendi = small("pendi", NE + 8, i32)
        npf = small("npf", 1)
        idxb = small("idxb", 2, i32)
        sidx = small("sidx", 2, i32)
        tbrow = small("tbrow", 4 * P, i32, parts=1)

        PS = ctx.enter_context(nc.psum_tensor("PS", [P, 8, HALF], fp32))

        def pair(p):
            return PS[:, 2 * p:2 * p + 2, :].rearrange("p b n -> p (b n)")

        acc = nc.dram_tensor("moe_sum_dram", (T + P, D), fp32, kind="Internal").ap()
        tabd = nc.dram_tensor("slot_table_dram", (P * P, 2), fp32, kind="Internal").ap()
        tbd = nc.dram_tensor("block_table_dram", (P, 4), i32, kind="Internal").ap()
        h2d = nc.dram_tensor("h2_dram", (T + P, D), fp32, kind="Internal").ap()

        s_small = sem("s_small")
        s_vt = sem("s_vt")
        s_vc = sem("s_vc")
        s_x = [sem("s_xin0"), sem("s_xin1")]
        s_ada = [sem("s_ada0"), sem("s_ada1")]
        s_w = [sem(f"s_w{j}") for j in range(4)]
        s_gw = [sem(f"s_gw{j}") for j in range(4)]
        s_const = sem("s_const")
        s_pool = sem("s_pool")
        s_cond = sem("s_cond")
        s_mod = sem("s_mod")
        s_modu = sem("s_modu")
        s_ss = sem("s_ss")
        s_rms = sem("s_rms")
        s_xn = sem("s_xn")
        s_xt = sem("s_xt")
        s_xe = sem("s_xe")
        s_dve = sem("s_dve")
        s_dve2 = sem("s_dve2")
        s_dve3 = sem("s_dve3")
        s_dve4 = sem("s_dve4")
        s_dve5 = sem("s_dve5")
        s_dve6 = sem("s_dve6")
        s_dve7 = sem("s_dve7")
        s_dve8 = sem("s_dve8")
        s_lnp = sem("s_lnp")
        s_act = sem("s_act")
        s_act2 = sem("s_act2")
        s_h = sem("s_h")
        s_mm = sem("s_mm")
        s_ev = [sem("s_ev0"), sem("s_ev1")]
        s_xp = sem("s_xp")
        s_xc = sem("s_xc")
        s_gate = sem("s_gate")
        s_ig = sem("s_ig")
        s_t = sem("s_t")
        s_a = sem("s_a")
        s_m2 = sem("s_m2")
        s_m = sem("s_m")
        s_yr = sem("s_yr")
        s_lam = sem("s_lam")
        s_lamp = sem("s_lamp")
        s_lamb = sem("s_lamb")
        s_S = sem("s_S")
        s_e = sem("s_e")
        s_A = sem("s_A")
        s_T = sem("s_T")
        s_pte = sem("s_pte")
        s_pv = sem("s_pv")
        s_oe = sem("s_oe")
        s_nss = sem("s_nss")
        s_nrm = sem("s_nrm")
        s_on = sem("s_on")
        s_oT = sem("s_oT")
        s_oTe = sem("s_oTe")
        s_mg = sem("s_mg")
        s_mod2 = sem("s_mod2")
        s_dg = sem("s_dg")
        s_bc = sem("s_bc")
        s_rows = sem("s_rows")
        s_yss = sem("s_yss")
        s_yrm = sem("s_yrm")
        s_x1 = sem("s_x1")
        s_h2 = sem("s_h2")
        s_h2T = sem("s_h2T")
        s_h2e = sem("s_h2e")
        s_h2d = [sem("s_h2d0"), sem("s_h2d1")]
        s_out = sem("s_out")
        s_ld = sem("s_ld")
        s_lg = sem("s_lg")
        s_sco = sem("s_sco")
        s_dr = sem("s_dr")
        s_M = sem("s_M")
        s_rk = sem("s_rk")
        s_slot = sem("s_slot")
        s_c2 = sem("s_c2")
        s_tb0 = sem("s_tb0")
        s_sct = sem("s_sct")
        s_tab = sem("s_tab")
        s_tabT = sem("s_tabT")
        s_tabc = sem("s_tabc")
        s_eid = sem("s_eid")
        s_tbd = sem("s_tbd")
        s_tbr = sem("s_tbr")
        s_acc0 = sem("s_acc0")
        sh = {n: sem("s_sh_" + n) for n in ("up", "sg", "t", "hb", "hT", "he", "dn", "ya", "yd", "st")}
        ro = {n: sem("s_ro_" + n) for n in ("up", "sg", "t", "hb", "hT", "he", "dn", "ya", "yd", "st")}
        s_shst = [sem("s_shst0"), sem("s_shst1")]
        s_w13 = [sem("s_w13_0"), sem("s_w13_1")]
        s_w2 = [sem("s_w2_0"), sem("s_w2_1")]
        s_ix = sem("s_ix")
        s_xg = [sem("s_xg0"), sem("s_xg1")]
        s_xgT = sem("s_xgT")
        s_xea = sem("s_xea")
        s_xed = sem("s_xed")
        s_six = sem("s_six")
        s_fl = [sem("s_fl0"), sem("s_fl1")]
        s_fss = sem("s_fss")
        s_frm = sem("s_frm")
        s_fdv = sem("s_fdv")
        s_fo = sem("s_fo")
        s_fst = [sem("s_fst0"), sem("s_fst1")]

        def vector_rows():
            r = 0
            for name in ("c", "b_ada", "g_pre_mix", "g_post_mix", "g_pre_ffn", "g_post_ffn", "conv_b"):
                src = a[name][0].rearrange("(k p) -> k p", p=P)
                yield vr0, r, src
                r += src.shape[0]
            yield vr0, r, a["conv_w"][0].rearrange("j (k p) -> (j k) p", p=P)
            yield vr1, 0, a["lru_ba"][0]
            yield vr1, KT, a["lru_bx"][0]
            yield vr1, 2 * KT, a["lru_lambda"][0].rearrange("(k p) -> k p", p=P)
            yield vr1, 3 * KT, a["g_subln"]

        N_SMALL = 12 + 4
        s_turn = {e: sem(f"s_turn_{e.name}") for e in (nc.sync.engine, nc.scalar.engine, nc.vector.engine,
                                                        nc.tensor.engine, nc.gpsimd.engine)}
        U_XR, U_GR, U_GA, U_YA, U_V, U_QK, U_GB, U_O, U_SH = 0, 8, 16, 24, 32, 40, 56, 72, 80
        EV_PER_HEAD = 9
        EV_ATT = U_QK // 2 + 1
        EV_AFTER = EV_ATT + NH * EV_PER_HEAD - U_GB // 2

        def ev(U):
            return U // 2 + 1 if isinstance(U, int) and U < U_QK else None

        class Link:

            def __init__(self, eng, s, start=0, per=0):
                self.eng, self.s, self.start, self.per, self.n, self.i = eng, s, start, per, 0, None

            def at(self, i):
                self.i, self.n = i, 0

            def __call__(self, ins, wait=True):
                ins.then_inc(self.s, 1)
                self.n += 1
                if wait:
                    self.wait()

            def wait(self):
                v = self.start + self.n
                hold(self.eng, self.s, v if self.i is None else self.i * self.per + v)

        def hold(eng, s, value):
            eng.wait_ge(s, value)
            eng.sem_inc(s_turn[eng.engine], 1)

        block = ctx.enter_context(nc.Block())

        def wtile(W, col):
            return W[:, col].rearrange("(k p) c -> p k c", p=P)

        @block.sync
        def _(sp):
            def x_tiles(first):
                with sp.Fori(0, TT // 2) as i:
                    for b in range(2):
                        hold(sp, s_xt if first else s_x1, 2 * i + b + 1)
                        sp.dma_start(xin[:, b, :], a["x"][0, ds(P * (2 * i + b), P), :]).then_inc(s_x[b], 16)

            for dst, r0, src in vector_rows():
                sp.dma_start(dst[r0:r0 + src.shape[0], :], src).then_inc(s_small, 16)
            for j, n in enumerate(("lam_q1", "lam_k1", "lam_q2", "lam_k2")):
                sp.dma_start(lqk[:, j * HD:(j + 1) * HD], a[n]).then_inc(s_small, 16)
            x_tiles(True)

            def tile(u, slot, W, c, quad):
                hold(sp, s_mm, quad if quad is not None else u - 3)
                sp.dma_start(WT[:, slot, :, :], wtile(W, ds(c, P))).then_inc(s_w[slot], 16)

            w_in = a["w_in"][0]
            for j in range(4):
                sp.dma_start(WT[:, j, :, :], wtile(w_in, ds(COL_XR + P * j, P))).then_inc(s_w[j], 16)
            for j in range(4):
                tile(U_XR + 4 + j, j, w_in, COL_XR + P * (4 + j), None)
            with sp.Fori(0, 2) as i:
                for j in range(4):
                    if j < 4:
                        hold(sp, s_gate, 4 * i + j + 1)
                        sp.dma_start(GW[:, j, 0, :], a["lru_wa"][0, ds(4 * i + j, 1)].rearrange("o c d -> (o c) d")).then_inc(s_gw[j], 16)
                        sp.dma_start(GW[:, j, 1, :], a["lru_wx"][0, ds(4 * i + j, 1)].rearrange("o c d -> (o c) d")).then_inc(s_gw[j], 16)
                    tile(U_GR + 4 * i + j, j, w_in, COL_GR + P * (4 * i + j), None)
            with sp.Fori(0, 2) as i:
                for j in range(4):
                    tile(U_GA + 4 * i + j, j, w_in, COL_GA + P * (4 * i + j), None)
            with sp.Fori(0, 2) as i:
                for j in range(4):
                    tile(U_YA + 4 * i + j, j, a["w_proj_rnn"][0], P * (4 * i + j), None)
            with sp.Fori(0, 2) as i:
                for j in range(4):
                    tile(0, j, w_in, COL_V + P * (4 * i + j), U_V + 4 * i)
            with sp.Fori(0, NH // 2) as i:
                for j in range(4):
                    h = 2 * i + j // 2
                    tile(0, j, w_in, (COL_Q if j % 2 == 0 else COL_K) + P * h, U_QK + 4 * i)
            with sp.Fori(0, 4) as i:
                for j in range(4):
                    n = 2 * i + j // 2
                    if j % 2 == 0:
                        tile(U_GB + 4 * i + j, j, w_in, COL_GB + P * n, None)
                    else:
                        tile(U_GB + 4 * i + j, j, a["w_proj_att"][0], P * n, None)
            with sp.Fori(0, 2) as i:
                for j in range(4):
                    tile(0, j, a["w_out"][0], P * (4 * i + j), U_O + 4 * i)
            for j, W in enumerate((a["w1_s"][0], a["w1_s"][0], a["w3_s"][0], a["w3_s"][0])):
                sp.wait_ge(s_mm, U_SH)
                sp.dma_start(WT[:, j, :, :], wtile(W, ds(P * (j % 2), P))).then_inc(s_w[j], 16)
            x_tiles(False)
            if STAGE == "x1":
                sp.wait_ge(s_h2d[0], 16 * (TT // 2) + 16)
                sp.wait_ge(s_h2d[1], 16 * (TT // 2) + 16)
                sp.wait_ge(s_x1, TT + 2)
                sp.dma_start(out[0].rearrange("(t p) d -> p t d", p=P), Y[:, :, :]).then_inc(s_out, 16)
                sp.wait_ge(s_out, 16)
                return
            sp.wait_ge(s_mm, U_SH)
            sp.wait_ge(s_yrm, 2 * TT)
            sp.wait_ge(s_h2d[0], 16)
            sp.wait_ge(s_h2d[1], 16)
            sp.dma_start(wr[:, :, :], a["w_router"][0].rearrange("(k p) e -> p k e", p=P)).then_inc(s_ld, 16)
            sp.dma_start(W2s[:, :, :], a["w2_s"][0].rearrange("(k p) n -> p k n", p=P)).then_inc(s_ld, 16)
            sp.dma_start(ebias[:, :], a["e_bias"].broadcast_to([P, NE])).then_inc(s_ld, 16)

            def expert_up(e, b):
                sp.dma_start(W13[:, b, :, 0:FE], a["w1_e"][0, ds(e, 1)].rearrange("o (k p) f -> p (o k) f", p=P))\
                    .then_inc(s_w13[b], 16)
                sp.dma_start(W13[:, b, :, FE:2 * FE], a["w3_e"][0, ds(e, 1)].rearrange("o (k p) f -> p (o k) f", p=P))\
                    .then_inc(s_w13[b], 16)

            def expert_down(e, b):
                sp.dma_start(W2[:, b, :, :], a["w2_e"][0, ds(e, 1)].rearrange("o (k p) n -> p (o k) n", p=P))\
                    .then_inc(s_w2[b], 16)

            for b in range(2):
                expert_up(b, b)
                expert_down(b, b)
            for t in range(TT):
                sp.wait_ge(sh["ya"], t + 1)
                sp.wait_ge(sh["yd"], t + 1)
                sp.dma_start(acc[t * P:(t + 1) * P, :], yo[:, t % 2, :]).then_inc(s_shst[t % 2], 16)
            sp.wait_ge(s_sct, 16 * TT * TOP)
            sp.dma_start(tab[:, :, :], tabd.rearrange("(g s) c -> g s c", s=P)).then_inc(s_tab, 16)
            sp.wait_ge(s_eid, 2)
            sp.dma_start(tbd, tbi[:, :]).then_inc(s_tbd, 16)
            sp.wait_ge(s_tbd, 16)
            sp.dma_start(tbrow[:, :], tbd.rearrange("(o g) c -> o (g c)", o=1)).then_inc(s_tbr, 16)
            with sp.Fori(0, NE // 2 - 1) as i:
                for b in range(2):
                    last = sp.value_load(pendi[0:1, ds(2 * i + b, 1)], min_val=1, max_val=NBLK)
                    hold(sp, ro["up"], last)
                    expert_up(2 * i + b + 2, b)
                    hold(sp, ro["dn"], last)
                    expert_down(2 * i + b + 2, b)
            pairs_n = sp.value_load(pendi[0:1, NE:NE + 1], min_val=1, max_val=NBLK // 2)
            hold(sp, ro["st"], 32 * pairs_n + 48)
            for t in range(TT):
                if t >= 2:
                    sp.wait_ge(s_fo, t - 1)
                sp.dma_start(xg[:, t % 2, :], acc[t * P:(t + 1) * P, :]).then_inc(s_fl[t % 2], 16)
                if t >= 1:
                    sp.wait_ge(s_fo, t)
                    sp.dma_start(out[0, (t - 1) * P:t * P, :], fin[:, (t - 1) % 2, :]).then_inc(s_fst[(t - 1) % 2], 16)
            sp.wait_ge(s_fo, TT)
            sp.dma_start(out[0, (TT - 1) * P:TT * P, :], fin[:, (TT - 1) % 2, :]).then_inc(s_fst[(TT - 1) % 2], 16)
            for b in range(2):
                sp.wait_ge(s_fst[b], 16 * TT // 2)

        @block.gpsimd
        def _(pool):
            link = Link(pool, s_pool)
            link(pool.memset(ident[:, :], 0.0))
            link(pool.affine_select(out=ident[:, :], in_=ident[:, :], compare_op=ALU.not_equal, fill=1.0, base=0,
                                    pattern=[[-1, P]], channel_multiplier=1))
            link(pool.memset(ones[:, :], 1.0), wait=False)
            link(pool.memset(MASK[:, :], 0.0))
            link(pool.affine_select(out=MASK[:, :], in_=MASK[:, :], compare_op=ALU.is_ge, fill=MASKED, base=0,
                                    pattern=[[-1, P]], channel_multiplier=1), wait=False)
            link(pool.iota(R[:, :], [[1, T]], base=P - T, channel_multiplier=-1,
                           allow_small_or_imprecise_dtypes=True), wait=False)
            for h in range(NH):
                link(pool.memset(SL[:, h:h + 1], 2.0 ** (-8.0 * (h + 1) / NH) * HD ** 0.5), wait=False)
            link.wait()
            pool.sem_inc(s_const, 1)

            def ada(lo, hi):
                with pool.Fori(lo, hi) as i:
                    for b in range(2):
                        pool.wait_ge(s_mod, 2 * i + b + 1)
                        pool.dma_start(AW[:, b, :, :], a["w_ada"][0][:, ds(HALF * (2 * i + b), HALF)]
                                       .rearrange("(k p) c -> p k c", p=P)).then_inc(s_ada[b], 16)

            ada(0, 2)
            pool.wait_ge(s_oTe, TT + 2)
            ada(2, 6)
            for b in range(2):
                pool.dma_start(h2d[T + HD * b:T + HD * (b + 1), :], R[HD * b:HD * (b + 1), :]).then_inc(s_h2d[b], 16)
            with pool.Fori(0, TT // 2) as i:
                for b in range(2):
                    hold(pool, s_h2, 2 * i + b + 1)
                    pool.dma_start(h2d[ds(P * (2 * i + b), P), :], h2t[:, b, :]).then_inc(s_h2d[b], 16)
            if STAGE == "x1":
                return
            for b in range(2):
                pool.wait_ge(s_h2d[b], 16)
            lp = Link(pool, s_c2)
            lp(pool.memset(tri[:, :], 1.0))
            lp(pool.affine_select(out=tri[:, :], in_=tri[:, :], compare_op=ALU.is_gt, fill=0.0, base=0,
                                  pattern=[[1, P]], channel_multiplier=-1), wait=False)
            lp(pool.iota(io64[:, :], [[1, NE]], base=0, channel_multiplier=0, allow_small_or_imprecise_dtypes=True),
               wait=False)
            lp(pool.iota(ioP[:, :], [[0, 1]], base=0, channel_multiplier=1, allow_small_or_imprecise_dtypes=True),
               wait=False)
            lp(pool.iota(thr[:, :], [[P, 8]], base=P, channel_multiplier=0, allow_small_or_imprecise_dtypes=True),
               wait=False)
            pv = pairs[:, :].rearrange("p (t k c) -> p t k c", t=TT, k=TOP)
            for t in range(TT):
                lp(pool.iota(pv[:, t, :, 0], [[0, TOP]], base=t * P, channel_multiplier=1,
                             allow_small_or_imprecise_dtypes=True), wait=False)
            pool.wait_ge(s_mm, U_SH)
            pool.wait_ge(sh["up"], TT)
            lp(pool.iota(tab[:, :, 0], [[1, P]], base=T, channel_multiplier=0, allow_small_or_imprecise_dtypes=True),
               wait=False)
            lp(pool.memset(tab[:, :, 1], 0.0))
            pool.dma_start(tabd.rearrange("(g s) c -> g s c", s=P), tab[:, :, :]).then_inc(s_tb0, 16)
            pool.wait_ge(s_h2d[0], 16 * (TT // 2) + 16)
            pool.wait_ge(s_h2d[1], 16 * (TT // 2) + 16)
            for b in range(2):
                pool.dma_start(acc[T + HD * b:T + HD * (b + 1), :], ROWS[HD * b:HD * (b + 1), 3, :])\
                    .then_inc(ro["st"], 16)
            pool.wait_ge(s_tb0, 16)
            pool.wait_ge(s_slot, 1)
            for t in range(TT):
                for k in range(TOP):
                    pool.indirect_dma_start(tabd, bass.IndirectOffsetOnAxis(slots[:, t * TOP + k:t * TOP + k + 1], 0),
                                            pv[:, t, k, :], None).then_inc(s_sct, 16)

            def gather(g, b):
                lq(pool.tensor_copy(idxb[:, b:b + 1], tokT[:, ds(g, 1)]))
                pool.indirect_dma_start(xg[:, b, :], None, h2d, bass.IndirectOffsetOnAxis(idxb[:, b:b + 1], 0))\
                    .then_inc(s_xg[b], 16)

            def add(g, b, done):
                hold(pool, ro["ya"], g + 2)
                hold(pool, ro["yd"], g + 2)
                lq(pool.tensor_copy(sidx[:, b:b + 1], tokT[:, ds(g, 1)]))
                if done is not None:
                    hold(pool, ro["st"], done)
                pool.indirect_dma_start(acc, bass.IndirectOffsetOnAxis(sidx[:, b:b + 1], 0), yo[:, b, :], None,
                                        compute_op=ALU.add).then_inc(ro["st"], 16)

            pool.wait_ge(s_tabc, 2)
            pool.wait_ge(s_eid, 2)
            np_ = pool.value_load(pendi[0:1, NE:NE + 1], min_val=1, max_val=NBLK // 2 - 1)
            lq = Link(pool, s_ix, 0, 4)
            for b in range(2):
                gather(b, b)
            for b in range(2):
                pool.wait_ge(s_shst[b], 16 * TT // 2)
            lq.start, lq.n = 2, 0
            with pool.Fori(0, np_) as i:
                lq.at(i)
                for j in range(2):
                    g = 2 * i + j + 1
                    hold(pool, s_xgT, g)
                    gather(g + 1, j)
                    add(g - 1, j, (2 * i + j) * 16 + 32)
            lq.i = np_
            lq.n = 0
            add(2 * np_, 0, 32 * np_ + 32)

        def unit(pe, slot, w_round, ev_at, p, moving):
            pe.wait_ge(s_w[slot], 16 * w_round)
            pe.wait_ge(s_ev[p], ev_at)
            for half in range(2):
                for k in range(KT):
                    last = pe.matmul(PS[:, 2 * p + half, :], WT[:, slot, k, :],
                                     moving[:, k, half * HALF:(half + 1) * HALF], start=(k == 0), stop=(k == KT - 1))
            last.then_inc(s_mm, 1)

        def rows_unit(pe, q, w_round, ev_at, p, lhs):
            if q == 0:
                for slot in range(4):
                    pe.wait_ge(s_w[slot], 16 * w_round)
            pe.wait_ge(s_ev[p], ev_at)
            for half in range(2):
                t = 2 * q + half
                for k in range(KT):
                    last = pe.matmul(PS[:, 2 * p + half, :], lhs[:, k, t * P:(t + 1) * P], WT[:, :, k, :],
                                     start=(k == 0), stop=(k == KT - 1))
            last.then_inc(s_mm, 1)

        MODB = 7

        def group(qt):
            return sum(t // 4 + 1 for t in range(qt))

        def tcols(buf, t):
            return buf[:, :, ds(t * P, P)]

        def pair3(p):
            return pair(p).rearrange("p (k n) -> p k n", k=KT)

        @block.tensor
        def _(pe):
            pe.sem_inc(s_pv, 2)
            pe.sem_inc(s_mod, 2)
            pe.sem_inc(s_xt, 2)
            pe.sem_inc(s_gate, 4)
            pe.wait_ge(s_const, 1)
            pe.wait_ge(s_small, 16 * N_SMALL)
            pe.transpose(PS[:, 4, 0:P], vr0[:, :], ident[:, :])
            pe.transpose(PS[:, 5, 0:3 * KT + 1], vr1[:, :], ident[0:3 * KT + 1, 0:3 * KT + 1]).then_inc(s_vt, 1)

            def ada(lo, hi):
                with pe.Fori(lo, hi) as i:
                    for b in range(2):
                        pe.wait_ge(s_ada[b], 16 * i + 16)
                        for c in range(4):
                            for k in range(KT):
                                last = pe.matmul(PS[:, MODB, ds(8 * i + 4 * b + c, 1)],
                                                 AW[:, b, k, c * P:(c + 1) * P], cond[:, k:k + 1],
                                                 start=(k == 0), stop=(k == KT - 1))
                        last.then_inc(s_mod, 1)

            with pe.Fori(0, TT // 2) as i:
                for b in range(2):
                    pe.wait_ge(s_xn, 2 * i + b + 1)
                    pe.wait_ge(s_xe, 2 * i + b + 1)
                    for k in range(KT):
                        last = pe.transpose(pair(b)[:, k * P:(k + 1) * P], xin[:, b, k * P:(k + 1) * P], ident[:, :])
                    last.then_inc(s_xt, 1)
            pe.wait_ge(s_cond, 1)
            ada(0, 2)
            pe.wait_ge(s_lam, 1)
            pe.matmul(PS[:, 6, 0:1], ones[0:1, :], ls[:, 4:5], start=True, stop=True).then_inc(s_lamp, 1)

            pe.wait_ge(s_h, KT)
            with pe.Fori(0, 2) as i:
                for j in range(4):
                    unit(pe, j, i + 1 + U_XR // 4, U_XR // 2 + 2 * i + j // 2 + 1, j % 2, hT)
            pe.wait_ge(s_lamb, 1)
            pe.wait_ge(s_modu, 1)
            with pe.Fori(0, 2) as i:
                for j in range(4):
                    n = 4 * i + j
                    unit(pe, j, i + 1 + U_GR // 4, U_GR // 2 + 2 * i + j // 2 + 1, j % 2, hT)
                    pe.wait_ge(s_gw[j], 32 * i + 32)
                    pe.wait_ge(s_xc, n + 3)
                    pe.wait_ge(s_ig, n + 1)
                    for g in range(2):
                        for half in range(2):
                            last = pe.matmul(PS[:, 4 + 2 * g + half, :], GW[:, j, g, :],
                                             xcT[:, ds(n, 1), half * HALF:(half + 1) * HALF]
                                             .rearrange("p o n -> p (o n)"), start=True, stop=True)
                    last.then_inc(s_gate, 1)
            with pe.Fori(0, 2) as i:
                for j in range(4):
                    unit(pe, j, i + 1 + U_GA // 4, U_GA // 2 + 2 * i + j // 2 + 1, j % 2, hT)
            pe.wait_ge(s_yr, KT + 1)
            with pe.Fori(0, 2) as i:
                for j in range(4):
                    unit(pe, j, i + 1 + U_YA // 4, U_YA // 2 + 2 * i + j // 2 + 1, j % 2, xcT)
            with pe.Fori(0, 2) as i:
                for q in range(4):
                    rows_unit(pe, q, i + 1 + U_V // 4, U_V // 2 + 2 * i + q // 2 + 1, q % 2, hT)

            with pe.Fori(0, NH // 2) as i:
                for b in range(2):
                    h = 2 * i + b
                    for c in range(2):
                        unit(pe, 2 * b + c, i + 1 + U_QK // 4, EV_ATT + EV_PER_HEAD * h, c, hT)

                    def scores(qt):
                        L = (qt + 1) * P
                        for c in range(2):
                            if qt == 0:
                                pe.wait_ge(s_ev[0], EV_ATT + EV_PER_HEAD * h + 1)
                                pe.wait_ge(s_ev[1], EV_ATT + EV_PER_HEAD * h + 1)
                            else:
                                pe.wait_ge(s_ev[c], EV_ATT + EV_PER_HEAD * h + 1 + qt)
                            for n0 in range(0, L, HALF):
                                n1 = min(L, n0 + HALF)
                                last = pe.matmul(pair(c)[:, n0:n1], qT[c * HD:(c + 1) * HD, b, qt * P:(qt + 1) * P],
                                                 kT[c * HD:(c + 1) * HD, b, n0:n1], start=True, stop=True)
                            last.then_inc(s_S, 1)

                    def turn(qt):
                        pe.wait_ge(s_A, 8 * h + qt + 1)
                        for g in range(qt // 4 + 1):
                            G = group(qt) + g
                            pe.wait_ge(s_pte, 12 * h + G + 1)
                            for kb in range(4 * g, min(4 * g + 4, qt + 1)):
                                last = pe.transpose(PS[:, 6 + G % 2, (kb % 4) * P:(kb % 4 + 1) * P],
                                                    SM[:, qt % 2, 0, kb * P:(kb + 1) * P], ident[:, :])
                            last.then_inc(s_T, 1)

                    def values(qt):
                        pe.wait_ge(s_pte, 12 * h + group(qt) + qt // 4 + 1 + 2)
                        pe.wait_ge(s_oe, 8 * h + qt + 1)
                        for kb in range(qt + 1):
                            last = pe.matmul(PS[:, 4 + qt % 2, 0:P], PT[:, qt % 2, kb, :],
                                             V[:, kb, ds(h * P, P)], start=(kb == 0), stop=(kb == qt))
                        last.then_inc(s_pv, 1)

                    scores(0)
                    for qt in range(TT):
                        if qt + 1 < TT:
                            scores(qt + 1)
                        turn(qt)
                        if qt >= 1:
                            values(qt - 1)
                    values(TT - 1)

            with pe.Fori(0, TT // 2) as i:
                for b in range(2):
                    pe.wait_ge(s_on, 2 * i + b + 1)
                    pe.wait_ge(s_oTe, 2 * i + b + 1)
                    if b == 0:
                        pe.wait_ge(s_ev[0], EV_ATT + NH * EV_PER_HEAD)
                        pe.wait_ge(s_ev[1], EV_ATT + NH * EV_PER_HEAD)
                    for k in range(KT):
                        last = pe.transpose(pair(b)[:, k * P:(k + 1) * P], on2[:, b, k * P:(k + 1) * P], ident[:, :])
                    last.then_inc(s_oT, 1)
            pe.wait_ge(s_oTe, TT + 2)
            E0 = EV_ATT + NH * EV_PER_HEAD
            with pe.Fori(0, 4) as i:
                for j in range(4):
                    unit(pe, j, i + 1 + U_GB // 4, E0 + 2 * i + j // 2, j % 2, hT if j % 2 == 0 else oT)
            ada(2, 6)
            for m in range(4 * KT):
                pe.wait_ge(s_dg, m + 1)
                if m >= 2:
                    pe.wait_ge(s_rows, m - 1)
                pe.matmul(PS[:, 4 + m % 2, 0:P], ones[:, :], dg[:, m % 2, :], start=True, stop=True).then_inc(s_bc, 1)
            pe.wait_ge(s_mg, KT + 2)
            with pe.Fori(0, 2) as i:
                for q in range(4):
                    rows_unit(pe, q, i + 1 + U_O // 4, E0 + (U_O - U_GB) // 2 + 2 * i + q // 2, q % 2, gT)
            with pe.Fori(0, TT // 2) as i:
                for b in range(2):
                    pe.wait_ge(s_h2, 2 * i + b + 1)
                    pe.wait_ge(s_h2e, 2 * i + b + 1)
                    for k in range(KT):
                        last = pe.transpose(pair(2 + b)[:, k * P:(k + 1) * P], h2t[:, b, k * P:(k + 1) * P], ident[:, :])
                    last.then_inc(s_h2T, 1)
            if STAGE == "x1":
                return
            pe.wait_ge(s_h2e, TT + 2)
            pe.wait_ge(s_ld, 48)
            for t in range(TT):
                for k in range(KT):
                    last = pe.matmul(PS[:, 7, t * NE:(t + 1) * NE], hT[:, k, t * P:(t + 1) * P], wr[:, k, :],
                                     start=(k == 0), stop=(k == KT - 1))
                last.then_inc(s_lg, 1)

            def turn_hidden(S, g, b):
                hold(pe, S["hb"], g + 1)
                for f in range(FT):
                    last = pe.transpose(PS[:, 6, f * P:(f + 1) * P], hb[:, b, f * P:(f + 1) * P], ident[:, :])
                last.then_inc(S["hT"], 1)

            def up(S, g, b, lhs, w):
                for k in range(KT):
                    last = pe.matmul(PS[:, 2 + b, :], lhs(k), w(k), start=(k == 0), stop=(k == KT - 1))
                last.then_inc(S["up"], 1)

            def down(S, g, b, w):
                hold(pe, S["he"], g + 1)
                for half in range(2):
                    for f in range(FT):
                        last = pe.matmul(PS[:, 4 + half, :], hbT[:, b, f, :], w(f, half),
                                         start=(f == 0), stop=(f == FT - 1))
                last.then_inc(S["dn"], 1)

            for j in range(4):
                pe.wait_ge(s_w[j], 16 * (U_SH // 4 + 1))
            for t in range(TT + 1):
                if t >= 1:
                    turn_hidden(sh, t - 1, (t - 1) % 2)
                if t < TT:
                    if t >= 2:
                        pe.wait_ge(sh["hb"], t - 1)
                    up(sh, t, t % 2, lambda k: hT[:, k, t * P:(t + 1) * P], lambda k: WT[:, :, k, :])
                if t >= 1:
                    if t >= 2:
                        pe.wait_ge(sh["ya"], t - 1)
                        pe.wait_ge(sh["yd"], t - 1)
                    down(sh, t - 1, (t - 1) % 2, lambda f, half: W2s[:, f, half * HALF:(half + 1) * HALF])
            pe.wait_ge(s_M, TT)
            for t in range(TT):
                for j in range(t + 1):
                    pe.matmul(PS[:, 0, t * NE:(t + 1) * NE], (tri if j == t else ones)[:, :], M[:, j, :],
                              start=(j == 0), stop=(j == t))
            for j in range(TT):
                last = pe.matmul(PS[:, 1, 0:NE], ones[:, :], M[:, j, :], start=(j == 0), stop=(j == TT - 1))
            last.then_inc(s_rk, 1)
            pe.wait_ge(s_tab, 16)
            pe.wait_ge(s_eid, 1)
            for c in range(2):
                pe.transpose(PS[:, c, 0:P], tab[:, :, c], ident[:, :]).then_inc(s_tabT, 1)
            pe.wait_ge(s_tabc, 2)
            pe.wait_ge(s_tbr, 16)
            np_ = pe.value_load(pendi[0:1, NE:NE + 1], min_val=1, max_val=NBLK // 2 - 1)

            def turn_rows(g, b, xg_round):
                hold(pe, s_xg[b], xg_round)
                hold(pe, s_xea, g + 1)
                hold(pe, s_xed, g + 1)
                for k in range(KT):
                    last = pe.transpose(PS[:, k // 4, (k % 4) * P:(k % 4 + 1) * P], xg[:, b, k * P:(k + 1) * P],
                                        ident[:, :])
                last.then_inc(s_xgT, 1)

            def expert_regs(g):
                par = pe.value_load(tbrow[0:1, ds(4 * g, 1)], min_val=0, max_val=1)
                even = pe.value_load(tbrow[0:1, ds(4 * g + 1, 1)], min_val=1, max_val=NE)
                odd = pe.value_load(tbrow[0:1, ds(4 * g + 2, 1)], min_val=1, max_val=NE)
                return par, even, odd

            def block_up(g, b):
                par, even, odd = expert_regs(g)
                hold(pe, s_xea, g + 2)
                hold(pe, s_xed, g + 2)
                hold(pe, s_w13[0], 32 * even)
                hold(pe, s_w13[1], 32 * odd)
                up(ro, g, b, lambda k: xT[:, b, k, :], lambda k: W13[:, ds(par, 1), k, :].rearrange("p o n -> p (o n)"))

            def block_down(g, b):
                par, even, odd = expert_regs(g)
                hold(pe, s_w2[0], 16 * even)
                hold(pe, s_w2[1], 16 * odd)
                down(ro, g, b, lambda f, half: W2[:, ds(par, 1), f, half * HALF:(half + 1) * HALF]
                     .rearrange("p o n -> p (o n)"))

            turn_rows(0, 0, 16)
            block_up(0, 0)
            turn_rows(1, 1, 16)
            with pe.Fori(0, np_) as i:
                for j in range(2):
                    g = 2 * i + j + 1
                    turn_hidden(ro, g - 1, j)
                    block_up(g, 1 - j)
                    hold(pe, ro["ya"], g)
                    hold(pe, ro["yd"], g)
                    block_down(g - 1, j)
                    turn_rows(g + 1, j, 16 * i + 32)
            turn_hidden(ro, 2 * np_, 0)
            hold(pe, ro["ya"], 2 * np_ + 1)
            hold(pe, ro["yd"], 2 * np_ + 1)
            block_down(2 * np_, 0)

        @block.scalar
        def _(act):
            for p in range(2):
                act.sem_inc(s_ev[p], 1)
            act.sem_inc(s_xe, 2)
            act.sem_inc(s_ig, 1)
            act.sem_inc(s_pte, 2)
            act.sem_inc(s_oe, 2)
            act.sem_inc(s_oTe, 2)
            act.sem_inc(s_h2e, 2)
            act.wait_ge(s_vt, 1)
            act.activation(vc0[:, :], PS[:, 4, 0:P], ACT.Copy).then_inc(s_vc, 1)
            act.activation(vc1[:, :], PS[:, 5, 0:3 * KT + 1], ACT.Copy).then_inc(s_vc, 1)
            act.wait_ge(s_vc, 1)
            act.activation(cond[:, :], ccol[:, :], ACT.Silu).then_inc(s_cond, 1)
            act.wait_ge(s_lnp, 2)
            act.activation(spt[:, 0:KT], spt[:, KT:2 * KT], ACT.Exp).then_inc(s_act, 1)
            act.wait_ge(s_lnp, 4)
            act.activation(ls[:, 2:4], ls[:, 0:2], ACT.Exp).then_inc(s_act, 1)

            def rms_of(src, i, b, s_sq, s_rt, n_in):
                t = 2 * i + b
                act.activation(junk[:, :], src, ACT.Square, accum_out=ss[:, ds(t, 1)]).then_inc(s_sq, 1)
                hold(act, s_sq, n_in)
                act.activation(rms[:, ds(t, 1)], ss[:, ds(t, 1)], ACT.Sqrt, scale=1.0 / D, bias=eps[:, 0:1]).then_inc(s_rt, 1)

            act.wait_ge(s_const, 1)
            with act.Fori(0, TT // 2) as i:
                for b in range(2):
                    hold(act, s_x[b], 16 * i + 16)
                    rms_of(xin[:, b, :], i, b, s_ss, s_rms, 2 * i + b + 1)
                    hold(act, s_xt, 2 * i + b + 3)
                    act.activation(tcols(hT, 2 * i + b), pair3(b), ACT.Copy).then_inc(s_xe, 1)
            act.wait_ge(s_lamp, 1)
            act.activation(nlam[:, :], PS[:, 6, 0:1], ACT.Copy, scale=-1.0).then_inc(s_lamb, 1)
            with act.Fori(0, 2) as i:
                for j in range(4):
                    n = 4 * i + j
                    act.wait_ge(s_mm, U_XR + n + 1)
                    hold(act, s_xc, n + 1)
                    act.activation(xpad[:, j % 2, 4:4 + T], pair(j % 2), ACT.Copy).then_inc(s_ev[j % 2], 1)
            with act.Fori(0, 2) as i:
                for j in range(4):
                    n = 4 * i + j
                    act.wait_ge(s_gate, n + 5)
                    hold(act, s_yr, n + 1)
                    act.activation(rT[:, :], pair(2), ACT.Sigmoid, bias=ba[:, ds(n, 1)]).then_inc(s_act2, 1)
                    act.activation(iT[:, :], pair(3), ACT.Sigmoid, bias=bx[:, ds(n, 1)]).then_inc(s_ig, 1)
                    hold(act, s_act2, n + 1)
                    act.activation(tT[:, :], rT[:, :], ACT.Tanh, scale=sp8[:, ds(n, 1)]).then_inc(s_t, 1)
                    act.activation(aT[:, :], rT[:, :], ACT.Exp, scale=nsp8[:, ds(n, 1)]).then_inc(s_a, 1)
                    hold(act, s_m2, n + 1)
                    act.activation(mT[:, :], mT[:, :], ACT.Sqrt).then_inc(s_m, 1)
                    hold(act, s_mm, U_GR + n + 1)
                    act.activation(geT[:, :], pair(j % 2), ACT.Gelu_apprx_tanh).then_inc(s_ev[j % 2], 1)
            with act.Fori(0, 2) as i:
                for j in range(4):
                    n = 4 * i + j
                    hold(act, s_mm, U_GA + n + 1)
                    act.activation(gT[:, ds(n, 1), :].rearrange("p o n -> p (o n)"), pair(j % 2), ACT.Sigmoid)\
                        .then_inc(s_ev[j % 2], 1)
            with act.Fori(0, 2) as i:
                for q in range(4):
                    hold(act, s_mm, U_V + 4 * i + q + 1)
                    act.activation(V[:, 2 * q:2 * q + 2, ds(i * HALF, HALF)], PS[:, 2 * (q % 2):2 * (q % 2) + 2, :],
                                   ACT.Copy).then_inc(s_ev[q % 2], 1)
            with act.Fori(0, NH // 2) as i:
                for b in range(2):
                    h = 2 * i + b
                    for c, dst in enumerate((qT, kT)):
                        hold(act, s_mm, U_QK + 2 * h + c + 1)
                        act.activation(dst[:, b, :], pair(c), ACT.Copy).then_inc(s_ev[c], 1)

                    def exps(qt):
                        L = (qt + 1) * P
                        for c in range(2):
                            hold(act, s_ev[c], EV_ATT + EV_PER_HEAD * h + 1 + qt + 1)
                            s = SM[:, qt % 2, c, 0:L]
                            m = 2 * (qt % 2) + c
                            act.activation(s, s, ACT.Exp, scale=-1.0, bias=mn[:, m:m + 1],
                                           accum_out=lsum[:, m:m + 1]).then_inc(s_e, 1)

                    def turned(qt):
                        if True:
                            hold(act, s_pv, 8 * h + qt + 1)
                        for g in range(qt // 4 + 1):
                            G = group(qt) + g
                            nb = min(4, qt + 1 - 4 * g)
                            hold(act, s_T, 12 * h + G + 1)
                            act.activation(PT[:, qt % 2, 4 * g:4 * g + nb, :].rearrange("p k n -> p (k n)"),
                                           PS[:, 6 + G % 2, 0:nb * P], ACT.Copy).then_inc(s_pte, 1)

                    def outs(qt):
                        hold(act, s_pv, 8 * h + qt + 3)
                        act.activation(ON[:, qt, ds(h * P, P)], PS[:, 4 + qt % 2, 0:P], ACT.Copy,
                                       scale=rl[:, 2 * (qt % 2):2 * (qt % 2) + 1]).then_inc(s_oe, 1)

                    exps(0)
                    for qt in range(TT):
                        if qt + 1 < TT:
                            exps(qt + 1)
                        turned(qt)
                        if qt >= 1:
                            outs(qt - 1)
                    outs(TT - 1)
            with act.Fori(0, TT // 2) as i:
                for b in range(2):
                    t = 2 * i + b
                    hold(act, s_nss, t + 1)
                    act.activation(rmn[:, b * NH:(b + 1) * NH], ssn[:, b * NH:(b + 1) * NH], ACT.Sqrt,
                                   scale=1.0 / P, bias=eps[:, 0:1]).then_inc(s_nrm, 1)
                    hold(act, s_oT, t + 1)
                    act.activation(tcols(oT, t), pair3(b), ACT.Copy, scale=gsub8[:, 0:1]).then_inc(s_oTe, 1)
            with act.Fori(0, 4) as i:
                for j in range(2):
                    n = 2 * i + j
                    act.wait_ge(s_mm, U_GB + 2 * n + 1)
                    hold(act, s_mg, n + 1)
                    act.activation(sg[:, j, :], pair(0), ACT.Sigmoid).then_inc(s_ev[0], 1)
            for m in range(4 * KT):
                act.wait_ge(s_bc, m + 1)
                act.activation(ROWS[:, m // KT, (m % KT) * P:(m % KT + 1) * P], PS[:, 4 + m % 2, 0:P], ACT.Copy)\
                    .then_inc(s_rows, 1)
            with act.Fori(0, 2) as i:
                for q in range(4):
                    hold(act, s_mm, U_O + 4 * i + q + 1)
                    act.activation(Y[:, 2 * q:2 * q + 2, ds(i * HALF, HALF)], PS[:, 2 * (q % 2):2 * (q % 2) + 2, :],
                                   ACT.Copy).then_inc(s_ev[q % 2], 1)
            act.wait_ge(s_ev[0], EV_ATT + NH * EV_PER_HEAD + (U_SH - U_GB) // 2)
            act.wait_ge(s_ev[1], EV_ATT + NH * EV_PER_HEAD + (U_SH - U_GB) // 2)
            with act.Fori(0, TT // 2) as i:
                for b in range(2):
                    t = 2 * i + b
                    y = Y[:, ds(t, 1), :].rearrange("p o n -> p (o n)")
                    rms_of(y, i, b, s_yss, s_yrm, 2 * t + 1)
                    hold(act, s_x1, t + 3)
                    rms_of(y, i, b, s_yss, s_yrm, 2 * t + 2)
                    hold(act, s_h2T, t + 1)
                    act.activation(tcols(hT, t), pair3(2 + b), ACT.Copy).then_inc(s_h2e, 1)
            if STAGE == "x1":
                return
            act.sem_inc(s_xea, 1)
            act.sem_inc(ro["ya"], 1)

            def hidden_act(S, g, b):
                hold(act, S["up"], g + 1)
                act.activation(sgm[:, b, :], PS[:, 2 + b, 0:FE], ACT.Sigmoid).then_inc(S["sg"], 1)

            def hidden_turned(S, g, b):
                hold(act, S["hT"], g + 1)
                act.activation(hbT[:, b, :, :].rearrange("p f n -> p (f n)"), PS[:, 6, 0:FE], ACT.Copy)\
                    .then_inc(S["he"], 1)

            for t in range(TT):
                act.wait_ge(s_lg, TT)
                if t >= 1:
                    act.wait_ge(s_M, t)
                act.activation(sco[:, :], PS[:, 7, t * NE:(t + 1) * NE], ACT.Sigmoid).then_inc(s_sco, 1)
            for t in range(TT + 1):
                if t >= 1:
                    hidden_turned(sh, t - 1, (t - 1) % 2)
                if t < TT:
                    hidden_act(sh, t, t % 2)
                if t >= 1:
                    act.wait_ge(sh["dn"], t)
                    if t >= 3:
                        act.wait_ge(s_shst[(t - 1) % 2], 16 * ((t - 1) // 2))
                    act.activation(yo[:, (t - 1) % 2, 0:HALF], PS[:, 4, :], ACT.Copy).then_inc(sh["ya"], 1)
            act.wait_ge(s_tabT, 2)
            act.activation(tokT[:, :], PS[:, 0, 0:P], ACT.Copy).then_inc(s_tabc, 1)
            act.activation(wtT[:, :], PS[:, 1, 0:P], ACT.Copy).then_inc(s_tabc, 1)
            act.wait_ge(s_tabc, 2)
            act.wait_ge(s_eid, 2)
            for b in range(2):
                act.wait_ge(s_shst[b], 16 * TT // 2)
            np_ = act.value_load(pendi[0:1, NE:NE + 1], min_val=1, max_val=NBLK // 2 - 1)

            def rows_turned(g, b):
                hold(act, s_xgT, g + 1)
                act.activation(xT[:, b, 0:4, :].rearrange("p k n -> p (k n)"), PS[:, 0, :], ACT.Copy)\
                    .then_inc(s_xea, 1)

            def out_half(g, b, done):
                hold(act, ro["dn"], g + 1)
                if done is not None:
                    hold(act, ro["st"], done)
                act.activation(yo[:, b, 0:HALF], PS[:, 4, :], ACT.Copy, scale=wtT[:, ds(g, 1)]).then_inc(ro["ya"], 1)

            rows_turned(0, 0)
            hidden_act(ro, 0, 0)
            rows_turned(1, 1)
            with act.Fori(0, np_) as i:
                for j in range(2):
                    g = 2 * i + j + 1
                    hidden_turned(ro, g - 1, j)
                    hidden_act(ro, g, 1 - j)
                    out_half(g - 1, j, 16 * g)
                    rows_turned(g + 1, j)
            hidden_turned(ro, 2 * np_, 0)
            out_half(2 * np_, 0, 32 * np_ + 16)
            for t in range(TT):
                act.wait_ge(s_fl[t % 2], 16 * (t // 2 + 1))
                act.activation(junk2[:, :], xg[:, t % 2, :], ACT.Square, accum_out=ss[:, t:t + 1]).then_inc(s_fss, 1)
                act.wait_ge(s_fss, t + 1)
                act.activation(rms[:, t:t + 1], ss[:, t:t + 1], ACT.Sqrt, scale=1.0 / D, bias=eps[:, 0:1])\
                    .then_inc(s_frm, 1)

        @block.vector
        def _(dve):
            stt = dve.scalar_tensor_tensor
            dve.sem_inc(s_xc, 2)
            dve.sem_inc(s_yr, 1)
            dve.sem_inc(s_mg, 2)
            dve.sem_inc(s_x1, 2)
            link = Link(dve, s_dve)
            dve.memset(eps[:, :], EPS).then_inc(s_lnp, 1)
            dve.wait_ge(s_small, 16 * N_SMALL)
            dve.wait_ge(s_vc, 2)
            link(dve.tensor_scalar(spt[:, KT:2 * KT], lamc[:, :], -1.0, None, ALU.mult), wait=True)
            dve.tensor_tensor(spt[:, KT:2 * KT], spt[:, KT:2 * KT], lamc[:, :], ALU.min).then_inc(s_lnp, 1)
            for j in range(2):
                dve.tensor_tensor_reduce(out=lpr[:, :], in0=lqk[:, 2 * j * HD:(2 * j + 1) * HD],
                                         in1=lqk[:, (2 * j + 1) * HD:(2 * j + 2) * HD], scale=1.0, scalar=0.0,
                                         op0=ALU.mult, op1=ALU.add, accum_out=ls[:, j:j + 1]).then_inc(s_lnp, 1)
                dve.wait_ge(s_lnp, 3 + j)
            dve.wait_ge(s_act, 1)
            e, w, w2, poly = (spt[:, j * KT:(j + 1) * KT] for j in range(4))
            link(dve.tensor_scalar(w, e, 2.0, None, ALU.add))
            link(dve.reciprocal(w, w))
            link(dve.tensor_tensor(w, w, e, ALU.mult))
            link(dve.tensor_tensor(w2, w, w, ALU.mult))
            link(dve.memset(poly, 1.0 / 19))
            for m in range(8, -1, -1):
                link(dve.tensor_tensor(poly, poly, w2, ALU.mult))
                link(dve.tensor_scalar(poly, poly, 1.0 / (2 * m + 1), None, ALU.add))
            link(stt(out=poly, in0=poly, scalar=2.0, in1=w, op0=ALU.mult, op1=ALU.mult))
            link(dve.tensor_scalar(w2, lamc[:, :], -1.0, 0.0, ALU.mult, ALU.max))
            link(dve.tensor_tensor(w2, w2, poly, ALU.add))
            link(dve.tensor_scalar(sp8[:, :], w2, LRU_C, None, ALU.mult), wait=False)
            link(dve.tensor_scalar(nsp8[:, :], w2, -LRU_C, None, ALU.mult), wait=False)
            link(dve.tensor_scalar(gsub8[:, :], gsub[:, :], 1.0 - LAM_INIT, None, ALU.mult), wait=False)
            dve.wait_ge(s_act, 2)
            link(dve.tensor_tensor(ls[:, 5:6], ls[:, 2:3], ls[:, 3:4], ALU.subtract))
            dve.tensor_scalar(ls[:, 4:5], ls[:, 5:6], LAM_INIT, None, ALU.add).then_inc(s_lam, 1)

            l1 = Link(dve, s_dve2, 0, 2)
            with dve.Fori(0, TT // 2) as i:
                l1.at(i)
                for b in range(2):
                    t = 2 * i + b
                    hold(dve, s_rms, t + 1)
                    l1(dve.reciprocal(rstd[:, ds(t, 1)], rms[:, ds(t, 1)]))
                    dve.tensor_scalar(xin[:, b, :], xin[:, b, :], rstd[:, ds(t, 1)], None, ALU.mult).then_inc(s_xn, 1)
            dve.wait_ge(s_mod, 4 + 2)
            dve.tensor_tensor(mod[:, 0:16], PS[:, MODB, 0:16], bada[:, 0:16], ALU.add).then_inc(s_modu, 1)
            dve.wait_ge(s_modu, 1)
            link(stt(out=a1[:, :], in0=mod[:, KT:2 * KT], scalar=1.0, in1=gpm[:, :], op0=ALU.add, op1=ALU.mult))
            dve.wait_ge(s_xe, TT + 2)
            for k in range(KT):
                dve.tensor_scalar(hT[:, k, :], hT[:, k, :], a1[:, k:k + 1], mod[:, k:k + 1], ALU.mult, ALU.add)\
                    .then_inc(s_h, 1)
            for b in range(2):
                link(dve.memset(xpad[:, b, 0:4], 0.0), wait=(b == 1))
            lc = Link(dve, s_dve3, 0, 4 * 3)
            with dve.Fori(0, 2) as i:
                lc.at(i)
                for j in range(4):
                    n = 4 * i + j
                    hold(dve, s_ev[j % 2], U_XR // 2 + 2 * i + j // 2 + 2)
                    y = xcT[:, ds(n, 1), :].rearrange("p o n -> p (o n)")
                    lc(dve.tensor_scalar(y, xpad[:, j % 2, 4:4 + T], cw[:, ds(3 * KT + n, 1)], cb[:, ds(n, 1)],
                                         ALU.mult, ALU.add))
                    for tap in (2, 1, 0):
                        ins = stt(out=y, in0=xpad[:, j % 2, 1 + tap:1 + tap + T], scalar=cw[:, ds(tap * KT + n, 1)],
                                  in1=y, op0=ALU.mult, op1=ALU.add)
                        if tap:
                            lc(ins)
                        else:
                            ins.then_inc(s_xc, 1)
            lg = Link(dve, s_dve4, 0, 4 * 6)
            with dve.Fori(0, 2) as i:
                lg.at(i)
                for j in range(4):
                    n = 4 * i + j
                    y = xcT[:, ds(n, 1), :].rearrange("p o n -> p (o n)")
                    hold(dve, s_t, n + 1)
                    lg(dve.tensor_scalar(hsT[:, :], tT[:, :], 1.0, None, ALU.add))
                    lg(dve.reciprocal(hsT[:, :], hsT[:, :]))
                    stt(out=mT[:, :], in0=tT[:, :], scalar=2.0, in1=hsT[:, :], op0=ALU.mult, op1=ALU.mult)\
                        .then_inc(s_m2, 1)
                    hold(dve, s_ig, n + 2)
                    lg(dve.tensor_tensor(ixT[:, :], iT[:, :], y, ALU.mult), wait=False)
                    hold(dve, s_m, n + 1)
                    lg(dve.memset(mT[:, 0:1], 1.0))
                    lg(dve.tensor_tensor(ixT[:, :], ixT[:, :], mT[:, :], ALU.mult))
                    hold(dve, s_a, n + 1)
                    lg(dve.tensor_tensor_scan(out=hsT[:, :], data0=aT[:, :], data1=ixT[:, :], initial=0.0,
                                              op0=ALU.mult, op1=ALU.add))
                    hold(dve, s_ev[j % 2], U_GR // 2 + 2 * i + j // 2 + 2)
                    dve.tensor_tensor(y, hsT[:, :], geT[:, :], ALU.mult).then_inc(s_yr, 1)
            with dve.Fori(0, 2) as i:
                for j in range(4):
                    n = 4 * i + j
                    g = gT[:, ds(n, 1), :].rearrange("p o n -> p (o n)")
                    hold(dve, s_mm, U_YA + n + 1)
                    dve.tensor_tensor(g, g, pair(j % 2), ALU.mult).then_inc(s_ev[j % 2], 1)

            la = Link(dve, s_dve5, 0, 2 * (2 + 16))
            with dve.Fori(0, NH // 2) as i:
                la.at(i)
                for b in range(2):
                    h = 2 * i + b
                    la(dve.tensor_scalar(B8[:, :], R[:, :], SL[:, ds(h, 1)], None, ALU.mult))
                    la(dve.tensor_tensor(B8[:, T - P:T], B8[:, T - P:T], MASK[:, :], ALU.add))

                    def soft(qt):
                        L = (qt + 1) * P
                        for c in range(2):
                            m = 2 * (qt % 2) + c
                            hold(dve, s_S, 16 * h + 2 * qt + c + 1)
                            if qt >= 2:
                                hold(dve, s_T, 12 * h + group(qt - 1))
                            dve.tensor_tensor_reduce(out=SM[:, qt % 2, c, 0:L], in0=pair(c)[:, 0:L],
                                                     in1=B8[:, T - L:T], scale=-HD ** -0.5, scalar=3e38,
                                                     op0=ALU.add, op1=ALU.min,
                                                     accum_out=mn[:, m:m + 1]).then_inc(s_ev[c], 1)

                    def merge(qt):
                        L = (qt + 1) * P
                        q = 2 * (qt % 2)
                        dve.wait_ge(s_e, 16 * h + 2 * qt + 2)
                        hold(dve, s_oe, 8 * h + qt + 1)
                        la(dve.reciprocal(rl[:, q:q + 2], lsum[:, q:q + 2]))
                        la(dve.tensor_scalar(c1[:, qt % 2:qt % 2 + 1], rl[:, q + 1:q + 2], nlam[:, 0:1],
                                             lsum[:, q:q + 1], ALU.mult, ALU.mult))
                        stt(out=SM[:, qt % 2, 0, 0:L], in0=SM[:, qt % 2, 1, 0:L], scalar=c1[:, qt % 2:qt % 2 + 1],
                            in1=SM[:, qt % 2, 0, 0:L], op0=ALU.mult, op1=ALU.add).then_inc(s_A, 1)

                    soft(0)
                    for qt in range(TT):
                        if qt + 1 < TT:
                            soft(qt + 1)
                        merge(qt)

            ln = Link(dve, s_dve6, 0, 2 * 2)
            dve.wait_ge(s_oe, 8 * NH + 2)
            with dve.Fori(0, TT // 2) as i:
                ln.at(i)
                for b in range(2):
                    t = 2 * i + b
                    o = ON[:, ds(t, 1), :].rearrange("p o n -> p (o n)")
                    ln(dve.tensor_tensor(sq[:, :], o, o, ALU.mult))
                    dve.tensor_reduce(ssn[:, b * NH:(b + 1) * NH], sq[:, :].rearrange("p (h n) -> p h n", h=NH),
                                      AX.X, ALU.add).then_inc(s_nss, 1)
                    hold(dve, s_nrm, t + 1)
                    ln(dve.reciprocal(rsn[:, b * NH:(b + 1) * NH], rmn[:, b * NH:(b + 1) * NH]))
                    hold(dve, s_oTe, t + 1)
                    dve.tensor_tensor(on2[:, b, :].rearrange("p (h n) -> p h n", h=NH),
                                      o.rearrange("p (h n) -> p h n", h=NH),
                                      rsn[:, b * NH:(b + 1) * NH].rearrange("p (h o) -> p h o", o=1)
                                      .broadcast_to([P, NH, P]), ALU.mult).then_inc(s_on, 1)
            lm = Link(dve, s_dve7, 0, 2)
            with dve.Fori(0, 4) as i:
                lm.at(i)
                for j in range(2):
                    n = 2 * i + j
                    g = gT[:, ds(n, 1), :].rearrange("p o n -> p (o n)")
                    dve.wait_ge(s_mm, U_GB + 2 * n + 2)
                    dve.wait_ge(s_mg, n + 2)
                    hold(dve, s_ev[0], EV_ATT + NH * EV_PER_HEAD + n + 1)
                    dve.tensor_tensor(ty[:, :], sg[:, j, :], pair(1), ALU.mult).then_inc(s_ev[1], 1)
                    hold(dve, s_ev[1], EV_ATT + NH * EV_PER_HEAD + n + 1)
                    dve.tensor_tensor(g, g, ty[:, :], ALU.add).then_inc(s_mg, 1)
            dve.wait_ge(s_mod, 12 + 2)
            dve.tensor_tensor(mod[:, 16:48], PS[:, MODB, 16:48], bada[:, 16:48], ALU.add).then_inc(s_mod2, 1)
            dve.wait_ge(s_mod2, 1)
            link(dve.tensor_tensor(rows_c[:, 0:8], mod[:, 16:24], gpo[:, :], ALU.mult), wait=False)
            link(stt(out=rows_c[:, 8:16], in0=mod[:, 32:40], scalar=1.0, in1=gpf[:, :], op0=ALU.add, op1=ALU.mult),
                 wait=False)
            link(dve.tensor_copy(rows_c[:, 16:24], mod[:, 24:32]), wait=False)
            link(dve.tensor_tensor(rows_c[:, 24:32], mod[:, 40:48], gpo2[:, :], ALU.mult))
            for m in range(4 * KT):
                if m >= 2:
                    dve.wait_ge(s_bc, m - 1)
                dve.tensor_scalar(dg[:, m % 2, :], ident[:, :], rows_c[:, m:m + 1], None, ALU.mult).then_inc(s_dg, 1)
            dve.wait_ge(s_rows, 4 * KT)
            lx = Link(dve, s_dve8, 0, 2 * 4)
            with dve.Fori(0, TT // 2) as i:
                lx.at(i)
                for b in range(2):
                    t = 2 * i + b
                    y = Y[:, ds(t, 1), :].rearrange("p o n -> p (o n)")
                    hold(dve, s_yrm, 2 * t + 1)
                    lx(dve.reciprocal(rstd[:, ds(t, 1)], rms[:, ds(t, 1)]))
                    lx(stt(out=y, in0=y, scalar=rstd[:, ds(t, 1)], in1=ROWS[:, 0, :], op0=ALU.mult, op1=ALU.mult))
                    hold(dve, s_x[b], 16 * (TT // 2) + 16 * i + 16)
                    dve.tensor_tensor(y, y, xin[:, b, :], ALU.add).then_inc(s_x1, 1)
                    hold(dve, s_yrm, 2 * t + 2)
                    lx(dve.reciprocal(rstd[:, ds(t, 1)], rms[:, ds(t, 1)]))
                    dve.wait_ge(s_h2e, t + 1)
                    hold(dve, s_h2d[b], 16 * i + 16)
                    lx(stt(out=h2t[:, b, :], in0=y, scalar=rstd[:, ds(t, 1)], in1=ROWS[:, 1, :],
                           op0=ALU.mult, op1=ALU.mult))
                    dve.tensor_tensor(h2t[:, b, :], h2t[:, b, :], ROWS[:, 2, :], ALU.add).then_inc(s_h2, 1)
            if STAGE == "x1":
                return
            dve.sem_inc(s_xed, 1)
            dve.sem_inc(ro["yd"], 1)
            lr = Link(dve, s_dr)
            dve.wait_ge(s_ld, 48)
            dve.wait_ge(s_c2, 13)

            def over(ap, n, last):
                m = ap.shape[1]
                if last:
                    return ap.rearrange("p (o m) -> p o m", o=1).broadcast_to([P, n, m])
                return ap.rearrange("p (m o) -> p m o", o=1).broadcast_to([P, m, n])

            def route(t):
                ix = idxf[:, t * TOP:(t + 1) * TOP]
                dve.wait_ge(s_sco, t + 1)
                lr(dve.tensor_tensor(cho[:, :], sco[:, :], ebias[:, :], ALU.add))
                for g in range(NG):
                    lr(dve.max(g8[:, g * 8:(g + 1) * 8], cho[:, g * 8:(g + 1) * 8]), wait=(g == NG - 1))
                g3 = g8[:, :].rearrange("p (g n) -> p g n", g=NG)
                lr(dve.tensor_tensor(gs[:, :], g3[:, :, 0], g3[:, :, 1], ALU.add))
                lr(dve.max(gv[:, :], gs[:, :]))
                lr(dve.max_index(gi[:, :], gv[:, :], gs[:, :]))
                lr(dve.tensor_copy(gif[:, :], gi[:, :]))
                m4 = gm4[:, :].rearrange("p (k g) -> p k g", k=TOPG)
                lr(dve.tensor_tensor(m4, over(io64[:, 0:NG], TOPG, True), over(gif[:, 0:TOPG], NG, False),
                                     ALU.is_equal))
                lr(dve.tensor_reduce(gmk[:, :], gm4[:, :].rearrange("p (k g) -> p g k", k=TOPG), AX.X, ALU.add))
                lr(dve.tensor_scalar(gmk[:, :], gmk[:, :], -1.0, -MASKED, ALU.add, ALU.mult))
                c3 = cho[:, :].rearrange("p (g n) -> p g n", g=NG)
                lr(dve.tensor_tensor(c3, c3, over(gmk[:, :], NE // NG, False), ALU.add))
                lr(dve.max(v8[:, :], cho[:, :]))
                lr(dve.max_index(i8[:, :], v8[:, :], cho[:, :]))
                lr(dve.tensor_copy(ix, i8[:, :]))
                lr(dve.tensor_tensor(oh[:, :, :], over(io64[:, :], TOP, True), over(ix, NE, False), ALU.is_equal))
                lr(dve.tensor_tensor(oh2[:, :, :], oh[:, :, :], over(sco[:, :], TOP, True), ALU.mult))
                lr(dve.tensor_reduce(w8[:, :], oh2[:, :, :], AX.X, ALU.add))
                lr(dve.tensor_reduce(wsm[:, :], w8[:, :], AX.X, ALU.add))
                lr(dve.tensor_scalar(wsm[:, :], wsm[:, :], 1e-20, None, ALU.add))
                lr(dve.reciprocal(wsm[:, :], wsm[:, :]))
                pw = pairs[:, :].rearrange("p (t k c) -> p t k c", t=TT, k=TOP)[:, t, :, 1]
                lr(dve.tensor_scalar(pw, w8[:, :], wsm[:, 0:1], ROUTED_SCALE, ALU.mult, ALU.mult))
                dve.tensor_reduce(M[:, t, :], oh[:, :, :].rearrange("p k e -> p e k"), AX.X, ALU.add).then_inc(s_M, 1)
                dve.wait_ge(s_M, t + 1)

            def hidden(S, g, b):
                hold(dve, S["sg"], g + 1)
                dve.tensor_tensor(sgm[:, b, :], sgm[:, b, :], PS[:, 2 + b, 0:FE], ALU.mult).then_inc(S["t"], 1)
                hold(dve, S["t"], g + 1)
                dve.tensor_tensor(hb[:, b, :], sgm[:, b, :], PS[:, 2 + b, FE:2 * FE], ALU.mult).then_inc(S["hb"], 1)

            for t in range(TT):
                route(t)
            for t in range(TT + 1):
                if t < TT:
                    hidden(sh, t, t % 2)
                if t >= 1:
                    dve.wait_ge(sh["dn"], t)
                    if t >= 3:
                        dve.wait_ge(s_shst[(t - 1) % 2], 16 * ((t - 1) // 2))
                    dve.tensor_copy(yo[:, (t - 1) % 2, HALF:D], PS[:, 5, :]).then_inc(sh["yd"], 1)
            dve.wait_ge(s_rk, 1)
            cmp = oh[:, :, :].rearrange("p k e -> p (k e)").rearrange("p (e k) -> p e k", k=8)
            lr(dve.tensor_copy(nbk[:, :], PS[:, 1, 0:NE]))
            lr(dve.tensor_tensor(cmp, over(nbk[:, :], 8, False), over(thr[:, :], NE, True), ALU.is_gt))
            lr(dve.tensor_reduce(nbk[:, :], cmp, AX.X, ALU.add))
            lr(dve.tensor_scalar(nbk[:, :], nbk[:, :], 1.0, None, ALU.add))
            lr(dve.tensor_tensor_scan(out=pend[:, :], data0=ones[:, 0:NE], data1=nbk[:, :], initial=0.0,
                                      op0=ALU.mult, op1=ALU.add))
            lr(dve.tensor_tensor(pst[:, :], pend[:, :], nbk[:, :], ALU.subtract))
            lr(dve.tensor_scalar(pst[:, :], pst[:, :], float(P), None, ALU.mult))
            for t in range(TT):
                lr(dve.tensor_tensor(posab[:, :], PS[:, 0, t * NE:(t + 1) * NE], pst[:, :], ALU.add))
                lr(dve.tensor_tensor(oh[:, :, :], over(io64[:, :], TOP, True),
                                     over(idxf[:, t * TOP:(t + 1) * TOP], NE, False), ALU.is_equal))
                lr(dve.tensor_tensor(oh2[:, :, :], oh[:, :, :], over(posab[:, :], TOP, True), ALU.mult))
                lr(dve.tensor_reduce(slotf[:, t * TOP:(t + 1) * TOP], oh2[:, :, :], AX.X, ALU.add))
            dve.tensor_copy(slots[:, :], slotf[:, :]).then_inc(s_slot, 1)
            lr(dve.tensor_scalar(posab[:, :], pend[:, :], ioP[:, 0:1], None, ALU.is_le))
            lr(dve.tensor_reduce(eidf[:, :], posab[:, :], AX.X, ALU.add))
            lr(dve.tensor_scalar(eidf[:, :], eidf[:, :], float(NE - 1), None, ALU.min))
            lr(dve.tensor_scalar(ehi[:, :], eidf[:, :], 0.5, -0.25, ALU.mult, ALU.add))
            lr(dve.tensor_copy(ehf[:, :], ehi[:, :]))
            lr(stt(out=tbf[:, 0:1], in0=ehf[:, :], scalar=-2.0, in1=eidf[:, :], op0=ALU.mult, op1=ALU.add))
            lr(dve.tensor_scalar(tbf[:, 1:2], ehf[:, :], 1.0, None, ALU.add))
            lr(dve.tensor_tensor(tbf[:, 2:3], ehf[:, :], tbf[:, 0:1], ALU.add))
            lr(dve.tensor_scalar(tbf[:, 2:3], tbf[:, 2:3], 1.0, None, ALU.max))
            lr(dve.tensor_copy(tbf[:, 3:4], eidf[:, :]))
            lr(dve.tensor_scalar(npf[:, :], pend[:, NE - 1:NE], -0.5, 0.5, ALU.add, ALU.mult))
            lr(dve.tensor_copy(pendi[:, 0:NE], pend[:, :]))
            lr(dve.tensor_copy(pendi[:, NE:NE + 1], npf[:, :]))
            dve.tensor_copy(tbi[:, :], tbf[:, :]).then_inc(s_eid, 2)

            for b in range(2):
                dve.wait_ge(s_shst[b], 16 * TT // 2)
            dve.wait_ge(s_eid, 2)
            np_ = dve.value_load(pendi[0:1, NE:NE + 1], min_val=1, max_val=NBLK // 2 - 1)

            dve.wait_ge(s_tabc, 2)

            def rows_turned(g, b):
                hold(dve, s_xgT, g + 1)
                dve.tensor_copy(xT[:, b, 4:8, :].rearrange("p k n -> p (k n)"), PS[:, 1, :]).then_inc(s_xed, 1)

            def out_half(g, b, done):
                hold(dve, ro["dn"], g + 1)
                hold(dve, ro["st"], done)
                dve.tensor_scalar(yo[:, b, HALF:D], PS[:, 5, :], wtT[:, ds(g, 1)], None, ALU.mult)\
                    .then_inc(ro["yd"], 1)

            rows_turned(0, 0)
            hidden(ro, 0, 0)
            rows_turned(1, 1)
            with dve.Fori(0, np_) as i:
                for j in range(2):
                    g = 2 * i + j + 1
                    hidden(ro, g, 1 - j)
                    out_half(g - 1, j, 16 * g)
                    rows_turned(g + 1, j)
            out_half(2 * np_, 0, 32 * np_ + 16)
            lf = Link(dve, s_fdv)
            for t in range(TT):
                dve.wait_ge(s_frm, t + 1)
                lf(dve.reciprocal(rstd[:, t:t + 1], rms[:, t:t + 1]))
                if t >= 2:
                    dve.wait_ge(s_fst[t % 2], 16 * (t // 2))
                lf(stt(out=fin[:, t % 2, :], in0=xg[:, t % 2, :], scalar=rstd[:, t:t + 1], in1=ROWS[:, 3, :],
                       op0=ALU.mult, op1=ALU.mult))
                dve.tensor_tensor(fin[:, t % 2, :], fin[:, t % 2, :], Y[:, t, :], ALU.add).then_inc(s_fo, 1)


_INS = ["x", "c", "w_ada", "b_ada", "g_pre_mix", "w_in", "conv_w", "conv_b", "lru_wa", "lru_ba", "lru_wx", "lru_bx",
        "lru_lambda", "lam_q1", "lam_k1", "lam_q2", "lam_k2", "g_subln", "w_proj_rnn", "w_proj_att", "w_out",
        "g_post_mix", "g_pre_ffn", "w_router", "e_bias", "w1_e", "w3_e", "w2_e", "w1_s", "w3_s", "w2_s", "g_post_ffn"]


def kernel(**inputs):
    import numpy as _np
    import concourse.bacc as _bacc
    from concourse import mybir as _mybir
    from concourse.bass_utils import run_bass_kernel_spmd as _run

    nc = _bacc.Bacc("TRN2", target_bir_lowering=False, num_devices=1)
    arrays, args = {}, {}
    for name in _INS:
        v = _np.ascontiguousarray(inputs[name])
        arrays[f"in_{name}_dram"] = v
        args[name] = nc.dram_tensor(f"in_{name}_dram", v.shape, _mybir.dt.from_np(v.dtype), kind="ExternalInput").ap()
    out = nc.dram_tensor("out_0_dram", (1, T, D), _mybir.dt.from_np(_np.dtype("float32")), kind="ExternalOutput").ap()
    layer(nc, args, out)
    r = _run(nc, [arrays], core_ids=[0])
    return r.results[0]["out_0_dram"]
```

```python
import math
import concourse.bass as bass
from concourse import mybir
from contextlib import ExitStack

P = 128
D = 1024
T = 1024
KT = D // P
TT = T // P
NH = 8
HD = 64
HALF = 512
EPS = 1e-6
LRU_C = 8.0
LAM_INIT = 0.8 - 0.6 * math.exp(-0.3 * 0)
MASKED = -1e30
NE = 64
TOP = 8
NG = 8
TOPG = 4
FE = 256
FT = FE // P
ROUTED_SCALE = 2.5
NBLK = T * TOP // P + NE
COL_XR, COL_GR, COL_Q, COL_K, COL_V, COL_GA, COL_GB = (i * D for i in range(7))


def layer(nc, a, out):
    fp32 = mybir.dt.float32
    ACT = mybir.ActivationFunctionType
    ALU = mybir.AluOpType
    AX = mybir.AxisListType
    ds = bass.ds
    ctx = ExitStack()
    with ctx:
        base = 17 * 1024

        def at(name, kb, shape, dt=fp32):
            return nc.alloc_sbuf_tensor_at(name, shape, dt, offset=base + int(kb * 1024))

        def sem(name):
            return ctx.enter_context(nc.semaphore(name))

        hT = at("hT", 0, [P, KT, T])
        xcT = at("xcT", 32, [P, KT, T])
        V = at("V", 32, [P, TT, D])
        oT = at("oT", 32, [P, KT, T])
        ON = at("ON", 64, [P, TT, D])
        Y = at("Y", 64, [P, TT, D])
        gT = at("gateT", 96, [P, KT, T])
        WT = at("WT", 128, [P, 4, KT, P])
        TMP = 144
        XS = at("XS", 32, [P, TT, D])
        junk = at("junk", TMP + 32, [P, D])
        AW = at("AW", 64, [P, 2, KT, HALF])
        xpad = at("xpad", TMP, [P, 2, 4 + T])
        rT = at("rT", TMP + 9, [P, T])
        iT = at("iT", TMP + 13, [P, T])
        tT = at("tT", TMP + 17, [P, T])
        aT = at("aT", TMP + 21, [P, T])
        mT = at("mT", TMP + 25, [P, T])
        geT = at("geT", TMP + 29, [P, T])
        hsT = at("hsT", TMP + 33, [P, T])
        ixT = at("ixT", TMP + 37, [P, T])
        GW = at("GW", TMP + 41, [P, 4, 2, P])
        SM = at("SM", TMP, [P, 2, 2, T])
        PT = at("PT", TMP + 16, [P, 2, TT, P])
        qT = at("qT", TMP + 24, [P, 2, T])
        kT = at("kT", TMP + 32, [P, 2, T])
        sq = at("sq", TMP + 24, [P, 2, D])
        sg = at("sg", TMP + 32, [P, 2, T])
        on2 = at("on2", TMP + 16, [P, 2, D])
        ty = at("ty", TMP + 40, [P, T])
        ROWS = at("ROWS", TMP, [P, 4, D])
        dg = at("dg", TMP + 24, [P, 2, KT, P])
        h2t = at("h2t", 32, [P, TT, D])
        W13 = at("W13", 32, [P, 2, KT, 2 * FE])
        W2 = at("W2", 96, [P, 2, FT, D])
        W2s = at("W2s", 112, [P, FT, D])
        sgm = at("sgm", 120, [P, 2, FE])
        hb = at("hb", 122, [P, 2, FE])
        hbT = at("hbT", 124, [P, 2, FT, P])
        xg = at("xg", TMP + 16, [P, 2, D])
        xT = at("xT", TMP + 24, [P, 2, KT, P])
        yo = at("yo", TMP + 32, [P, 2, D])
        wr = at("wr", TMP + 40, [P, KT, NE])
        M = at("M", TMP + 42, [P, TT, NE])
        oh = at("oh", 48, [P, TT * TOP, NE])
        oh2 = at("oh2", 32, [P, TT * TOP, NE])
        sco = at("sco", TMP + 16, [P, TT, NE])
        cho = at("cho", TMP + 18, [P, TT, NE])
        pos = at("pos", TMP + 20, [P, TT, NE])
        g8 = at("g8", TMP + 22, [P, TT * NG, 8])
        gm4 = at("gm4", TMP + 24, [P, TT, TOPG, NG])
        i32 = mybir.dt.int32
        u32 = mybir.dt.uint32
        tab = at("tab", TMP, [P, P, 2])
        tokT = at("tokT", TMP + 1, [P, P + 8], i32)
        wtT = at("wtT", TMP + 2, [P, P])
        FS = at("FS", 0, [P, TT, D])
        vr0 = at("vr0", TMP + 44, [P, P])
        vr1 = at("vr1", TMP + 44.5, [3 * KT + 1, P])
        CON = 192
        ident = at("ident", CON, [P, P])
        ones = at("ones", CON + .5, [P, P])
        MASK = at("MASK", CON + 1, [P, P])
        R = at("R", CON + 2, [P, T])
        B8 = at("B8", CON + 6, [P, T])
        sm0 = CON + 10
        small_at = [int(sm0 * 256)]

        def small(name, n, dt=fp32, parts=P):
            t = at(name, small_at[0] / 256, [parts, n], dt)
            small_at[0] += -(-n // 8) * 8
            assert small_at[0] <= 207 * 256 - 64, small_at
            return t

        vc0 = small("vc0", P)
        vc1 = small("vc1", 3 * KT + 1)
        ccol, bada = vc0[:, 0:8], vc0[:, 8:56]
        gpm, gpo, gpf, gpo2, cb = (vc0[:, 56 + 8 * j:64 + 8 * j] for j in range(5))
        cw = vc0[:, 96:128]
        ba, bx, lamc, gsub = vc1[:, 0:8], vc1[:, 8:16], vc1[:, 16:24], vc1[:, 24:25]
        cond = small("cond", KT)
        mod = small("mod", 48)
        rows_c = small("rows_c", 4 * KT)
        a1 = small("a1", KT)
        sp8 = small("sp8", KT)
        nsp8 = small("nsp8", KT)
        spt = small("spt", 4 * KT)
        gsub8 = small("gsub8", 1)
        lqk = small("lqk", 4 * HD, parts=1)
        lpr = small("lpr", HD, parts=1)
        ls = small("ls", 8, parts=1)
        nlam = small("nlam", 1)
        SL = small("SL", NH)
        ss = small("ss", TT)
        rms = small("rms", TT)
        rstd = small("rstd", TT)
        ssn = small("ssn", TT * NH)
        mn = small("mn", 4)
        lsum = small("lsum", 4)
        rl = small("rl", 4)
        c1 = small("c1", 2)
        eps = small("eps", 1)
        small_at[0] = int((CON + 2) * 256)
        tri = small("tri", P)
        ebias = small("ebias", NE)
        io64 = small("io64", NE)
        ioP = small("ioP", 1)
        thr = small("thr", 8)
        gs = small("gs", TT * NG)
        gv = small("gv", TT * 8)
        gi = small("gi", TT * 8, u32)
        gif = small("gif", TT * 8)
        gmk = small("gmk", TT * NG)
        v8 = small("v8", TT * 8)
        i8 = small("i8", TT * 8, u32)
        idxf = small("idxf", TT * TOP)
        w8 = small("w8", TT * TOP)
        wsm = small("wsm", TT)
        pairs = small("pairs", TT * TOP * 2)
        slotf = small("slotf", TT * TOP)
        slots = small("slots", TT * TOP, i32)
        posab = small("posab", NE)
        nbk = small("nbk", NE)
        pend = small("pend", NE)
        pst = small("pst", NE)
        eidf = small("eidf", 1)
        ehi = small("ehi", 1, i32)
        ehf = small("ehf", 1)
        tbf = small("tbf", 4)
        tbi = small("tbi", 4, i32)
        pendi = small("pendi", NE + 8, i32)
        npf = small("npf", 1)
        idxb = small("idxb", 2, i32)
        sidx = small("sidx", 2, i32)
        tbrow = small("tbrow", 4 * P, i32, parts=1)

        PS = ctx.enter_context(nc.psum_tensor("PS", [P, 8, HALF], fp32))

        def pair(p):
            return PS[:, 2 * p:2 * p + 2, :].rearrange("p b n -> p (b n)")

        acc = nc.dram_tensor("moe_sum_dram", (T + P, D), fp32, kind="Internal").ap()
        tabd = nc.dram_tensor("slot_table_dram", (P * P, 2), fp32, kind="Internal").ap()
        tbd = nc.dram_tensor("block_table_dram", (P, 4), i32, kind="Internal").ap()
        h2d = nc.dram_tensor("h2_dram", (T + P, D), fp32, kind="Internal").ap()

        s_small = sem("s_small")
        s_vt = sem("s_vt")
        s_vc = sem("s_vc")
        s_x = [sem(f"s_xin{j}") for j in range(TT // 2)]
        s_ada = [sem("s_ada0"), sem("s_ada1")]
        s_w = [sem(f"s_w{j}") for j in range(4)]
        s_gw = [sem(f"s_gw{j}") for j in range(4)]
        s_const = sem("s_const")
        s_pool = sem("s_pool")
        s_cond = sem("s_cond")
        s_mod = sem("s_mod")
        s_modu = sem("s_modu")
        s_ss = sem("s_ss")
        s_rms = sem("s_rms")
        s_xn = sem("s_xn")
        s_xt = sem("s_xt")
        s_xe = sem("s_xe")
        s_dve = sem("s_dve")
        s_dve2 = sem("s_dve2")
        s_dve3 = sem("s_dve3")
        s_dve4 = sem("s_dve4")
        s_dve5 = sem("s_dve5")
        s_dve6 = sem("s_dve6")
        s_dve7 = sem("s_dve7")
        s_dve8 = sem("s_dve8")
        s_lnp = sem("s_lnp")
        s_act = sem("s_act")
        s_act2 = sem("s_act2")
        s_h = sem("s_h")
        s_mm = sem("s_mm")
        s_ev = [sem("s_ev0"), sem("s_ev1")]
        s_xc = sem("s_xc")
        s_gate = sem("s_gate")
        s_ig = sem("s_ig")
        s_t = sem("s_t")
        s_a = sem("s_a")
        s_m2 = sem("s_m2")
        s_m = sem("s_m")
        s_yr = sem("s_yr")
        s_lam = sem("s_lam")
        s_lamp = sem("s_lamp")
        s_lamb = sem("s_lamb")
        s_S = sem("s_S")
        s_e = sem("s_e")
        s_A = sem("s_A")
        s_T = sem("s_T")
        s_pte = sem("s_pte")
        s_pv = sem("s_pv")
        s_oe = sem("s_oe")
        s_nss = sem("s_nss")
        s_sq = sem("s_sq")
        s_nrm = sem("s_nrm")
        s_on = sem("s_on")
        s_oT = sem("s_oT")
        s_oTe = sem("s_oTe")
        s_mg = sem("s_mg")
        s_mod2 = sem("s_mod2")
        s_dg = sem("s_dg")
        s_bc = sem("s_bc")
        s_rows = sem("s_rows")
        s_yss = sem("s_yss")
        s_yrm = sem("s_yrm")
        s_x1 = sem("s_x1")
        s_h2 = sem("s_h2")
        s_h2T = sem("s_h2T")
        s_h2e = sem("s_h2e")
        s_h2p = sem("s_h2p")
        s_h2d = [sem("s_h2d0"), sem("s_h2d1")]
        s_out = sem("s_out")
        s_ld = sem("s_ld")
        s_lg = sem("s_lg")
        s_sco = sem("s_sco")
        s_dr = sem("s_dr")
        s_M = sem("s_M")
        s_rk = sem("s_rk")
        s_slot = sem("s_slot")
        s_c2 = sem("s_c2")
        s_tb0 = sem("s_tb0")
        s_sct = sem("s_sct")
        s_tab = sem("s_tab")
        s_tabT = sem("s_tabT")
        s_tabc = sem("s_tabc")
        s_eid = sem("s_eid")
        s_tbd = sem("s_tbd")
        s_tbr = sem("s_tbr")
        s_acc0 = sem("s_acc0")
        sh = {n: sem("s_sh_" + n) for n in ("up", "sg", "t", "hb", "hT", "he", "dn", "ya", "yd", "st")}
        ro = {n: sem("s_ro_" + n) for n in ("up", "sg", "t", "hb", "hT", "he", "dn", "ya", "yd", "st")}
        s_shst = [sem("s_shst0"), sem("s_shst1")]
        s_w13 = [sem("s_w13_0"), sem("s_w13_1")]
        s_w2 = [sem("s_w2_0"), sem("s_w2_1")]
        s_ix = sem("s_ix")
        s_xg = [sem("s_xg0"), sem("s_xg1")]
        s_xgT = sem("s_xgT")
        s_xea = sem("s_xea")
        s_xed = sem("s_xed")
        s_six = sem("s_six")
        s_fl = [sem(f"s_fl{j}") for j in range(TT)]
        s_fss = sem("s_fss")
        s_frm = sem("s_frm")
        s_fdv = sem("s_fdv")
        s_fo = sem("s_fo")
        s_fst = sem("s_fst")

        def vector_rows():
            r = 0
            for name in ("c", "b_ada", "g_pre_mix", "g_post_mix", "g_pre_ffn", "g_post_ffn", "conv_b"):
                src = a[name][0].rearrange("(k p) -> k p", p=P)
                yield vr0, r, src
                r += src.shape[0]
            yield vr0, r, a["conv_w"][0].rearrange("j (k p) -> (j k) p", p=P)
            yield vr1, 0, a["lru_ba"][0]
            yield vr1, KT, a["lru_bx"][0]
            yield vr1, 2 * KT, a["lru_lambda"][0].rearrange("(k p) -> k p", p=P)
            yield vr1, 3 * KT, a["g_subln"]

        N_SMALL = 12 + 4
        s_turn = {e: sem(f"s_turn_{e.name}") for e in (nc.sync.engine, nc.scalar.engine, nc.vector.engine,
                                                        nc.tensor.engine, nc.gpsimd.engine)}
        U_XR, U_GR, U_GA, U_YA, U_V, U_QK, U_GB, U_O, U_SH = 0, 8, 16, 24, 32, 40, 56, 72, 80
        EV_PER_HEAD = 9
        EV_ATT = U_QK // 2 + 1

        class Link:

            def __init__(self, eng, s, start=0, per=0):
                self.eng, self.s, self.start, self.per, self.n, self.i = eng, s, start, per, 0, None

            def at(self, i):
                self.i, self.n = i, 0

            def __call__(self, ins, wait=True):
                ins.then_inc(self.s, 1)
                self.n += 1
                if wait:
                    self.wait()

            def wait(self):
                v = self.start + self.n
                hold(self.eng, self.s, v if self.i is None else self.i * self.per + v)

        def hold(eng, s, value):
            eng.wait_ge(s, value)
            eng.sem_inc(s_turn[eng.engine], 1)

        block = ctx.enter_context(nc.Block())

        def wtile(W, col):
            return W[:, col].rearrange("(k p) c -> p k c", p=P)

        @block.sync
        def _(sp):
            def x_tiles():
                for q in range(TT // 2):
                    sp.dma_start(XS[:, 2 * q:2 * q + 2, :], a["x"][0, 2 * P * q:2 * P * (q + 1), :]
                                 .rearrange("(t p) d -> p t d", p=P)).then_inc(s_x[q], 16)

            x_tiles()

            def tile(u, slot, W, c, quad):
                hold(sp, s_mm, quad if quad is not None else u - 3)
                sp.dma_start(WT[:, slot, :, :], wtile(W, ds(c, P))).then_inc(s_w[slot], 16)

            w_in = a["w_in"][0]
            for j in range(4):
                sp.dma_start(WT[:, j, :, :], wtile(w_in, ds(COL_XR + P * j, P))).then_inc(s_w[j], 16)
            for j in range(4):
                tile(U_XR + 4 + j, j, w_in, COL_XR + P * (4 + j), None)
            with sp.Fori(0, 2) as i:
                for j in range(4):
                    hold(sp, s_gate, 4 * i + j + 1)
                    for g, W in enumerate((a["lru_wa"], a["lru_wx"])):
                        sp.dma_start(GW[:, j, g, :], W[0, ds(4 * i + j, 1)].rearrange("o c d -> (o c) d"))\
                            .then_inc(s_gw[j], 16)
                    tile(U_GR + 4 * i + j, j, w_in, COL_GR + P * (4 * i + j), None)
            with sp.Fori(0, 2) as i:
                for j in range(4):
                    tile(U_GA + 4 * i + j, j, w_in, COL_GA + P * (4 * i + j), None)
            with sp.Fori(0, 2) as i:
                for j in range(4):
                    tile(U_YA + 4 * i + j, j, a["w_proj_rnn"][0], P * (4 * i + j), None)
            with sp.Fori(0, 2) as i:
                for j in range(4):
                    tile(0, j, w_in, COL_V + P * (4 * i + j), U_V + 4 * i)
            with sp.Fori(0, NH // 2) as i:
                for j in range(4):
                    h = 2 * i + j // 2
                    tile(0, j, w_in, (COL_Q if j % 2 == 0 else COL_K) + P * h, U_QK + 4 * i)
            with sp.Fori(0, 4) as i:
                for j in range(4):
                    n = 2 * i + j // 2
                    if j % 2 == 0:
                        tile(U_GB + 4 * i + j, j, w_in, COL_GB + P * n, None)
                    else:
                        tile(U_GB + 4 * i + j, j, a["w_proj_att"][0], P * n, None)
            for i in range(2):
                for j in range(4):
                    tile(0, j, a["w_out"][0], P * (4 * i + j), U_O + 4 * i)
                if i == 0:
                    x_tiles()
                    sp.wait_ge(s_mg, KT + 2)
                    sp.dma_start(wr[:, :, :], a["w_router"][0].rearrange("(k p) e -> p k e", p=P)).then_inc(s_ld, 16)
            for j, W in enumerate((a["w1_s"][0], a["w1_s"][0], a["w3_s"][0], a["w3_s"][0])):
                sp.wait_ge(s_mm, U_SH)
                sp.dma_start(WT[:, j, :, :], wtile(W, ds(P * (j % 2), P))).then_inc(s_w[j], 16)
            sp.wait_ge(s_h2p, 32)
            sp.dma_start(W2s[:, :, :], a["w2_s"][0].rearrange("(k p) n -> p k n", p=P)).then_inc(s_ld, 16)
            sp.dma_start(ebias[:, :], a["e_bias"].broadcast_to([P, NE])).then_inc(s_ld, 16)

            def expert_up(e, b):
                sp.dma_start(W13[:, b, :, 0:FE], a["w1_e"][0, ds(e, 1)].rearrange("o (k p) f -> p (o k) f", p=P))\
                    .then_inc(s_w13[b], 16)
                sp.dma_start(W13[:, b, :, FE:2 * FE], a["w3_e"][0, ds(e, 1)].rearrange("o (k p) f -> p (o k) f", p=P))\
                    .then_inc(s_w13[b], 16)

            def expert_down(e, b):
                sp.dma_start(W2[:, b, :, :], a["w2_e"][0, ds(e, 1)].rearrange("o (k p) n -> p (o k) n", p=P))\
                    .then_inc(s_w2[b], 16)

            for b in range(2):
                expert_down(b, b)
            sp.wait_ge(s_slot, 1)
            for b in range(2):
                expert_up(b, b)
            for t in range(TT):
                sp.wait_ge(sh["ya"], t + 1)
                sp.wait_ge(sh["yd"], t + 1)
                sp.dma_start(acc[t * P:(t + 1) * P, :], yo[:, t % 2, :]).then_inc(s_shst[t % 2], 16)
            sp.wait_ge(s_sct, 16 * TT * TOP)
            sp.dma_start(tab[:, :, :], tabd.rearrange("(g s) c -> g s c", s=P)).then_inc(s_tab, 16)
            sp.wait_ge(s_eid, 2)
            sp.dma_start(tbd, tbi[:, :]).then_inc(s_tbd, 16)
            sp.wait_ge(s_tbd, 16)
            sp.dma_start(tbrow[:, :], tbd.rearrange("(o g) c -> o (g c)", o=1)).then_inc(s_tbr, 16)
            with sp.Fori(0, NE // 2 - 1) as i:
                for b in range(2):
                    last = sp.value_load(pendi[0:1, ds(2 * i + b, 1)], min_val=1, max_val=NBLK)
                    hold(sp, ro["up"], last)
                    expert_up(2 * i + b + 2, b)
                    hold(sp, ro["dn"], last)
                    expert_down(2 * i + b + 2, b)
            pairs_n = sp.value_load(pendi[0:1, NE:NE + 1], min_val=1, max_val=NBLK // 2)
            hold(sp, ro["st"], 32 * pairs_n + 48)
            for t in range(TT):
                sp.dma_start(FS[:, t, :], acc[t * P:(t + 1) * P, :]).then_inc(s_fl[t], 16)
            for t in range(TT):
                sp.wait_ge(s_fo, t + 1)
                sp.dma_start(out[0, t * P:(t + 1) * P, :], FS[:, t, :]).then_inc(s_fst, 16)
            sp.wait_ge(s_fst, 16 * TT)
            hold(sp, s_xg[0], 16 * pairs_n + 32)

        @block.gpsimd
        def _(pool):
            link = Link(pool, s_pool)
            link(pool.memset(ident[:, :], 0.0))
            link(pool.affine_select(out=ident[:, :], in_=ident[:, :], compare_op=ALU.not_equal, fill=1.0, base=0,
                                    pattern=[[-1, P]], channel_multiplier=1))
            link(pool.memset(ones[:, :], 1.0), wait=False)
            link(pool.memset(MASK[:, :], 0.0))
            link(pool.affine_select(out=MASK[:, :], in_=MASK[:, :], compare_op=ALU.is_ge, fill=MASKED, base=0,
                                    pattern=[[-1, P]], channel_multiplier=1), wait=False)
            link(pool.iota(R[:, :], [[1, T]], base=P - T, channel_multiplier=-1,
                           allow_small_or_imprecise_dtypes=True), wait=False)
            for h in range(NH):
                link(pool.memset(SL[:, h:h + 1], 2.0 ** (-8.0 * (h + 1) / NH) * HD ** 0.5), wait=False)
            link.wait()
            pool.sem_inc(s_const, 1)

            def ada(lo, hi):
                with pool.Fori(lo, hi) as i:
                    for b in range(2):
                        pool.wait_ge(s_mod, 2 * i + b + 1)
                        pool.dma_start(AW[:, b, :, :], a["w_ada"][0][:, ds(HALF * (2 * i + b), HALF)]
                                       .rearrange("(k p) c -> p k c", p=P)).then_inc(s_ada[b], 16)

            ada(0, 6)
            for b in range(2):
                pool.dma_start(h2d[T + HD * b:T + HD * (b + 1), :], R[HD * b:HD * (b + 1), :]).then_inc(s_h2p, 16)
            with pool.Fori(0, TT // 2) as i:
                for b in range(2):
                    hold(pool, s_h2, 2 * i + b + 1)
                    pool.dma_start(h2d[ds(P * (2 * i + b), P), :], h2t[:, ds(2 * i + b, 1), :]
                                   .rearrange("p o n -> p (o n)")).then_inc(s_h2d[b], 16)
            pool.wait_ge(s_h2p, 32)
            lp = Link(pool, s_c2)
            lp(pool.memset(tri[:, :], 1.0))
            lp(pool.affine_select(out=tri[:, :], in_=tri[:, :], compare_op=ALU.is_gt, fill=0.0, base=0,
                                  pattern=[[1, P]], channel_multiplier=-1), wait=False)
            lp(pool.iota(io64[:, :], [[1, NE]], base=0, channel_multiplier=0, allow_small_or_imprecise_dtypes=True),
               wait=False)
            lp(pool.iota(ioP[:, :], [[0, 1]], base=0, channel_multiplier=1, allow_small_or_imprecise_dtypes=True),
               wait=False)
            lp(pool.iota(thr[:, :], [[P, 8]], base=P, channel_multiplier=0, allow_small_or_imprecise_dtypes=True),
               wait=False)
            pv = pairs[:, :].rearrange("p (t k c) -> p t k c", t=TT, k=TOP)
            for t in range(TT):
                lp(pool.iota(pv[:, t, :, 0], [[0, TOP]], base=t * P, channel_multiplier=1,
                             allow_small_or_imprecise_dtypes=True), wait=False)
            lp(pool.iota(tab[:, :, 0], [[1, P]], base=T, channel_multiplier=0, allow_small_or_imprecise_dtypes=True),
               wait=False)
            lp(pool.iota(tokT[:, P:P + 1], [[0, 1]], base=T, channel_multiplier=1), wait=False)
            lp(pool.memset(tab[:, :, 1], 0.0))
            pool.dma_start(tabd.rearrange("(g s) c -> g s c", s=P), tab[:, :, :]).then_inc(s_tb0, 16)
            pool.wait_ge(s_h2d[0], 16 * (TT // 2))
            pool.wait_ge(s_h2d[1], 16 * (TT // 2))
            for b in range(2):
                pool.dma_start(acc[T + HD * b:T + HD * (b + 1), :], ROWS[HD * b:HD * (b + 1), 3, :])\
                    .then_inc(ro["st"], 16)
            pool.wait_ge(s_tb0, 16)
            pool.wait_ge(s_slot, 1)
            for t in range(TT):
                for k in range(TOP):
                    pool.indirect_dma_start(tabd, bass.IndirectOffsetOnAxis(slots[:, t * TOP + k:t * TOP + k + 1], 0),
                                            pv[:, t, k, :], None).then_inc(s_sct, 16)

            def gather(g, b):
                lq(pool.tensor_copy(idxb[:, b:b + 1], tokT[:, ds(g, 1)]))
                pool.indirect_dma_start(xg[:, b, :], None, h2d, bass.IndirectOffsetOnAxis(idxb[:, b:b + 1], 0))\
                    .then_inc(s_xg[b], 16)

            def add(g, b, done):
                hold(pool, ro["ya"], g + 2)
                hold(pool, ro["yd"], g + 2)
                lq(pool.tensor_copy(sidx[:, b:b + 1], tokT[:, ds(g, 1)]))
                if done is not None:
                    hold(pool, ro["st"], done)
                pool.indirect_dma_start(acc, bass.IndirectOffsetOnAxis(sidx[:, b:b + 1], 0), yo[:, b, :], None,
                                        compute_op=ALU.add).then_inc(ro["st"], 16)

            pool.wait_ge(s_tabc, 2)
            pool.wait_ge(s_eid, 2)
            np_ = pool.value_load(pendi[0:1, NE:NE + 1], min_val=1, max_val=NBLK // 2 - 1)
            lq = Link(pool, s_ix, 0, 4)
            for b in range(2):
                gather(b, b)
            for b in range(2):
                pool.wait_ge(s_shst[b], 16 * TT // 2)
            pool.wait_ge(s_xgT, 1)
            gather(2, 0)
            lq.start, lq.n = 3, 0
            with pool.Fori(0, np_) as i:
                lq.at(i)
                for j in range(2):
                    g = 2 * i + j + 1
                    hold(pool, s_xgT, g + 1)
                    gather(g + 2, 1 - j)
                    add(g - 1, j, (2 * i + j) * 16 + 32)
            lq.i = np_
            lq.n = 0
            add(2 * np_, 0, 32 * np_ + 32)

        def unit(pe, slot, w_round, ev_at, p, moving):
            pe.wait_ge(s_w[slot], 16 * w_round)
            pe.wait_ge(s_ev[p], ev_at)
            for half in range(2):
                for k in range(KT):
                    last = pe.matmul(PS[:, 2 * p + half, :], WT[:, slot, k, :],
                                     moving[:, k, half * HALF:(half + 1) * HALF], start=(k == 0), stop=(k == KT - 1))
            last.then_inc(s_mm, 1)

        def rows_unit(pe, q, w_round, ev_at, p, lhs):
            if q == 0:
                for slot in range(4):
                    pe.wait_ge(s_w[slot], 16 * w_round)
            pe.wait_ge(s_ev[p], ev_at)
            for half in range(2):
                t = 2 * q + half
                for k in range(KT):
                    last = pe.matmul(PS[:, 2 * p + half, :], lhs[:, k, t * P:(t + 1) * P], WT[:, :, k, :],
                                     start=(k == 0), stop=(k == KT - 1))
            last.then_inc(s_mm, 1)

        MODB = 7

        def group(qt):
            return sum(t // 4 + 1 for t in range(qt))

        def tcols(buf, t):
            return buf[:, :, ds(t * P, P)]

        def pair3(p):
            return pair(p).rearrange("p (k n) -> p k n", k=KT)

        @block.tensor
        def _(pe):
            pe.sem_inc(s_pv, 2)
            pe.sem_inc(s_mod, 2)
            pe.sem_inc(s_gate, 4)
            pe.wait_ge(s_const, 1)
            pe.wait_ge(s_small, 16 * N_SMALL)
            pe.transpose(PS[:, 4, 0:P], vr0[:, :], ident[:, :])
            pe.transpose(PS[:, 5, 0:3 * KT + 1], vr1[:, :], ident[0:3 * KT + 1, 0:3 * KT + 1]).then_inc(s_vt, 1)

            def ada(lo, hi):
                with pe.Fori(lo, hi) as i:
                    for b in range(2):
                        pe.wait_ge(s_ada[b], 16 * i + 16)
                        for c in range(4):
                            for k in range(KT):
                                last = pe.matmul(PS[:, MODB, ds(8 * i + 4 * b + c, 1)],
                                                 AW[:, b, k, c * P:(c + 1) * P], cond[:, k:k + 1],
                                                 start=(k == 0), stop=(k == KT - 1))
                        last.then_inc(s_mod, 1)

            for t in range(TT):
                pe.wait_ge(s_xn, t + 1)
                pe.wait_ge(s_xe, t + 1)
                for k in range(KT):
                    last = pe.transpose(pair(t % 2)[:, k * P:(k + 1) * P], XS[:, t, k * P:(k + 1) * P], ident[:, :])
                last.then_inc(s_xt, 1)
            pe.wait_ge(s_cond, 1)
            ada(0, 2)
            pe.wait_ge(s_lam, 1)
            pe.matmul(PS[:, 6, 0:1], ones[0:1, :], ls[:, 4:5], start=True, stop=True).then_inc(s_lamp, 1)

            pe.wait_ge(s_h, KT)
            with pe.Fori(0, 2) as i:
                for j in range(4):
                    unit(pe, j, i + 1 + U_XR // 4, U_XR // 2 + 2 * i + j // 2 + 1, j % 2, hT)
            pe.wait_ge(s_lamb, 1)
            pe.wait_ge(s_modu, 1)
            with pe.Fori(0, 2) as i:
                for j in range(4):
                    n = 4 * i + j
                    unit(pe, j, i + 1 + U_GR // 4, U_GR // 2 + 2 * i + j // 2 + 1, j % 2, hT)
                    pe.wait_ge(s_gw[j], 32 * i + 32)
                    pe.wait_ge(s_xc, n + 3)
                    pe.wait_ge(s_ig, n + 1)
                    for g in range(2):
                        for half in range(2):
                            last = pe.matmul(PS[:, 4 + 2 * g + half, :], GW[:, j, g, :],
                                             xcT[:, ds(n, 1), half * HALF:(half + 1) * HALF]
                                             .rearrange("p o n -> p (o n)"), start=True, stop=True)
                    last.then_inc(s_gate, 1)
            pe.wait_ge(s_ig, KT + 1)
            ada(2, 3)
            with pe.Fori(0, 2) as i:
                for j in range(4):
                    unit(pe, j, i + 1 + U_GA // 4, U_GA // 2 + 2 * i + j // 2 + 1, j % 2, hT)
            ada(3, 4)
            pe.wait_ge(s_yr, KT + 1)
            with pe.Fori(0, 2) as i:
                for j in range(4):
                    unit(pe, j, i + 1 + U_YA // 4, U_YA // 2 + 2 * i + j // 2 + 1, j % 2, xcT)
            ada(4, 5)
            with pe.Fori(0, 2) as i:
                for q in range(4):
                    rows_unit(pe, q, i + 1 + U_V // 4, U_V // 2 + 2 * i + q // 2 + 1, q % 2, hT)
            ada(5, 6)
            pe.wait_ge(s_mod2, 1)

            with pe.Fori(0, NH // 2) as i:
                for b in range(2):
                    h = 2 * i + b
                    for c in range(2):
                        unit(pe, 2 * b + c, i + 1 + U_QK // 4, EV_ATT + EV_PER_HEAD * h, c, hT)

                    def scores(qt):
                        L = (qt + 1) * P
                        for c in range(2):
                            if qt == 0:
                                pe.wait_ge(s_ev[0], EV_ATT + EV_PER_HEAD * h + 1)
                                pe.wait_ge(s_ev[1], EV_ATT + EV_PER_HEAD * h + 1)
                            else:
                                pe.wait_ge(s_ev[c], EV_ATT + EV_PER_HEAD * h + 1 + qt)
                            for n0 in range(0, L, HALF):
                                n1 = min(L, n0 + HALF)
                                last = pe.matmul(pair(c)[:, n0:n1], qT[c * HD:(c + 1) * HD, b, qt * P:(qt + 1) * P],
                                                 kT[c * HD:(c + 1) * HD, b, n0:n1], start=True, stop=True)
                            last.then_inc(s_S, 1)

                    def turn(qt):
                        pe.wait_ge(s_A, 8 * h + qt + 1)
                        for g in range(qt // 4 + 1):
                            G = group(qt) + g
                            pe.wait_ge(s_pte, 12 * h + G + 1)
                            for kb in range(4 * g, min(4 * g + 4, qt + 1)):
                                last = pe.transpose(PS[:, 6 + G % 2, (kb % 4) * P:(kb % 4 + 1) * P],
                                                    SM[:, qt % 2, 0, kb * P:(kb + 1) * P], ident[:, :])
                            last.then_inc(s_T, 1)

                    def values(qt):
                        pe.wait_ge(s_pte, 12 * h + group(qt) + qt // 4 + 1 + 2)
                        pe.wait_ge(s_oe, 8 * h + qt + 1)
                        for kb in range(qt + 1):
                            last = pe.matmul(PS[:, 4 + qt % 2, 0:P], PT[:, qt % 2, kb, :],
                                             V[:, kb, ds(h * P, P)], start=(kb == 0), stop=(kb == qt))
                        last.then_inc(s_pv, 1)

                    scores(0)
                    for qt in range(TT):
                        if qt + 1 < TT:
                            scores(qt + 1)
                        turn(qt)
                        if qt >= 1:
                            values(qt - 1)
                    values(TT - 1)

            E0 = EV_ATT + NH * EV_PER_HEAD

            def gate_unit(i, j):
                unit(pe, j, i + 1 + U_GB // 4, E0 + 2 * i + j // 2, j % 2, hT if j % 2 == 0 else oT)

            gate_unit(0, 0)
            pe.wait_ge(s_pte, 12 * NH + 2)
            pe.wait_ge(s_oe, 8 * NH + 2)
            with pe.Fori(0, TT // 2) as i:
                for b in range(2):
                    pe.wait_ge(s_on, 2 * i + b + 1)
                    pe.wait_ge(s_oTe, 2 * i + b + 1)
                    for k in range(KT):
                        last = pe.transpose(pair(2 + b)[:, k * P:(k + 1) * P], on2[:, b, k * P:(k + 1) * P],
                                            ident[:, :])
                    last.then_inc(s_oT, 1)
            pe.wait_ge(s_oTe, TT + 2)
            for j in range(1, 4):
                gate_unit(0, j)
            with pe.Fori(1, 4) as i:
                for j in range(4):
                    gate_unit(i, j)
            for r in range(4):
                pe.wait_ge(s_dg, KT * (r + 1))
                if r >= 2:
                    pe.wait_ge(s_rows, r - 1)
                for half in range(2):
                    last = pe.matmul(PS[:, 4 + 2 * (r % 2) + half, :], ones[:, :],
                                     dg[:, r % 2, 4 * half:4 * half + 4, :].rearrange("p k n -> p (k n)"),
                                     start=True, stop=True)
                last.then_inc(s_bc, 1)
            pe.wait_ge(s_mg, KT + 2)
            def turn_h2(t):
                pe.wait_ge(s_h2, t + 1)
                pe.wait_ge(s_h2e, t + 1)
                for k in range(KT):
                    last = pe.transpose(pair(2 + t % 2)[:, k * P:(k + 1) * P], h2t[:, t, k * P:(k + 1) * P],
                                        ident[:, :])
                last.then_inc(s_h2T, 1)

            def out_unit(i, q):
                rows_unit(pe, q, i + 1 + U_O // 4, E0 + (U_O - U_GB) // 2 + 2 * i + q // 2, q % 2, gT)

            for q in range(4):
                out_unit(0, q)
            pe.wait_ge(s_rows, 4)
            for q in range(4):
                out_unit(1, q)
                if q >= 2:
                    turn_h2(2 * q - 4)
                    turn_h2(2 * q - 3)
            for t in range(4, TT):
                turn_h2(t)
            pe.wait_ge(s_h2e, TT + 2)
            pe.wait_ge(s_ld, 48)
            for t in range(TT):
                for k in range(KT):
                    last = pe.matmul(PS[:, 7, t * NE:(t + 1) * NE], hT[:, k, t * P:(t + 1) * P], wr[:, k, :],
                                     start=(k == 0), stop=(k == KT - 1))
                last.then_inc(s_lg, 1)

            def turn_hidden(S, g, b):
                hold(pe, S["hb"], g + 1)
                for f in range(FT):
                    last = pe.transpose(PS[:, 6, f * P:(f + 1) * P], hb[:, b, f * P:(f + 1) * P], ident[:, :])
                last.then_inc(S["hT"], 1)

            def up(S, g, b, lhs, w):
                for k in range(KT):
                    last = pe.matmul(PS[:, 2 + b, :], lhs(k), w(k), start=(k == 0), stop=(k == KT - 1))
                last.then_inc(S["up"], 1)

            def down(S, g, b, w):
                hold(pe, S["he"], g + 1)
                for half in range(2):
                    for f in range(FT):
                        last = pe.matmul(PS[:, 4 + half, :], hbT[:, b, f, :], w(f, half),
                                         start=(f == 0), stop=(f == FT - 1))
                last.then_inc(S["dn"], 1)

            for j in range(4):
                pe.wait_ge(s_w[j], 16 * (U_SH // 4 + 1))
            def shared_up(t):
                if t >= 2:
                    pe.wait_ge(sh["hb"], t - 1)
                up(sh, t, t % 2, lambda k: hT[:, k, t * P:(t + 1) * P], lambda k: WT[:, :, k, :])

            for t in range(2):
                shared_up(t)
            pe.wait_ge(s_M, TT)
            for t in range(TT):
                for j in range(t + 1):
                    pe.matmul(PS[:, 0, t * NE:(t + 1) * NE], (tri if j == t else ones)[:, :], M[:, j, :],
                              start=(j == 0), stop=(j == t))
            for j in range(TT):
                last = pe.matmul(PS[:, 1, 0:NE], ones[:, :], M[:, j, :], start=(j == 0), stop=(j == TT - 1))
            last.then_inc(s_rk, 1)
            for t in range(TT):
                turn_hidden(sh, t, t % 2)
                if 1 <= t < TT - 1:
                    shared_up(t + 1)
                if t >= 1:
                    pe.wait_ge(sh["ya"], t)
                    pe.wait_ge(sh["yd"], t)
                down(sh, t, t % 2, lambda f, half: W2s[:, f, half * HALF:(half + 1) * HALF])
            pe.wait_ge(s_tab, 16)
            pe.wait_ge(s_eid, 1)
            for c in range(2):
                pe.transpose(PS[:, c, 0:P], tab[:, :, c], ident[:, :]).then_inc(s_tabT, 1)
            pe.wait_ge(s_tabc, 2)
            pe.wait_ge(s_tbr, 16)
            np_ = pe.value_load(pendi[0:1, NE:NE + 1], min_val=1, max_val=NBLK // 2 - 1)

            def turn_rows(g, b, xg_round):
                hold(pe, s_xg[b], xg_round)
                hold(pe, s_xea, g + 1)
                hold(pe, s_xed, g + 1)
                for k in range(KT):
                    last = pe.transpose(PS[:, k // 4, (k % 4) * P:(k % 4 + 1) * P], xg[:, b, k * P:(k + 1) * P],
                                        ident[:, :])
                last.then_inc(s_xgT, 1)

            def expert_regs(g):
                par = pe.value_load(tbrow[0:1, ds(4 * g, 1)], min_val=0, max_val=1)
                even = pe.value_load(tbrow[0:1, ds(4 * g + 1, 1)], min_val=1, max_val=NE)
                odd = pe.value_load(tbrow[0:1, ds(4 * g + 2, 1)], min_val=1, max_val=NE)
                return par, even, odd

            def block_up(g, b):
                par, even, odd = expert_regs(g)
                hold(pe, s_xea, g + 2)
                hold(pe, s_xed, g + 2)
                hold(pe, s_w13[0], 32 * even)
                hold(pe, s_w13[1], 32 * odd)
                up(ro, g, b, lambda k: xT[:, b, k, :], lambda k: W13[:, ds(par, 1), k, :].rearrange("p o n -> p (o n)"))

            def block_down(g, b):
                par, even, odd = expert_regs(g)
                hold(pe, s_w2[0], 16 * even)
                hold(pe, s_w2[1], 16 * odd)
                down(ro, g, b, lambda f, half: W2[:, ds(par, 1), f, half * HALF:(half + 1) * HALF]
                     .rearrange("p o n -> p (o n)"))

            turn_rows(0, 0, 16)
            block_up(0, 0)
            turn_rows(1, 1, 16)
            with pe.Fori(0, np_) as i:
                for j in range(2):
                    g = 2 * i + j + 1
                    turn_hidden(ro, g - 1, j)
                    block_up(g, 1 - j)
                    turn_rows(g + 1, j, 16 * i + 32)
                    hold(pe, ro["ya"], g)
                    hold(pe, ro["yd"], g)
                    block_down(g - 1, j)
            turn_hidden(ro, 2 * np_, 0)
            hold(pe, ro["ya"], 2 * np_ + 1)
            hold(pe, ro["yd"], 2 * np_ + 1)
            block_down(2 * np_, 0)

        @block.scalar
        def _(act):
            for p in range(2):
                act.sem_inc(s_ev[p], 1)
            act.sem_inc(s_xe, 2)
            act.sem_inc(s_ig, 1)
            act.sem_inc(s_pte, 2)
            act.sem_inc(s_oe, 2)
            act.sem_inc(s_oTe, 2)
            act.sem_inc(s_h2e, 2)
            for dst, r0, src in vector_rows():
                act.dma_start(dst[r0:r0 + src.shape[0], :], src).then_inc(s_small, 16)
            for j, n in enumerate(("lam_q1", "lam_k1", "lam_q2", "lam_k2")):
                act.dma_start(lqk[:, j * HD:(j + 1) * HD], a[n]).then_inc(s_small, 16)
            act.wait_ge(s_vt, 1)
            act.activation(vc0[:, :], PS[:, 4, 0:P], ACT.Copy).then_inc(s_vc, 1)
            act.activation(vc1[:, :], PS[:, 5, 0:3 * KT + 1], ACT.Copy).then_inc(s_vc, 1)
            act.wait_ge(s_vc, 1)
            act.activation(cond[:, :], ccol[:, :], ACT.Silu).then_inc(s_cond, 1)
            act.wait_ge(s_lnp, 2)
            act.activation(spt[:, 0:KT], spt[:, KT:2 * KT], ACT.Exp).then_inc(s_act, 1)
            act.wait_ge(s_lnp, 4)
            act.activation(ls[:, 2:4], ls[:, 0:2], ACT.Exp).then_inc(s_act, 1)

            def rms_of(src, q, s_in, s_sq, s_rt, n):
                for t in (2 * q, 2 * q + 1):
                    if s_in is not None:
                        act.wait_ge(s_in, t + 1)
                    act.activation(junk[:, :], src[:, t, :], ACT.Square, accum_out=ss[:, t:t + 1]).then_inc(s_sq, 1)
                    act.wait_ge(s_sq, n + t % 2 + 1)
                act.activation(rms[:, 2 * q:2 * q + 2], ss[:, 2 * q:2 * q + 2], ACT.Sqrt, scale=1.0 / D,
                               bias=eps[:, 0:1]).then_inc(s_rt, 1)

            act.wait_ge(s_const, 1)
            for q in range(TT // 2 + 1):
                if q < TT // 2:
                    act.wait_ge(s_x[q], 16)
                    rms_of(XS, q, None, s_ss, s_rms, 2 * q)
                if q >= 1:
                    for t in (2 * q - 2, 2 * q - 1):
                        act.wait_ge(s_xt, t + 1)
                        act.activation(hT[:, :, t * P:(t + 1) * P], pair3(t % 2), ACT.Copy).then_inc(s_xe, 1)
            act.wait_ge(s_lamp, 1)
            act.activation(nlam[:, :], PS[:, 6, 0:1], ACT.Copy, scale=-1.0).then_inc(s_lamb, 1)
            with act.Fori(0, 2) as i:
                for j in range(4):
                    n = 4 * i + j
                    act.wait_ge(s_mm, U_XR + n + 1)
                    hold(act, s_xc, n + 1)
                    act.activation(xpad[:, j % 2, 4:4 + T], pair(j % 2), ACT.Copy).then_inc(s_ev[j % 2], 1)
            with act.Fori(0, 2) as i:
                for j in range(4):
                    n = 4 * i + j
                    act.wait_ge(s_gate, n + 5)
                    hold(act, s_yr, n + 1)
                    act.activation(rT[:, :], pair(2), ACT.Sigmoid, bias=ba[:, ds(n, 1)]).then_inc(s_act2, 1)
                    act.activation(iT[:, :], pair(3), ACT.Sigmoid, bias=bx[:, ds(n, 1)]).then_inc(s_ig, 1)
                    hold(act, s_act2, n + 1)
                    act.activation(tT[:, :], rT[:, :], ACT.Tanh, scale=sp8[:, ds(n, 1)]).then_inc(s_t, 1)
                    act.activation(aT[:, :], rT[:, :], ACT.Exp, scale=nsp8[:, ds(n, 1)]).then_inc(s_a, 1)
                    hold(act, s_m2, n + 1)
                    act.activation(mT[:, :], mT[:, :], ACT.Sqrt).then_inc(s_m, 1)
                    hold(act, s_mm, U_GR + n + 1)
                    act.activation(geT[:, :], pair(j % 2), ACT.Gelu_apprx_tanh).then_inc(s_ev[j % 2], 1)
            with act.Fori(0, 2) as i:
                for j in range(4):
                    n = 4 * i + j
                    hold(act, s_mm, U_GA + n + 1)
                    act.activation(gT[:, ds(n, 1), :].rearrange("p o n -> p (o n)"), pair(j % 2), ACT.Sigmoid)\
                        .then_inc(s_ev[j % 2], 1)
            with act.Fori(0, 2) as i:
                for q in range(4):
                    hold(act, s_mm, U_V + 4 * i + q + 1)
                    act.activation(V[:, 2 * q:2 * q + 2, ds(i * HALF, HALF)], PS[:, 2 * (q % 2):2 * (q % 2) + 2, :],
                                   ACT.Copy).then_inc(s_ev[q % 2], 1)
            with act.Fori(0, NH // 2) as i:
                for b in range(2):
                    h = 2 * i + b
                    for c, dst in enumerate((qT, kT)):
                        hold(act, s_mm, U_QK + 2 * h + c + 1)
                        act.activation(dst[:, b, :], pair(c), ACT.Copy).then_inc(s_ev[c], 1)

                    def exps(qt):
                        L = (qt + 1) * P
                        for c in range(2):
                            hold(act, s_ev[c], EV_ATT + EV_PER_HEAD * h + 1 + qt + 1)
                            s = SM[:, qt % 2, c, 0:L]
                            m = 2 * (qt % 2) + c
                            act.activation(s, s, ACT.Exp, scale=-1.0, bias=mn[:, m:m + 1],
                                           accum_out=lsum[:, m:m + 1]).then_inc(s_e, 1)

                    def turned(qt):
                        hold(act, s_pv, 8 * h + qt + 1)
                        for g in range(qt // 4 + 1):
                            G = group(qt) + g
                            nb = min(4, qt + 1 - 4 * g)
                            hold(act, s_T, 12 * h + G + 1)
                            act.activation(PT[:, qt % 2, 4 * g:4 * g + nb, :].rearrange("p k n -> p (k n)"),
                                           PS[:, 6 + G % 2, 0:nb * P], ACT.Copy).then_inc(s_pte, 1)

                    def outs(qt):
                        hold(act, s_pv, 8 * h + qt + 3)
                        act.activation(ON[:, qt, ds(h * P, P)], PS[:, 4 + qt % 2, 0:P], ACT.Copy,
                                       scale=rl[:, 2 * (qt % 2):2 * (qt % 2) + 1]).then_inc(s_oe, 1)

                    exps(0)
                    for qt in range(TT):
                        if qt + 1 < TT:
                            exps(qt + 1)
                        turned(qt)
                        if qt >= 1:
                            outs(qt - 1)
                    outs(TT - 1)
            act.wait_ge(s_oe, 8 * NH + 2)
            for t in range(TT):
                act.wait_ge(s_nss, t + 1)
                act.activation(sq[:, t % 2, :], ON[:, t, :], ACT.Square).then_inc(s_sq, 1)
            act.wait_ge(s_nss, TT + 2)
            act.activation(ssn[:, :], ssn[:, :], ACT.Sqrt, scale=1.0 / P, bias=eps[:, 0:1]).then_inc(s_nrm, 1)

            def gate_b(i, j):
                n = 2 * i + j
                act.wait_ge(s_mm, U_GB + 2 * n + 1)
                hold(act, s_mg, n + 1)
                act.activation(sg[:, j, :], pair(0), ACT.Sigmoid).then_inc(s_ev[0], 1)

            with act.Fori(0, TT // 2) as i:
                for b in range(2):
                    t = 2 * i + b
                    hold(act, s_oT, t + 1)
                    act.activation(tcols(oT, t), pair3(2 + b), ACT.Copy, scale=gsub8[:, 0:1]).then_inc(s_oTe, 1)
            with act.Fori(0, 4) as i:
                for j in range(2):
                    gate_b(i, j)
            for r in range(4):
                act.wait_ge(s_bc, r + 1)
                act.activation(ROWS[:, r, :], pair(2 + r % 2), ACT.Copy).then_inc(s_rows, 1)

            def out_rows(i, q):
                act.wait_ge(s_mm, U_O + 4 * i + q + 1)
                act.activation(Y[:, 2 * q:2 * q + 2, i * HALF:(i + 1) * HALF],
                               PS[:, 2 * (q % 2):2 * (q % 2) + 2, :], ACT.Copy).then_inc(s_ev[q % 2], 1)

            def h2_turned(q):
                for t in (2 * q, 2 * q + 1):
                    act.wait_ge(s_h2T, t + 1)
                    act.activation(hT[:, :, t * P:(t + 1) * P], pair3(2 + t % 2), ACT.Copy).then_inc(s_h2e, 1)

            for q in range(4):
                out_rows(0, q)
            E1 = EV_ATT + NH * EV_PER_HEAD + (U_O - U_GB) // 2
            for q in range(4):
                out_rows(1, q)
                act.wait_ge(s_ev[q % 2], E1 + 2 + q // 2 + 1)
                rms_of(Y, q, None, s_yss, s_yrm, 4 * q - 2 * min(q, 1))
                if q >= 1:
                    rms_of(Y, q - 1, s_x1, s_yss, s_yrm, 4 * q)
                if q >= 2:
                    h2_turned(q - 2)
            rms_of(Y, 3, s_x1, s_yss, s_yrm, 14)
            h2_turned(2)
            h2_turned(3)
            act.sem_inc(s_xea, 1)
            act.sem_inc(ro["ya"], 1)

            def hidden_act(S, g, b):
                hold(act, S["up"], g + 1)
                act.activation(sgm[:, b, :], PS[:, 2 + b, 0:FE], ACT.Sigmoid).then_inc(S["sg"], 1)

            def hidden_turned(S, g, b):
                hold(act, S["hT"], g + 1)
                act.activation(hbT[:, b, :, :].rearrange("p f n -> p (f n)"), PS[:, 6, 0:FE], ACT.Copy)\
                    .then_inc(S["he"], 1)

            act.wait_ge(s_lg, TT)
            act.activation(sco[:, :, :].rearrange("p t e -> p (t e)"), PS[:, 7, :], ACT.Sigmoid).then_inc(s_sco, 1)
            for t in range(2):
                hidden_act(sh, t, t)
            for t in range(TT):
                hidden_turned(sh, t, t % 2)
                if 1 <= t < TT - 1:
                    hidden_act(sh, t + 1, (t + 1) % 2)
                act.wait_ge(sh["dn"], t + 1)
                if t >= 2:
                    act.wait_ge(s_shst[t % 2], 16 * (t // 2))
                act.activation(yo[:, t % 2, 0:HALF], PS[:, 4, :], ACT.Copy).then_inc(sh["ya"], 1)
            act.wait_ge(s_tabT, 2)
            act.activation(tokT[:, 0:P], PS[:, 0, 0:P], ACT.Copy).then_inc(s_tabc, 1)
            act.activation(wtT[:, :], PS[:, 1, 0:P], ACT.Copy).then_inc(s_tabc, 1)
            act.wait_ge(s_tabc, 2)
            act.wait_ge(s_eid, 2)
            for b in range(2):
                act.wait_ge(s_shst[b], 16 * TT // 2)
            np_ = act.value_load(pendi[0:1, NE:NE + 1], min_val=1, max_val=NBLK // 2 - 1)

            def rows_turned(g, b):
                hold(act, s_xgT, g + 1)
                act.activation(xT[:, b, 0:4, :].rearrange("p k n -> p (k n)"), PS[:, 0, :], ACT.Copy)\
                    .then_inc(s_xea, 1)

            def out_half(g, b, done):
                hold(act, ro["dn"], g + 1)
                if done is not None:
                    hold(act, ro["st"], done)
                act.activation(yo[:, b, 0:HALF], PS[:, 4, :], ACT.Copy, scale=wtT[:, ds(g, 1)]).then_inc(ro["ya"], 1)

            rows_turned(0, 0)
            hidden_act(ro, 0, 0)
            rows_turned(1, 1)
            with act.Fori(0, np_) as i:
                for j in range(2):
                    g = 2 * i + j + 1
                    hidden_turned(ro, g - 1, j)
                    hidden_act(ro, g, 1 - j)
                    rows_turned(g + 1, j)
                    out_half(g - 1, j, 16 * g)
            hidden_turned(ro, 2 * np_, 0)
            out_half(2 * np_, 0, 32 * np_ + 16)
            for t in range(TT):
                act.wait_ge(s_fl[t], 16)
                act.activation(junk[:, :], FS[:, t, :], ACT.Square, accum_out=ss[:, t:t + 1]).then_inc(s_fss, 1)
                act.wait_ge(s_fss, t + 1)
                if t % 2:
                    act.activation(rms[:, t - 1:t + 1], ss[:, t - 1:t + 1], ACT.Sqrt, scale=1.0 / D,
                                   bias=eps[:, 0:1]).then_inc(s_frm, 1)

        @block.vector
        def _(dve):
            stt = dve.scalar_tensor_tensor
            dve.sem_inc(s_xc, 2)
            dve.sem_inc(s_yr, 1)
            dve.sem_inc(s_mg, 2)
            dve.sem_inc(s_nss, 2)
            link = Link(dve, s_dve)
            dve.memset(eps[:, :], EPS).then_inc(s_lnp, 1)
            dve.wait_ge(s_small, 16 * N_SMALL)
            dve.wait_ge(s_vc, 2)
            link(dve.tensor_scalar(spt[:, KT:2 * KT], lamc[:, :], -1.0, None, ALU.mult), wait=True)
            dve.tensor_tensor(spt[:, KT:2 * KT], spt[:, KT:2 * KT], lamc[:, :], ALU.min).then_inc(s_lnp, 1)
            for j in range(2):
                dve.tensor_tensor_reduce(out=lpr[:, :], in0=lqk[:, 2 * j * HD:(2 * j + 1) * HD],
                                         in1=lqk[:, (2 * j + 1) * HD:(2 * j + 2) * HD], scale=1.0, scalar=0.0,
                                         op0=ALU.mult, op1=ALU.add, accum_out=ls[:, j:j + 1]).then_inc(s_lnp, 1)
                dve.wait_ge(s_lnp, 3 + j)
            dve.wait_ge(s_act, 1)
            e, w, w2, poly = (spt[:, j * KT:(j + 1) * KT] for j in range(4))
            link(dve.tensor_scalar(w, e, 2.0, None, ALU.add))
            link(dve.reciprocal(w, w))
            link(dve.tensor_tensor(w, w, e, ALU.mult))
            link(dve.tensor_tensor(w2, w, w, ALU.mult))
            link(dve.memset(poly, 1.0 / 19))
            for m in range(8, -1, -1):
                link(dve.tensor_tensor(poly, poly, w2, ALU.mult))
                link(dve.tensor_scalar(poly, poly, 1.0 / (2 * m + 1), None, ALU.add))
            link(stt(out=poly, in0=poly, scalar=2.0, in1=w, op0=ALU.mult, op1=ALU.mult))
            link(dve.tensor_scalar(w2, lamc[:, :], -1.0, 0.0, ALU.mult, ALU.max))
            link(dve.tensor_tensor(w2, w2, poly, ALU.add))
            link(dve.tensor_scalar(sp8[:, :], w2, LRU_C, None, ALU.mult), wait=False)
            link(dve.tensor_scalar(nsp8[:, :], w2, -LRU_C, None, ALU.mult), wait=False)
            link(dve.tensor_scalar(gsub8[:, :], gsub[:, :], 1.0 - LAM_INIT, None, ALU.mult), wait=False)
            dve.wait_ge(s_act, 2)
            link(dve.tensor_tensor(ls[:, 5:6], ls[:, 2:3], ls[:, 3:4], ALU.subtract))
            dve.tensor_scalar(ls[:, 4:5], ls[:, 5:6], LAM_INIT, None, ALU.add).then_inc(s_lam, 1)

            l1 = Link(dve, s_dve2)
            for q in range(TT // 2):
                dve.wait_ge(s_rms, q + 1)
                l1(dve.reciprocal(rstd[:, 2 * q:2 * q + 2], rms[:, 2 * q:2 * q + 2]))
                for t in (2 * q, 2 * q + 1):
                    dve.tensor_scalar(XS[:, t, :], XS[:, t, :], rstd[:, t:t + 1], None, ALU.mult).then_inc(s_xn, 1)
            dve.wait_ge(s_mod, 4 + 2)
            dve.tensor_tensor(mod[:, 0:16], PS[:, MODB, 0:16], bada[:, 0:16], ALU.add).then_inc(s_modu, 1)
            dve.wait_ge(s_modu, 1)
            link(stt(out=a1[:, :], in0=mod[:, KT:2 * KT], scalar=1.0, in1=gpm[:, :], op0=ALU.add, op1=ALU.mult))
            dve.wait_ge(s_xe, TT + 2)
            for k in range(KT):
                dve.tensor_scalar(hT[:, k, :], hT[:, k, :], a1[:, k:k + 1], mod[:, k:k + 1], ALU.mult, ALU.add)\
                    .then_inc(s_h, 1)
            for b in range(2):
                link(dve.memset(xpad[:, b, 0:4], 0.0), wait=(b == 1))
            lc = Link(dve, s_dve3, 0, 4 * 3)
            with dve.Fori(0, 2) as i:
                lc.at(i)
                for j in range(4):
                    n = 4 * i + j
                    hold(dve, s_ev[j % 2], U_XR // 2 + 2 * i + j // 2 + 2)
                    y = xcT[:, ds(n, 1), :].rearrange("p o n -> p (o n)")
                    lc(dve.tensor_scalar(y, xpad[:, j % 2, 4:4 + T], cw[:, ds(3 * KT + n, 1)], cb[:, ds(n, 1)],
                                         ALU.mult, ALU.add))
                    for tap in (2, 1, 0):
                        ins = stt(out=y, in0=xpad[:, j % 2, 1 + tap:1 + tap + T], scalar=cw[:, ds(tap * KT + n, 1)],
                                  in1=y, op0=ALU.mult, op1=ALU.add)
                        if tap:
                            lc(ins)
                        else:
                            ins.then_inc(s_xc, 1)
            lg = Link(dve, s_dve4, 0, 4 * 6)
            with dve.Fori(0, 2) as i:
                lg.at(i)
                for j in range(4):
                    n = 4 * i + j
                    y = xcT[:, ds(n, 1), :].rearrange("p o n -> p (o n)")
                    hold(dve, s_t, n + 1)
                    lg(dve.tensor_scalar(hsT[:, :], tT[:, :], 1.0, None, ALU.add))
                    lg(dve.reciprocal(hsT[:, :], hsT[:, :]))
                    stt(out=mT[:, :], in0=tT[:, :], scalar=2.0, in1=hsT[:, :], op0=ALU.mult, op1=ALU.mult)\
                        .then_inc(s_m2, 1)
                    hold(dve, s_ig, n + 2)
                    lg(dve.tensor_tensor(ixT[:, :], iT[:, :], y, ALU.mult), wait=False)
                    hold(dve, s_m, n + 1)
                    lg(dve.memset(mT[:, 0:1], 1.0))
                    lg(dve.tensor_tensor(ixT[:, :], ixT[:, :], mT[:, :], ALU.mult))
                    hold(dve, s_a, n + 1)
                    lg(dve.tensor_tensor_scan(out=hsT[:, :], data0=aT[:, :], data1=ixT[:, :], initial=0.0,
                                              op0=ALU.mult, op1=ALU.add))
                    hold(dve, s_ev[j % 2], U_GR // 2 + 2 * i + j // 2 + 2)
                    dve.tensor_tensor(y, hsT[:, :], geT[:, :], ALU.mult).then_inc(s_yr, 1)
            with dve.Fori(0, 2) as i:
                for j in range(4):
                    n = 4 * i + j
                    g = gT[:, ds(n, 1), :].rearrange("p o n -> p (o n)")
                    hold(dve, s_mm, U_YA + n + 1)
                    dve.tensor_tensor(g, g, pair(j % 2), ALU.mult).then_inc(s_ev[j % 2], 1)

            dve.wait_ge(s_mod, 12 + 2)
            dve.tensor_tensor(mod[:, 16:48], PS[:, MODB, 16:48], bada[:, 16:48], ALU.add).then_inc(s_mod2, 1)
            dve.wait_ge(s_mod2, 1)
            link(dve.tensor_tensor(rows_c[:, 0:8], mod[:, 16:24], gpo[:, :], ALU.mult), wait=False)
            link(stt(out=rows_c[:, 8:16], in0=mod[:, 32:40], scalar=1.0, in1=gpf[:, :], op0=ALU.add, op1=ALU.mult),
                 wait=False)
            link(dve.tensor_copy(rows_c[:, 16:24], mod[:, 24:32]), wait=False)
            link(dve.tensor_tensor(rows_c[:, 24:32], mod[:, 40:48], gpo2[:, :], ALU.mult))

            la = Link(dve, s_dve5, 0, 2 * (2 + 16))
            with dve.Fori(0, NH // 2) as i:
                la.at(i)
                for b in range(2):
                    h = 2 * i + b
                    la(dve.tensor_scalar(B8[:, :], R[:, :], SL[:, ds(h, 1)], None, ALU.mult))
                    la(dve.tensor_tensor(B8[:, T - P:T], B8[:, T - P:T], MASK[:, :], ALU.add))

                    def soft(qt):
                        L = (qt + 1) * P
                        for c in range(2):
                            m = 2 * (qt % 2) + c
                            hold(dve, s_S, 16 * h + 2 * qt + c + 1)
                            if qt >= 2:
                                hold(dve, s_T, 12 * h + group(qt - 1))
                            dve.tensor_tensor_reduce(out=SM[:, qt % 2, c, 0:L], in0=pair(c)[:, 0:L],
                                                     in1=B8[:, T - L:T], scale=-HD ** -0.5, scalar=3e38,
                                                     op0=ALU.add, op1=ALU.min,
                                                     accum_out=mn[:, m:m + 1]).then_inc(s_ev[c], 1)

                    def merge(qt):
                        L = (qt + 1) * P
                        q = 2 * (qt % 2)
                        dve.wait_ge(s_e, 16 * h + 2 * qt + 2)
                        hold(dve, s_oe, 8 * h + qt + 1)
                        la(dve.reciprocal(rl[:, q:q + 2], lsum[:, q:q + 2]))
                        la(dve.tensor_scalar(c1[:, qt % 2:qt % 2 + 1], rl[:, q + 1:q + 2], nlam[:, 0:1],
                                             lsum[:, q:q + 1], ALU.mult, ALU.mult))
                        stt(out=SM[:, qt % 2, 0, 0:L], in0=SM[:, qt % 2, 1, 0:L], scalar=c1[:, qt % 2:qt % 2 + 1],
                            in1=SM[:, qt % 2, 0, 0:L], op0=ALU.mult, op1=ALU.add).then_inc(s_A, 1)

                    soft(0)
                    for qt in range(TT):
                        merge(qt)
                        if qt + 1 < TT:
                            soft(qt + 1)

            ln = Link(dve, s_dve6)
            for t in range(TT):
                dve.wait_ge(s_sq, t + 1)
                dve.tensor_reduce(ssn[:, t * NH:(t + 1) * NH], sq[:, t % 2, :].rearrange("p (h n) -> p h n", h=NH),
                                  AX.X, ALU.add).then_inc(s_nss, 1)
            dve.wait_ge(s_nrm, 1)
            ln(dve.reciprocal(ssn[:, :], ssn[:, :]))
            with dve.Fori(0, TT // 2) as i:
                for b in range(2):
                    t = 2 * i + b
                    hold(dve, s_oTe, t + 1)
                    dve.tensor_tensor(on2[:, b, :].rearrange("p (h n) -> p h n", h=NH),
                                      ON[:, ds(t, 1), :].rearrange("p o (h n) -> p (o h) n", h=NH),
                                      ssn[:, ds(t * NH, NH)].rearrange("p (h o) -> p h o", o=1)
                                      .broadcast_to([P, NH, P]), ALU.mult).then_inc(s_on, 1)

            def diagonals(r):
                if r >= 2:
                    dve.wait_ge(s_bc, r - 1)
                for k in range(KT):
                    dve.tensor_scalar(dg[:, r % 2, k, :], ident[:, :], rows_c[:, r * KT + k:r * KT + k + 1], None,
                                      ALU.mult).then_inc(s_dg, 1)

            diagonals(0)
            diagonals(1)
            lm = Link(dve, s_dve7, 0, 2)
            with dve.Fori(0, 4) as i:
                lm.at(i)
                for j in range(2):
                    n = 2 * i + j
                    g = gT[:, ds(n, 1), :].rearrange("p o n -> p (o n)")
                    dve.wait_ge(s_mm, U_GB + 2 * n + 2)
                    dve.wait_ge(s_mg, n + 2)
                    hold(dve, s_ev[0], EV_ATT + NH * EV_PER_HEAD + n + 1)
                    dve.tensor_tensor(ty[:, :], sg[:, j, :], pair(1), ALU.mult).then_inc(s_ev[1], 1)
                    hold(dve, s_ev[1], EV_ATT + NH * EV_PER_HEAD + n + 1)
                    dve.tensor_tensor(g, g, ty[:, :], ALU.add).then_inc(s_mg, 1)
            diagonals(2)
            diagonals(3)
            dve.wait_ge(s_rows, 4)
            lx = Link(dve, s_dve8)
            for q in range(TT // 2):
                dve.wait_ge(s_x[q], 32)

            def residual(q, turn):
                dve.wait_ge(s_yrm, turn)
                lx(dve.reciprocal(rstd[:, 2 * q:2 * q + 2], rms[:, 2 * q:2 * q + 2]))
                for t in (2 * q, 2 * q + 1):
                    lx(stt(out=Y[:, t, :], in0=Y[:, t, :], scalar=rstd[:, t:t + 1], in1=ROWS[:, 0, :],
                           op0=ALU.mult, op1=ALU.mult))
                    dve.tensor_tensor(Y[:, t, :], Y[:, t, :], XS[:, t, :], ALU.add).then_inc(s_x1, 1)

            def modulated(q, turn):
                dve.wait_ge(s_yrm, turn)
                lx(dve.reciprocal(rstd[:, 2 * q:2 * q + 2], rms[:, 2 * q:2 * q + 2]))
                for t in (2 * q, 2 * q + 1):
                    lx(stt(out=h2t[:, t, :], in0=Y[:, t, :], scalar=rstd[:, t:t + 1], in1=ROWS[:, 1, :],
                           op0=ALU.mult, op1=ALU.mult))
                    dve.tensor_tensor(h2t[:, t, :], h2t[:, t, :], ROWS[:, 2, :], ALU.add).then_inc(s_h2, 1)

            residual(0, 1)
            for q in range(1, TT // 2):
                residual(q, 2 * q)
                modulated(q - 1, 2 * q + 1)
            modulated(TT // 2 - 1, 2 * (TT // 2))
            dve.sem_inc(s_xed, 1)
            dve.sem_inc(ro["yd"], 1)
            lr = Link(dve, s_dr)
            dve.wait_ge(s_ld, 48)
            dve.wait_ge(s_c2, 13)

            def over(ap, n, last):
                m = ap.shape[1]
                if last:
                    return ap.rearrange("p (o m) -> p o m", o=1).broadcast_to([P, n, m])
                return ap.rearrange("p (m o) -> p m o", o=1).broadcast_to([P, m, n])

            tiles = range(TT)

            def each(op, ns=tiles):
                for n in ns:
                    lr(op(n), wait=False)
                lr.wait()

            def eight(buf, t):
                return buf[:, 8 * t:8 * t + 8]

            dve.wait_ge(s_sco, 1)
            each(lambda t: dve.tensor_tensor(cho[:, t, :], sco[:, t, :], ebias[:, :], ALU.add))
            each(lambda n: dve.max(g8[:, n, :], cho[:, n // NG, n % NG * 8:n % NG * 8 + 8]), range(TT * NG))
            lr(dve.tensor_tensor(gs[:, :], g8[:, :, 0], g8[:, :, 1], ALU.add))
            each(lambda t: dve.max(eight(gv, t), eight(gs, t)))
            each(lambda t: dve.max_index(eight(gi, t), eight(gv, t), eight(gs, t)))
            lr(dve.tensor_copy(gif[:, :], gi[:, :]))
            each(lambda t: dve.tensor_tensor(gm4[:, t, :, :], over(io64[:, 0:NG], TOPG, True),
                                             over(gif[:, 8 * t:8 * t + TOPG], NG, False), ALU.is_equal))
            each(lambda t: dve.tensor_reduce(eight(gmk, t), gm4[:, t, :, :].rearrange("p k g -> p g k"), AX.X, ALU.add))
            lr(dve.tensor_scalar(gmk[:, :], gmk[:, :], -1.0, -MASKED, ALU.add, ALU.mult))
            c3 = cho[:, :, :].rearrange("p t (g n) -> p (t g) n", g=NG)
            lr(dve.tensor_tensor(c3, c3, over(gmk[:, :], NE // NG, False), ALU.add))
            each(lambda t: dve.max(eight(v8, t), cho[:, t, :]))
            each(lambda t: dve.max_index(eight(i8, t), eight(v8, t), cho[:, t, :]))
            lr(dve.tensor_copy(idxf[:, :], i8[:, :]))

            def hot(t):
                return oh[:, TOP * t:TOP * (t + 1), :]

            def hot2(t):
                return oh2[:, TOP * t:TOP * (t + 1), :]

            for b in range(2):
                dve.wait_ge(s_h2d[b], 16 * (TT // 2))
            each(lambda t: dve.tensor_tensor(hot(t), over(io64[:, :], TOP, True), over(eight(idxf, t), NE, False),
                                             ALU.is_equal))
            for t in tiles:
                dve.tensor_reduce(M[:, t, :], hot(t).rearrange("p k e -> p e k"), AX.X, ALU.add).then_inc(s_M, 1)
            def hidden(S, g, b):
                hold(dve, S["sg"], g + 1)
                dve.tensor_tensor(sgm[:, b, :], sgm[:, b, :], PS[:, 2 + b, 0:FE], ALU.mult).then_inc(S["t"], 1)
                hold(dve, S["t"], g + 1)
                dve.tensor_tensor(hb[:, b, :], sgm[:, b, :], PS[:, 2 + b, FE:2 * FE], ALU.mult).then_inc(S["hb"], 1)

            each(lambda t: dve.tensor_tensor(hot2(t), hot(t), over(sco[:, t, :], TOP, True), ALU.mult))
            each(lambda t: dve.tensor_reduce(eight(w8, t), hot2(t), AX.X, ALU.add))
            lr(dve.tensor_reduce(wsm[:, :], w8[:, :].rearrange("p (t k) -> p t k", k=TOP), AX.X, ALU.add))
            lr(dve.tensor_scalar(wsm[:, :], wsm[:, :], 1e-20, None, ALU.add))
            lr(dve.reciprocal(wsm[:, :], wsm[:, :]))
            pw = pairs[:, :].rearrange("p (t k c) -> p t k c", t=TT, k=TOP)
            each(lambda t: dve.tensor_scalar(pw[:, t, :, 1], eight(w8, t), wsm[:, t:t + 1], ROUTED_SCALE,
                                             ALU.mult, ALU.mult))
            for t in range(2):
                hidden(sh, t, t)
            dve.wait_ge(s_rk, 1)
            cmp = oh2[:, 0:8, :].rearrange("p k e -> p (k e)").rearrange("p (e k) -> p e k", k=8)
            lr(dve.tensor_copy(nbk[:, :], PS[:, 1, 0:NE]))
            lr(dve.tensor_tensor(cmp, over(nbk[:, :], 8, False), over(thr[:, :], NE, True), ALU.is_gt))
            lr(dve.tensor_reduce(nbk[:, :], cmp, AX.X, ALU.add))
            lr(dve.tensor_scalar(nbk[:, :], nbk[:, :], 1.0, None, ALU.add))
            lr(dve.tensor_tensor_scan(out=pend[:, :], data0=ones[:, 0:NE], data1=nbk[:, :], initial=0.0,
                                      op0=ALU.mult, op1=ALU.add))
            lr(dve.tensor_tensor(pst[:, :], pend[:, :], nbk[:, :], ALU.subtract))
            lr(dve.tensor_scalar(pst[:, :], pst[:, :], float(P), None, ALU.mult))
            each(lambda t: dve.tensor_tensor(pos[:, t, :], PS[:, 0, t * NE:(t + 1) * NE], pst[:, :], ALU.add))
            each(lambda t: dve.tensor_tensor(hot2(t), hot(t), over(pos[:, t, :], TOP, True), ALU.mult))
            each(lambda t: dve.tensor_reduce(eight(slotf, t), hot2(t), AX.X, ALU.add))
            dve.tensor_copy(slots[:, :], slotf[:, :]).then_inc(s_slot, 1)
            lr(dve.tensor_scalar(posab[:, :], pend[:, :], ioP[:, 0:1], None, ALU.is_le))
            lr(dve.tensor_reduce(eidf[:, :], posab[:, :], AX.X, ALU.add))
            lr(dve.tensor_scalar(eidf[:, :], eidf[:, :], float(NE - 1), None, ALU.min))
            lr(dve.tensor_scalar(ehi[:, :], eidf[:, :], 0.5, -0.25, ALU.mult, ALU.add))
            lr(dve.tensor_copy(ehf[:, :], ehi[:, :]))
            lr(stt(out=tbf[:, 0:1], in0=ehf[:, :], scalar=-2.0, in1=eidf[:, :], op0=ALU.mult, op1=ALU.add))
            lr(dve.tensor_scalar(tbf[:, 1:2], ehf[:, :], 1.0, None, ALU.add))
            lr(dve.tensor_tensor(tbf[:, 2:3], ehf[:, :], tbf[:, 0:1], ALU.add))
            lr(dve.tensor_scalar(tbf[:, 2:3], tbf[:, 2:3], 1.0, None, ALU.max))
            lr(dve.tensor_copy(tbf[:, 3:4], eidf[:, :]))
            lr(dve.tensor_scalar(npf[:, :], pend[:, NE - 1:NE], -0.5, 0.5, ALU.add, ALU.mult))
            lr(dve.tensor_copy(pendi[:, 0:NE], pend[:, :]))
            lr(dve.tensor_copy(pendi[:, NE:NE + 1], npf[:, :]))
            dve.tensor_copy(tbi[:, :], tbf[:, :]).then_inc(s_eid, 2)
            for t in range(TT):
                if 1 <= t < TT - 1:
                    hidden(sh, t + 1, (t + 1) % 2)
                dve.wait_ge(sh["dn"], t + 1)
                if t >= 2:
                    dve.wait_ge(s_shst[t % 2], 16 * (t // 2))
                dve.tensor_copy(yo[:, t % 2, HALF:D], PS[:, 5, :]).then_inc(sh["yd"], 1)

            for b in range(2):
                dve.wait_ge(s_shst[b], 16 * TT // 2)
            dve.wait_ge(s_eid, 2)
            np_ = dve.value_load(pendi[0:1, NE:NE + 1], min_val=1, max_val=NBLK // 2 - 1)

            dve.wait_ge(s_tabc, 2)

            def rows_turned(g, b):
                hold(dve, s_xgT, g + 1)
                dve.tensor_copy(xT[:, b, 4:8, :].rearrange("p k n -> p (k n)"), PS[:, 1, :]).then_inc(s_xed, 1)

            def out_half(g, b, done):
                hold(dve, ro["dn"], g + 1)
                hold(dve, ro["st"], done)
                dve.tensor_scalar(yo[:, b, HALF:D], PS[:, 5, :], wtT[:, ds(g, 1)], None, ALU.mult)\
                    .then_inc(ro["yd"], 1)

            rows_turned(0, 0)
            hidden(ro, 0, 0)
            rows_turned(1, 1)
            with dve.Fori(0, np_) as i:
                for j in range(2):
                    g = 2 * i + j + 1
                    hidden(ro, g, 1 - j)
                    rows_turned(g + 1, j)
                    out_half(g - 1, j, 16 * g)
            out_half(2 * np_, 0, 32 * np_ + 16)
            lf = Link(dve, s_fdv)
            for t in range(TT):
                if t % 2 == 0:
                    dve.wait_ge(s_frm, t // 2 + 1)
                    lf(dve.reciprocal(rstd[:, t:t + 2], rms[:, t:t + 2]))
                lf(stt(out=FS[:, t, :], in0=FS[:, t, :], scalar=rstd[:, t:t + 1], in1=ROWS[:, 3, :],
                       op0=ALU.mult, op1=ALU.mult))
                dve.tensor_tensor(FS[:, t, :], FS[:, t, :], Y[:, t, :], ALU.add).then_inc(s_fo, 1)


_INS = ["x", "c", "w_ada", "b_ada", "g_pre_mix", "w_in", "conv_w", "conv_b", "lru_wa", "lru_ba", "lru_wx", "lru_bx",
        "lru_lambda", "lam_q1", "lam_k1", "lam_q2", "lam_k2", "g_subln", "w_proj_rnn", "w_proj_att", "w_out",
        "g_post_mix", "g_pre_ffn", "w_router", "e_bias", "w1_e", "w3_e", "w2_e", "w1_s", "w3_s", "w2_s", "g_post_ffn"]


def kernel(**inputs):
    import numpy as _np
    import concourse.bacc as _bacc
    from concourse import mybir as _mybir
    from concourse.bass_utils import run_bass_kernel_spmd as _run

    nc = _bacc.Bacc("TRN2", target_bir_lowering=False, num_devices=1)
    arrays, args = {}, {}
    for name in _INS:
        v = _np.ascontiguousarray(inputs[name])
        arrays[f"in_{name}_dram"] = v
        args[name] = nc.dram_tensor(f"in_{name}_dram", v.shape, _mybir.dt.from_np(v.dtype), kind="ExternalInput").ap()
    out = nc.dram_tensor("out_0_dram", (1, T, D), _mybir.dt.from_np(_np.dtype("float32")), kind="ExternalOutput").ap()
    layer(nc, args, out)
    r = _run(nc, [arrays], core_ids=[0])
    return r.results[0]["out_0_dram"]
```

```python
import math
import concourse.bass as bass
from concourse import mybir
from contextlib import ExitStack

P = 128
D = 1024
T = 1024
KT = D // P
TT = T // P
NH = 8
HD = 64
HALF = 512
EPS = 1e-6
LRU_C = 8.0
LAM_INIT = 0.8 - 0.6 * math.exp(-0.3 * 0)
MASKED = -1e30
NE = 64
TOP = 8
NG = 8
TOPG = 4
FE = 256
FT = FE // P
ROUTED_SCALE = 2.5
NBLK = T * TOP // P + NE
COL_XR, COL_GR, COL_Q, COL_K, COL_V, COL_GA, COL_GB = (i * D for i in range(7))


def layer(nc, a, out):
    fp32 = mybir.dt.float32
    ACT = mybir.ActivationFunctionType
    ALU = mybir.AluOpType
    AX = mybir.AxisListType
    ds = bass.ds
    ctx = ExitStack()
    with ctx:
        base = 17 * 1024

        def at(name, kb, shape, dt=fp32):
            return nc.alloc_sbuf_tensor_at(name, shape, dt, offset=base + int(kb * 1024))

        def sem(name):
            return ctx.enter_context(nc.semaphore(name))

        hT = at("hT", 0, [P, KT, T])
        xcT = at("xcT", 32, [P, KT, T])
        V = at("V", 32, [P, TT, D])
        oT = at("oT", 32, [P, KT, T])
        ON = at("ON", 64, [P, TT, D])
        Y = at("Y", 64, [P, TT, D])
        gT = at("gateT", 96, [P, KT, T])
        WT = at("WT", 128, [P, 4, KT, P])
        TMP = 144
        XS = at("XS", 32, [P, TT, D])
        junk = at("junk", TMP + 32, [P, D])
        AW = at("AW", 64, [P, 4, KT, HALF])
        AA = at("AA", TMP + 16, [P, 8, HALF])
        xpad = at("xpad", TMP, [P, 2, 4 + T])
        rT = at("rT", TMP + 9, [P, T])
        iT = at("iT", TMP + 13, [P, T])
        tT = at("tT", TMP + 17, [P, T])
        aT = at("aT", TMP + 21, [P, T])
        mT = at("mT", TMP + 25, [P, T])
        geT = at("geT", TMP + 29, [P, T])
        hsT = at("hsT", TMP + 33, [P, T])
        ixT = at("ixT", TMP + 37, [P, T])
        GW = at("GW", TMP + 41, [P, 4, 2, P])
        WV = at("WV", TMP, [P, 4, KT, P])
        f32r = mybir.dt.float32r
        hTrest = at("hTrest", 0, [P, KT, T], f32r)
        hTexact = at("hTexact", 64, [P, KT, T], f32r)
        VWl = [at("VWl0", TMP, [P, 4, KT, P], f32r), at("VWl1", 128, [P, 4, KT, P], f32r)]
        VWh = [at("VWh0", TMP + 16, [P, 4, KT, P], f32r), at("VWh1", TMP + 32, [P, 4, KT, P], f32r)]
        SM = at("SM", TMP, [P, 2, 2, T])
        PT = at("PT", TMP + 16, [P, 2, TT, P])
        qT = at("qT", TMP + 24, [P, 2, T])
        kT = at("kT", TMP + 32, [P, 2, T])
        osq = at("osq", TMP + 40, [P, 2, P])
        sg = at("sg", TMP + 32, [P, 2, T])
        on2 = at("on2", TMP + 16, [P, 2, D])
        ty = at("ty", TMP + 40, [P, T])
        ROWS = at("ROWS", TMP, [P, 4, D])
        dg = at("dg", TMP + 24, [P, 2, KT, P])
        WO = at("WO", TMP + 16, [P, 4, KT, P])
        h2t = at("h2t", 32, [P, TT, D])
        W13 = at("W13", 32, [P, 2, KT, 2 * FE])
        W13h = at("W13h", 0, [P, 2, KT, 2 * FE], f32r)
        W13l = at("W13l", 112, [P, 2, KT, 2 * FE], f32r)
        W2 = at("W2", 96, [P, 2, FT, D])
        W2h = at("W2h", TMP, [P, FT, D], f32r)
        W2l = [at("W2l0", TMP + 8, [P, D], f32r), at("W2l1", TMP + 44, [P, D], f32r)]
        xTh = at("xTh", TMP + 24, [P, KT, P], f32r)
        xTl = at("xTl", TMP + 28, [P, KT, P], f32r)
        sgr = at("sgr", TMP + 40, [P, FE])
        hbr = at("hbr", TMP + 41, [P, FE])
        hTh = at("hTh", TMP + 42, [P, FT, P], f32r)
        hTl = at("hTl", TMP + 43, [P, FT, P], f32r)
        W2s = at("W2s", 112, [P, FT, D])
        sgm = at("sgm", 120, [P, 2, FE])
        hb = at("hb", 122, [P, 2, FE])
        hbT = at("hbT", 124, [P, 2, FT, P])
        xg = at("xg", TMP + 16, [P, 2, D])
        yo = at("yo", TMP + 32, [P, 2, D])
        wr = at("wr", TMP + 40, [P, KT, NE])
        M = at("M", TMP + 42, [P, TT, NE])
        oh = at("oh", 48, [P, TT * TOP, NE])
        oh2 = at("oh2", 32, [P, TT * TOP, NE])
        sco = at("sco", TMP + 16, [P, TT, NE])
        cho = at("cho", TMP + 18, [P, TT, NE])
        pos = at("pos", TMP + 20, [P, TT, NE])
        g8 = at("g8", TMP + 22, [P, TT * NG, 8])
        gm4 = at("gm4", TMP + 24, [P, TT, TOPG, NG])
        i32 = mybir.dt.int32
        u32 = mybir.dt.uint32
        tab = at("tab", TMP + 44, [P, P, 2])
        FS = at("FS", 0, [P, TT, D])
        vr0 = at("vr0", TMP + 44, [P, P])
        vr1 = at("vr1", TMP + 44.5, [3 * KT + 1, P])
        CON = 192
        ident = at("ident", CON, [P, P])
        ones = at("ones", CON + .5, [P, P])
        MASK = at("MASK", CON + 1, [P, P])
        wtT = at("wtT", CON + 1, [P, P])
        R = at("R", CON + 2, [P, T])
        B8 = at("B8", CON + 6, [P, T])
        sm0 = CON + 10
        small_at = [int(sm0 * 256)]

        def small(name, n, dt=fp32, parts=P):
            t = at(name, small_at[0] / 256, [parts, n], dt)
            small_at[0] += -(-n // 8) * 8
            assert small_at[0] <= 207 * 256 - 64, small_at
            return t

        vc0 = small("vc0", P)
        vc1 = small("vc1", 3 * KT + 1)
        ccol, bada = vc0[:, 0:8], vc0[:, 8:56]
        gpm, gpo, gpf, gpo2, cb = (vc0[:, 56 + 8 * j:64 + 8 * j] for j in range(5))
        cw = vc0[:, 96:128]
        ba, bx, lamc, gsub = vc1[:, 0:8], vc1[:, 8:16], vc1[:, 16:24], vc1[:, 24:25]
        cond = small("cond", KT)
        mod = small("mod", 48)
        rows_c = small("rows_c", 4 * KT)
        a1 = small("a1", KT)
        sp8 = small("sp8", KT)
        nsp8 = small("nsp8", KT)
        spt = small("spt", 4 * KT)
        gsub8 = small("gsub8", 1)
        lqk = small("lqk", 4 * HD, parts=1)
        lpr = small("lpr", HD, parts=1)
        ls = small("ls", 8, parts=1)
        nlam = small("nlam", 1)
        SL = small("SL", NH)
        ss = small("ss", TT)
        rms = small("rms", TT)
        rstd = small("rstd", TT)
        ssn = small("ssn", TT * NH)
        mn = small("mn", 4)
        lsum = small("lsum", 4)
        rl = small("rl", 4)
        c1 = small("c1", 2)
        eps = small("eps", 1)
        small_at[0] = int((CON + 2) * 256)
        tri = small("tri", P)
        tokT = small("tokT", P + 8, i32)
        ebias = small("ebias", NE)
        io64 = small("io64", NE)
        ioP = small("ioP", 1)
        thr = small("thr", 8)
        gs = small("gs", TT * NG)
        gv = small("gv", TT * 8)
        gi = small("gi", TT * 8, u32)
        gif = small("gif", TT * 8)
        gmk = small("gmk", TT * NG)
        v8 = small("v8", TT * 8)
        i8 = small("i8", TT * 8, u32)
        idxf = small("idxf", TT * TOP)
        w8 = small("w8", TT * TOP)
        wsm = small("wsm", TT)
        pairs = small("pairs", TT * TOP * 2)
        slotf = small("slotf", TT * TOP)
        slots = small("slots", TT * TOP, i32)
        posab = small("posab", NE)
        nbk = small("nbk", NE)
        pend = small("pend", NE)
        pst = small("pst", NE)
        eidf = small("eidf", 1)
        ehi = small("ehi", 1, i32)
        ehf = small("ehf", 1)
        tbf = small("tbf", 4)
        tbi = small("tbi", 4, i32)
        pendi = small("pendi", NE + 8, i32)
        npf = small("npf", 1)
        idxb = small("idxb", 2, i32)
        sidx = small("sidx", 2, i32)
        tbrow = small("tbrow", 4 * P, i32, parts=1)

        PS = ctx.enter_context(nc.psum_tensor("PS", [P, 8, HALF], fp32))

        def pair(p):
            return PS[:, 2 * p:2 * p + 2, :].rearrange("p b n -> p (b n)")

        acc = nc.dram_tensor("moe_sum_dram", (T + P, D), fp32, kind="Internal").ap()
        tabd = nc.dram_tensor("slot_table_dram", (P * P, 2), fp32, kind="Internal").ap()
        tbd = nc.dram_tensor("block_table_dram", (P, 4), i32, kind="Internal").ap()
        h2d = nc.dram_tensor("h2_dram", (T + P, D), fp32, kind="Internal").ap()

        s_vectors_loaded = sem("s_vectors_loaded")
        s_vectors_turned = sem("s_vectors_turned")
        s_columns_copied = sem("s_columns_copied")
        s_x_loaded = [sem(f"s_xin{j}") for j in range(TT // 2)]
        s_ada_loaded = [sem(f"s_ada{j}") for j in range(4)]
        s_w_loaded = [sem(f"s_w{j}") for j in range(4)]
        s_half_loaded = sem("s_half_loaded")
        s_vh = sem("s_vh")
        s_vl = sem("s_vl")
        s_gate_w_loaded = [sem(f"s_gw{j}") for j in range(4)]
        s_const_ready = sem("s_const_ready")
        s_pool_step = sem("s_pool_step")
        s_cond_ready = sem("s_cond_ready")
        s_mod_summed = sem("s_mod_summed")
        s_mod1_ready = sem("s_mod1_ready")
        s_ada_used = sem("s_ada_used")
        s_ada_partial = sem("s_ada_partial")
        s_ada_summed = sem("s_ada_summed")
        s_x_squared = sem("s_x_squared")
        s_x_rms = sem("s_x_rms")
        s_x_normed = sem("s_x_normed")
        s_x_turned = sem("s_x_turned")
        s_x_copied = sem("s_x_copied")
        s_dve_step = sem("s_dve_step")
        s_conv_step = sem("s_conv_step")
        s_lru_step = sem("s_lru_step")
        s_att_step = sem("s_att_step")
        s_merge_step = sem("s_merge_step")
        s_act_input = sem("s_act_input")
        s_exps_done = sem("s_exps_done")
        s_r_ready = sem("s_r_ready")
        s_h_ready = sem("s_h_ready")
        s_units_mul = sem("s_units_mul")
        s_bank_emptied = [sem("s_ev0"), sem("s_ev1")]
        s_conv_done = sem("s_conv_done")
        s_gates_mul = sem("s_gates_mul")
        s_i_ready = sem("s_i_ready")
        s_tanh_ready = sem("s_tanh_ready")
        s_a_ready = sem("s_a_ready")
        s_m2_ready = sem("s_m2_ready")
        s_m_ready = sem("s_m_ready")
        s_yr_ready = sem("s_yr_ready")
        s_lam_ready = sem("s_lam_ready")
        s_lam_spread = sem("s_lam_spread")
        s_nlam_ready = sem("s_nlam_ready")
        s_scores_ready = sem("s_scores_ready")
        s_exps_ready = sem("s_exps_ready")
        s_probs_ready = sem("s_probs_ready")
        s_probs_turned = sem("s_probs_turned")
        s_probs_copied = sem("s_probs_copied")
        s_values_mul = sem("s_values_mul")
        s_outs_copied = sem("s_outs_copied")
        s_head_rms = sem("s_head_rms")
        s_o_normed = sem("s_o_normed")
        s_o_turned = sem("s_o_turned")
        s_o_copied = sem("s_o_copied")
        s_merged = sem("s_merged")
        s_mod2_ready = sem("s_mod2_ready")
        s_diag_ready = sem("s_diag_ready")
        s_row_spread = sem("s_row_spread")
        s_rows_ready = sem("s_rows_ready")
        s_y_squared = sem("s_y_squared")
        s_y_rms = sem("s_y_rms")
        s_x1_ready = sem("s_x1_ready")
        s_h2_ready = sem("s_h2_ready")
        s_h2_turned = sem("s_h2_turned")
        s_h2_copied = sem("s_h2_copied")
        s_h2p = sem("s_h2p")
        s_h2_stored = [sem("s_h2d0"), sem("s_h2d1")]
        s_out = sem("s_out")
        s_ld = sem("s_ld")
        s_lg = sem("s_lg")
        s_sco = sem("s_sco")
        s_route_step = sem("s_route_step")
        s_M = sem("s_M")
        s_rk = sem("s_rk")
        s_slot = sem("s_slot")
        s_c2 = sem("s_c2")
        s_tb0 = sem("s_tb0")
        s_sct = sem("s_sct")
        s_table_loaded = sem("s_table_loaded")
        s_table_turned = sem("s_table_turned")
        s_table_copied = sem("s_table_copied")
        s_blocks_ready = sem("s_blocks_ready")
        s_blocks_stored = sem("s_blocks_stored")
        s_blocks_loaded = sem("s_blocks_loaded")
        s_acc0 = sem("s_acc0")
        sh = {n: sem("s_sh_" + n) for n in ("up", "sg", "t", "hb", "hT", "he", "dn", "ya", "yd")}
        ro = {n: sem("s_ro_" + n) for n in ("up", "sg", "t", "hb", "hT", "dn", "ya", "st")}
        s_shared_stored = [sem("s_shst0"), sem("s_shst1")]
        s_up_loaded = [sem("s_w13_0"), sem("s_w13_1")]
        s_down_loaded = [sem("s_w2_0"), sem("s_w2_1")]
        s_index_step = sem("s_index_step")
        s_rows_gathered = [sem("s_xg0"), sem("s_xg1")]
        s_rows_turned = sem("s_rows_turned")
        s_xh = sem("s_xh")
        s_xl = sem("s_xl")
        s_wh = sem("s_wh")
        s_wl = sem("s_wl")
        s_w2h = sem("s_w2h")
        s_w2l = sem("s_w2l")
        s_w2lp = sem("s_w2lp")
        s_hh = sem("s_hh")
        s_hl = sem("s_hl")
        s_six = sem("s_six")
        s_sum_loaded = [sem(f"s_fl{j}") for j in range(TT)]
        s_sum_squared = sem("s_sum_squared")
        s_sum_rms = sem("s_sum_rms")
        s_out_ready = sem("s_out_ready")
        s_out_stored = sem("s_out_stored")

        def vector_rows():
            r = 0
            for name in ("c", "b_ada", "g_pre_mix", "g_post_mix", "g_pre_ffn", "g_post_ffn", "conv_b"):
                src = a[name][0].rearrange("(k p) -> k p", p=P)
                yield vr0, r, src
                r += src.shape[0]
            yield vr0, r, a["conv_w"][0].rearrange("j (k p) -> (j k) p", p=P)
            yield vr1, 0, a["lru_ba"][0]
            yield vr1, KT, a["lru_bx"][0]
            yield vr1, 2 * KT, a["lru_lambda"][0].rearrange("(k p) -> k p", p=P)
            yield vr1, 3 * KT, a["g_subln"]

        N_SMALL = 12 + 4
        s_turn = {e: sem(f"s_turn_{e.name}") for e in (nc.sync.engine, nc.scalar.engine, nc.vector.engine,
                                                        nc.tensor.engine, nc.gpsimd.engine)}
        U_XR, U_GR, U_GA, U_YA, U_V, U_QK, U_GB, U_O, U_SH = 0, 8, 16, 24, 32, 40, 56, 72, 80
        EV_PER_HEAD = 9
        EV_ATT = U_QK // 2 + 1

        class Link:

            def __init__(self, eng, s, start=0, per=0):
                self.eng, self.s, self.start, self.per, self.n, self.i = eng, s, start, per, 0, None

            def at(self, i):
                self.i, self.n = i, 0

            def __call__(self, ins, wait=True):
                ins.then_inc(self.s, 1)
                self.n += 1
                if wait:
                    self.wait()

            def wait(self):
                v = self.start + self.n
                hold(self.eng, self.s, v if self.i is None else self.i * self.per + v)

        def hold(eng, s, value):
            eng.wait_ge(s, value)
            eng.sem_inc(s_turn[eng.engine], 1)

        block = ctx.enter_context(nc.Block())

        def wtile(W, col):
            return W[:, col].rearrange("(k p) c -> p k c", p=P)

        def expert_raw(eng, g):
            return eng.value_load(tbrow[0:1, ds(4 * g, 1)], min_val=0, max_val=1)

        def expert_loads(eng, g):
            return [eng.value_load(tbrow[0:1, ds(4 * g + 1 + b, 1)], min_val=1, max_val=NE) for b in range(2)]

        @block.sync
        def _(sp):
            def x_tiles():
                for q in range(TT // 2):
                    sp.dma_start(XS[:, 2 * q:2 * q + 2, :], a["x"][0, 2 * P * q:2 * P * (q + 1), :]
                                 .rearrange("(t p) d -> p t d", p=P)).then_inc(s_x_loaded[q], 16)

            x_tiles()
            for dst, r0, src in vector_rows():
                if dst is vr1:
                    sp.dma_start(dst[r0:r0 + src.shape[0], :], src).then_inc(s_vectors_loaded, 16)
            for j, n in enumerate(("lam_q1", "lam_k1", "lam_q2", "lam_k2")):
                sp.dma_start(lqk[:, j * HD:(j + 1) * HD], a[n]).then_inc(s_vectors_loaded, 16)

            def tile(u, slot, W, c, quad):
                hold(sp, s_units_mul, quad if quad is not None else u - 3)
                sp.dma_start(WT[:, slot, :, :], wtile(W, ds(c, P))).then_inc(s_w_loaded[slot], 16)

            w_in = a["w_in"][0]
            for j in range(4):
                sp.dma_start(WT[:, j, :, :], wtile(w_in, ds(COL_XR + P * j, P))).then_inc(s_w_loaded[j], 16)
            for j in range(4):
                tile(U_XR + 4 + j, j, w_in, COL_XR + P * (4 + j), None)
            with sp.Fori(0, 2) as i:
                for j in range(4):
                    hold(sp, s_gates_mul, 4 * i + j + 1)
                    for g, W in enumerate((a["lru_wa"], a["lru_wx"])):
                        sp.dma_start(GW[:, j, g, :], W[0, ds(4 * i + j, 1)].rearrange("o c d -> (o c) d"))\
                            .then_inc(s_gate_w_loaded[j], 16)
                    tile(U_GR + 4 * i + j, j, w_in, COL_GR + P * (4 * i + j), None)
            with sp.Fori(0, 2) as i:
                for j in range(4):
                    tile(U_GA + 4 * i + j, j, w_in, COL_GA + P * (4 * i + j), None)
            sp.wait_ge(s_yr_ready, KT + 1)
            for j in range(4):
                sp.dma_start(WV[:, j, :, :], wtile(w_in, ds(COL_V + P * j, P))).then_inc(s_half_loaded, 16)
            with sp.Fori(0, 2) as i:
                for j in range(4):
                    tile(U_YA + 4 * i + j, j, a["w_proj_rnn"][0], P * (4 * i + j), None)
            for j in range(4):
                tile(0, j, w_in, COL_V + P * (4 + j), U_V - 3 + j)

            def qk_tiles(i, quad):
                for j in range(4):
                    tile(0, j, w_in, (COL_Q if j % 2 == 0 else COL_K) + P * (2 * i + j // 2), quad)

            qk_tiles(0, U_QK)
            with sp.Fori(1, NH // 2) as i:
                qk_tiles(i, U_QK + 4 * i)
            with sp.Fori(0, 4) as i:
                for j in range(4):
                    n = 2 * i + j // 2
                    if j % 2 == 0:
                        tile(U_GB + 4 * i + j, j, w_in, COL_GB + P * n, None)
                    else:
                        tile(U_GB + 4 * i + j, j, a["w_proj_att"][0], P * n, None)
            for j in range(4):
                tile(0, j, a["w_out"][0], P * j, U_O - 3 + j)
            sp.wait_ge(s_units_mul, U_O)
            x_tiles()
            sp.wait_ge(s_merged, KT + 2)
            sp.dma_start(wr[:, :, :], a["w_router"][0].rearrange("(k p) e -> p k e", p=P)).then_inc(s_ld, 16)
            sp.wait_ge(s_row_spread, 4)
            for j in range(4):
                sp.dma_start(WO[:, j, :, :], wtile(a["w_out"][0], ds(P * (4 + j), P))).then_inc(s_half_loaded, 16)
            for j, W in enumerate((a["w1_s"][0], a["w1_s"][0], a["w3_s"][0], a["w3_s"][0])):
                sp.wait_ge(s_units_mul, U_O + 4)
                sp.dma_start(WT[:, j, :, :], wtile(W, ds(P * (j % 2), P))).then_inc(s_w_loaded[j], 16)
            sp.wait_ge(s_units_mul, U_SH)
            sp.wait_ge(s_h2p, 32)
            sp.dma_start(W2s[:, :, :], a["w2_s"][0].rearrange("(k p) n -> p k n", p=P)).then_inc(s_ld, 16)
            sp.dma_start(ebias[:, :], a["e_bias"].broadcast_to([P, NE])).then_inc(s_ld, 16)

            def expert_up(e, b):
                sp.dma_start(W13[:, b, :, 0:FE], a["w1_e"][0, ds(e, 1)].rearrange("o (k p) f -> p (o k) f", p=P))\
                    .then_inc(s_up_loaded[b], 16)
                sp.dma_start(W13[:, b, :, FE:2 * FE], a["w3_e"][0, ds(e, 1)].rearrange("o (k p) f -> p (o k) f", p=P))\
                    .then_inc(s_up_loaded[b], 16)

            def expert_down(e, b):
                sp.dma_start(W2[:, b, :, :], a["w2_e"][0, ds(e, 1)].rearrange("o (k p) n -> p (o k) n", p=P))\
                    .then_inc(s_down_loaded[b], 16)

            for b in range(2):
                expert_down(b, b)
            sp.wait_ge(s_slot, 1)
            for b in range(2):
                expert_up(b, b)
            for t in range(TT):
                sp.wait_ge(sh["ya"], t + 1)
                sp.wait_ge(sh["yd"], t + 1)
                sp.dma_start(acc[t * P:(t + 1) * P, :], yo[:, t % 2, :]).then_inc(s_shared_stored[t % 2], 16)
            sp.wait_ge(s_sct, 16 * TT * TOP)
            sp.dma_start(tab[:, :, :], tabd.rearrange("(g s) c -> g s c", s=P)).then_inc(s_table_loaded, 16)
            sp.wait_ge(s_blocks_ready, 2)
            sp.dma_start(tbd, tbi[:, :]).then_inc(s_blocks_stored, 16)
            sp.wait_ge(s_blocks_stored, 16)
            sp.dma_start(tbrow[:, :], tbd.rearrange("(o g) c -> o (g c)", o=1)).then_inc(s_blocks_loaded, 16)
            def blocks_to(e):
                return sp.value_load(pendi[0:1, ds(e, 1)], min_val=1, max_val=NBLK)

            def next_up(e, b):
                hold(sp, s_wl, 4 * blocks_to(e))
                expert_up(e + 2, b)

            def next_down(e, b):
                last = blocks_to(e)
                hold(sp, s_w2l, last)
                hold(sp, s_w2lp, last)
                expert_down(e + 2, b)

            next_up(0, 0)
            with sp.Fori(0, NE // 2 - 2) as i:
                for b in range(2):
                    next_up(2 * i + b + 1, 1 - b)
                    next_down(2 * i + b, b)
            next_up(NE - 3, 1)
            next_down(NE - 4, 0)
            next_down(NE - 3, 1)
            pairs_n = sp.value_load(pendi[0:1, NE:NE + 1], min_val=1, max_val=NBLK // 2)
            hold(sp, ro["st"], 32 * pairs_n + 48)
            for t in range(TT):
                sp.dma_start(FS[:, t, :], acc[t * P:(t + 1) * P, :]).then_inc(s_sum_loaded[t], 16)
            for t in range(TT):
                sp.wait_ge(s_out_ready, t + 1)
                sp.dma_start(out[0, t * P:(t + 1) * P, :], FS[:, t, :]).then_inc(s_out_stored, 16)
            sp.wait_ge(s_out_stored, 16 * TT)
            for b in range(2):
                hold(sp, s_rows_gathered[b], 16 * pairs_n + 32)

        @block.gpsimd
        def _(pool):
            link = Link(pool, s_pool_step)
            link(pool.memset(ident[:, :], 0.0))
            link(pool.affine_select(out=ident[:, :], in_=ident[:, :], compare_op=ALU.not_equal, fill=1.0, base=0,
                                    pattern=[[-1, P]], channel_multiplier=1))
            link(pool.memset(ones[:, :], 1.0), wait=False)
            link(pool.memset(MASK[:, :], 0.0))
            link(pool.affine_select(out=MASK[:, :], in_=MASK[:, :], compare_op=ALU.is_ge, fill=MASKED, base=0,
                                    pattern=[[-1, P]], channel_multiplier=1), wait=False)
            link(pool.iota(R[:, :], [[1, T]], base=P - T, channel_multiplier=-1,
                           allow_small_or_imprecise_dtypes=True), wait=False)
            for h in range(NH):
                link(pool.memset(SL[:, h:h + 1], 2.0 ** (-8.0 * (h + 1) / NH) * HD ** 0.5), wait=False)
            link.wait()
            pool.sem_inc(s_const_ready, 1)

            def ada(c, b):
                pool.dma_start(AW[:, b, :, :], a["w_ada"][0][:, ds(HALF * c, HALF)]
                               .rearrange("(k p) c -> p k c", p=P)).then_inc(s_ada_loaded[b], 16)

            pool.wait_ge(s_vectors_loaded, 16 * N_SMALL)
            for c in range(4):
                ada(c, c)
            with pool.Fori(2, 6) as i:
                for b in range(2):
                    pool.wait_ge(s_ada_used, 2 * i + b + 1)
                    ada(2 * i + b, b)
            for b in range(2):
                pool.dma_start(h2d[T + HD * b:T + HD * (b + 1), :], R[HD * b:HD * (b + 1), :]).then_inc(s_h2p, 16)
            with pool.Fori(0, TT // 2) as i:
                for b in range(2):
                    hold(pool, s_h2_ready, 2 * i + b + 1)
                    pool.dma_start(h2d[ds(P * (2 * i + b), P), :], h2t[:, ds(2 * i + b, 1), :]
                                   .rearrange("p o n -> p (o n)")).then_inc(s_h2_stored[b], 16)
            pool.wait_ge(s_h2p, 32)
            lp = Link(pool, s_c2)
            lp(pool.memset(tri[:, :], 1.0))
            lp(pool.affine_select(out=tri[:, :], in_=tri[:, :], compare_op=ALU.is_gt, fill=0.0, base=0,
                                  pattern=[[1, P]], channel_multiplier=-1), wait=False)
            lp(pool.iota(io64[:, :], [[1, NE]], base=0, channel_multiplier=0, allow_small_or_imprecise_dtypes=True),
               wait=False)
            lp(pool.iota(ioP[:, :], [[0, 1]], base=0, channel_multiplier=1, allow_small_or_imprecise_dtypes=True),
               wait=False)
            lp(pool.iota(thr[:, :], [[P, 8]], base=P, channel_multiplier=0, allow_small_or_imprecise_dtypes=True),
               wait=False)
            pv = pairs[:, :].rearrange("p (t k c) -> p t k c", t=TT, k=TOP)
            for t in range(TT):
                lp(pool.iota(pv[:, t, :, 0], [[0, TOP]], base=t * P, channel_multiplier=1,
                             allow_small_or_imprecise_dtypes=True), wait=False)
            lp(pool.iota(tab[:, :, 0], [[1, P]], base=T, channel_multiplier=0, allow_small_or_imprecise_dtypes=True),
               wait=False)
            lp(pool.iota(tokT[:, P:P + 2], [[0, 2]], base=T, channel_multiplier=1), wait=False)
            lp(pool.memset(tab[:, :, 1], 0.0))
            pool.dma_start(tabd.rearrange("(g s) c -> g s c", s=P), tab[:, :, :]).then_inc(s_tb0, 16)
            pool.wait_ge(s_h2_stored[0], 16 * (TT // 2))
            pool.wait_ge(s_h2_stored[1], 16 * (TT // 2))
            for b in range(2):
                pool.dma_start(acc[T + HD * b:T + HD * (b + 1), :], ROWS[HD * b:HD * (b + 1), 3, :])\
                    .then_inc(ro["st"], 16)
            pool.wait_ge(s_tb0, 16)
            pool.wait_ge(s_slot, 1)
            for t in range(TT):
                for k in range(TOP):
                    pool.indirect_dma_start(tabd, bass.IndirectOffsetOnAxis(slots[:, t * TOP + k:t * TOP + k + 1], 0),
                                            pv[:, t, k, :], None).then_inc(s_sct, 16)

            def gather(g, b):
                lq(pool.tensor_copy(idxb[:, b:b + 1], tokT[:, ds(g, 1)]))
                pool.indirect_dma_start(xg[:, b, :], None, h2d, bass.IndirectOffsetOnAxis(idxb[:, b:b + 1], 0))\
                    .then_inc(s_rows_gathered[b], 16)

            def add(g, b, done):
                hold(pool, ro["ya"], g + 2)
                lq(pool.tensor_copy(sidx[:, b:b + 1], tokT[:, ds(g, 1)]))
                if done is not None:
                    hold(pool, ro["st"], done)
                pool.indirect_dma_start(acc, bass.IndirectOffsetOnAxis(sidx[:, b:b + 1], 0), yo[:, b, :], None,
                                        compute_op=ALU.add).then_inc(ro["st"], 16)

            def down_rest(g):
                par = expert_raw(pool, g)
                hold(pool, s_w2h, 2 * g + 2)
                pool.tensor_tensor(W2l[1][:, :], W2[:, ds(par, 1), 1, :].rearrange("p o n -> p (o n)"),
                                   W2h[:, 1, :].bitcast(fp32), ALU.subtract).then_inc(s_w2lp, 1)

            pool.wait_ge(s_table_copied, 2)
            pool.wait_ge(s_blocks_ready, 2)
            pool.wait_ge(s_blocks_loaded, 16)
            np_ = pool.value_load(pendi[0:1, NE:NE + 1], min_val=1, max_val=NBLK // 2 - 1)
            lq = Link(pool, s_index_step, 0, 4)
            for b in range(2):
                gather(b, b)
            for b in range(2):
                pool.wait_ge(s_shared_stored[b], 16 * TT // 2)
            pool.wait_ge(s_rows_turned, 1)
            gather(2, 0)
            pool.wait_ge(s_rows_turned, 2)
            gather(3, 1)
            down_rest(0)
            lq.start, lq.n = 4, 0
            with pool.Fori(0, np_) as i:
                lq.at(i)
                for j in range(2):
                    g = 2 * i + j + 1
                    hold(pool, s_rows_turned, g + 2)
                    gather(g + 3, j)
                    down_rest(g)
                    add(g - 1, j, (2 * i + j) * 16 + 32)
            lq.i = np_
            lq.n = 0
            add(2 * np_, 0, 32 * np_ + 32)

        def unit(pe, slot, w_round, ev_at, p, moving, tiles_from=None):
            pe.wait_ge(s_w_loaded[slot], 16 * w_round)
            pe.wait_ge(s_bank_emptied[p], ev_at)
            for half in range(2):
                for k in range(KT):
                    if tiles_from is not None and half == 0:
                        pe.wait_ge(s_h_ready, tiles_from + k + 1)
                    last = pe.matmul(PS[:, 2 * p + half, :], WT[:, slot, k, :],
                                     moving[:, k, half * HALF:(half + 1) * HALF], start=(k == 0), stop=(k == KT - 1))
            last.then_inc(s_units_mul, 1)

        def rows_unit(pe, q, w_round, ev_at, p, lhs, W):
            if q == 0 and W is WT:
                for slot in range(4):
                    pe.wait_ge(s_w_loaded[slot], 16 * w_round)
            elif q == 0:
                pe.wait_ge(s_half_loaded, 64 * w_round)
            pe.wait_ge(s_bank_emptied[p], ev_at)
            for half in range(2):
                t = 2 * q + half
                for k in range(KT):
                    last = pe.matmul(PS[:, 2 * p + half, :], lhs[:, k, t * P:(t + 1) * P], W[:, :, k, :],
                                     start=(k == 0), stop=(k == KT - 1))
            last.then_inc(s_units_mul, 1)

        def split(dst, lh, ll, rh, rl, first, last):
            pe = nc.tensor
            pe.matmul(dst, lh, rh, start=first, stop=False)
            pe.matmul(dst, lh, rl, start=False, stop=False)
            return pe.matmul(dst, ll, rh, start=False, stop=last)

        MODB = 7

        def group(qt):
            return sum(t // 4 + 1 for t in range(qt))

        def tcols(buf, t):
            return buf[:, :, ds(t * P, P)]

        def pair3(p):
            return pair(p).rearrange("p (k n) -> p k n", k=KT)

        @block.tensor
        def _(pe):
            pe.sem_inc(s_values_mul, 2)
            pe.sem_inc(ro["dn"], 1)
            pe.sem_inc(s_gates_mul, 4)
            pe.wait_ge(s_const_ready, 1)
            pe.wait_ge(s_vectors_loaded, 16 * N_SMALL)
            pe.transpose(PS[:, 4, 0:P], vr0[:, :], ident[:, :])
            pe.transpose(PS[:, 5, 0:3 * KT + 1], vr1[:, :], ident[0:3 * KT + 1, 0:3 * KT + 1])\
                .then_inc(s_vectors_turned, 1)

            def ada(chunks):
                for c in chunks:
                    pe.wait_ge(s_ada_summed, c + 1)
                    for q in range(4):
                        last = pe.matmul(PS[:, MODB, 4 * c + q:4 * c + q + 1], AA[:, c % 4 if c < 4 else c - 4,
                                         q * P:(q + 1) * P], ones[:, 0:1], start=True, stop=True)
                    last.then_inc(s_mod_summed, 1)

            for t in range(TT):
                pe.wait_ge(s_x_normed, t + 1)
                pe.wait_ge(s_x_copied, t + 1)
                for k in range(KT):
                    last = pe.transpose(pair(t % 2)[:, k * P:(k + 1) * P], XS[:, t, k * P:(k + 1) * P], ident[:, :])
                last.then_inc(s_x_turned, 1)
            ada(range(4))
            with pe.Fori(0, 2) as i:
                for j in range(4):
                    unit(pe, j, i + 1 + U_XR // 4, U_XR // 2 + 2 * i + j // 2 + 1, j % 2, hT,
                         tiles_from=0 if j == 0 else None)
            pe.wait_ge(s_lam_ready, 1)
            pe.matmul(PS[:, 6, 0:1], ones[0:1, :], ls[:, 4:5], start=True, stop=True).then_inc(s_lam_spread, 1)
            pe.wait_ge(s_nlam_ready, 1)
            pe.wait_ge(s_mod1_ready, 1)
            with pe.Fori(0, 2) as i:
                for j in range(4):
                    n = 4 * i + j
                    unit(pe, j, i + 1 + U_GR // 4, U_GR // 2 + 2 * i + j // 2 + 1, j % 2, hT)
                    pe.wait_ge(s_gate_w_loaded[j], 32 * i + 32)
                    pe.wait_ge(s_conv_done, n + 3)
                    pe.wait_ge(s_i_ready, n + 1)
                    for g in range(2):
                        for half in range(2):
                            last = pe.matmul(PS[:, 4 + 2 * g + half, :], GW[:, j, g, :],
                                             xcT[:, ds(n, 1), half * HALF:(half + 1) * HALF]
                                             .rearrange("p o n -> p (o n)"), start=True, stop=True)
                    last.then_inc(s_gates_mul, 1)
            with pe.Fori(0, 2) as i:
                for j in range(4):
                    unit(pe, j, i + 1 + U_GA // 4, U_GA // 2 + 2 * i + j // 2 + 1, j % 2, hT)
            pe.wait_ge(s_i_ready, KT + 1)
            ada(range(4, 12))
            pe.wait_ge(s_yr_ready, KT + 1)
            with pe.Fori(0, 2) as i:
                for j in range(4):
                    unit(pe, j, i + 1 + U_YA // 4, U_YA // 2 + 2 * i + j // 2 + 1, j % 2, xcT)
            for i in range(2):
                pe.wait_ge(s_vl, KT + 4 * i + 4)
                for q in range(4):
                    pe.wait_ge(s_bank_emptied[q % 2], U_V // 2 + 2 * i + q // 2 + 1)
                    for half in range(2):
                        t = slice((2 * q + half) * P, (2 * q + half + 1) * P)
                        for k in range(KT):
                            last = split(PS[:, 2 * (q % 2) + half, :], hTexact[:, k, t], hTrest[:, k, t],
                                         VWh[i][:, :, k, :], VWl[i][:, :, k, :], k == 0, k == KT - 1)
                    last.then_inc(s_units_mul, 1)
            pe.wait_ge(s_mod2_ready, 1)

            unit(pe, 0, U_QK // 4, EV_ATT, 0, hT, tiles_from=KT)
            with pe.Fori(0, NH // 2) as i:
                for b in range(2):
                    h = 2 * i + b
                    unit(pe, 2 * b + 1, i + U_QK // 4, EV_ATT + EV_PER_HEAD * h, 1, hT)

                    def scores(qt):
                        L = (qt + 1) * P
                        for c in range(2):
                            if qt == 0:
                                pe.wait_ge(s_bank_emptied[0], EV_ATT + EV_PER_HEAD * h + 1)
                                pe.wait_ge(s_bank_emptied[1], EV_ATT + EV_PER_HEAD * h + 1)
                            else:
                                pe.wait_ge(s_bank_emptied[c], EV_ATT + EV_PER_HEAD * h + 1 + qt)
                            for n0 in range(0, L, HALF):
                                n1 = min(L, n0 + HALF)
                                last = pe.matmul(pair(c)[:, n0:n1], qT[c * HD:(c + 1) * HD, b, qt * P:(qt + 1) * P],
                                                 kT[c * HD:(c + 1) * HD, b, n0:n1], start=True, stop=True)
                            last.then_inc(s_scores_ready, 1)

                    def turn(qt):
                        pe.wait_ge(s_probs_ready, 8 * h + qt + 1)
                        for g in range(qt // 4 + 1):
                            G = group(qt) + g
                            pe.wait_ge(s_probs_copied, 12 * h + G + 1)
                            for kb in range(4 * g, min(4 * g + 4, qt + 1)):
                                last = pe.transpose(PS[:, 6 + G % 2, (kb % 4) * P:(kb % 4 + 1) * P],
                                                    SM[:, qt % 2, 0, kb * P:(kb + 1) * P], ident[:, :])
                            last.then_inc(s_probs_turned, 1)

                    def values(qt):
                        pe.wait_ge(s_probs_copied, 12 * h + group(qt) + qt // 4 + 1 + 2)
                        pe.wait_ge(s_outs_copied, 8 * h + qt + 1)
                        for kb in range(qt + 1):
                            last = pe.matmul(PS[:, 4 + qt % 2, 0:P], PT[:, qt % 2, kb, :],
                                             V[:, kb, ds(h * P, P)], start=(kb == 0), stop=(kb == qt))
                        last.then_inc(s_values_mul, 1)

                    scores(0)
                    for qt in range(TT):
                        if qt + 1 < TT:
                            scores(qt + 1)
                        else:
                            unit(pe, 2 - 2 * b, i + b + U_QK // 4, EV_ATT + EV_PER_HEAD * (h + 1), 0, hT)
                        turn(qt)
                        if qt >= 1:
                            values(qt - 1)
                    values(TT - 1)

            E0 = EV_ATT + NH * EV_PER_HEAD

            def gate_unit(i, j):
                unit(pe, j, i + U_GB // 4, E0 + 2 * i + j // 2, j % 2, hT if j % 2 == 0 else oT)

            pe.wait_ge(s_probs_copied, 12 * NH + 2)
            pe.wait_ge(s_outs_copied, 8 * NH + 2)
            with pe.Fori(0, TT // 2) as i:
                for b in range(2):
                    pe.wait_ge(s_o_normed, 2 * i + b + 1)
                    pe.wait_ge(s_o_copied, 2 * i + b + 1)
                    for k in range(KT):
                        last = pe.transpose(pair(2 + b)[:, k * P:(k + 1) * P], on2[:, b, k * P:(k + 1) * P],
                                            ident[:, :])
                    last.then_inc(s_o_turned, 1)
            pe.wait_ge(s_o_copied, TT + 2)
            for j in range(1, 4):
                gate_unit(0, j)
            with pe.Fori(1, 4) as i:
                for j in range(4):
                    gate_unit(i, j)
            for r in range(4):
                pe.wait_ge(s_diag_ready, KT * (r + 1))
                if r >= 2:
                    pe.wait_ge(s_rows_ready, r - 1)
                for half in range(2):
                    last = pe.matmul(PS[:, 4 + 2 * (r % 2) + half, :], ones[:, :],
                                     dg[:, r % 2, 4 * half:4 * half + 4, :].rearrange("p k n -> p (k n)"),
                                     start=True, stop=True)
                last.then_inc(s_row_spread, 1)
            pe.wait_ge(s_merged, KT + 2)
            def turn_h2(t):
                pe.wait_ge(s_h2_ready, t + 1)
                pe.wait_ge(s_h2_copied, t + 1)
                for k in range(KT):
                    last = pe.transpose(pair(2 + t % 2)[:, k * P:(k + 1) * P], h2t[:, t, k * P:(k + 1) * P],
                                        ident[:, :])
                last.then_inc(s_h2_turned, 1)

            def out_unit(i, q):
                rows_unit(pe, q, U_O // 4 if i == 0 else 2, E0 + (U_O - U_GB) // 2 + 2 * i + q // 2, q % 2, gT,
                          WO if i else WT)

            for q in range(4):
                out_unit(0, q)
            pe.wait_ge(s_rows_ready, 4)
            for q in range(4):
                out_unit(1, q)
                if q >= 2:
                    turn_h2(2 * q - 4)
                    turn_h2(2 * q - 3)
            for t in range(4, TT):
                turn_h2(t)
            pe.wait_ge(s_h2_copied, TT + 2)
            pe.wait_ge(s_ld, 48)
            for t in range(TT):
                for k in range(KT):
                    last = pe.matmul(PS[:, 7, t * NE:(t + 1) * NE], hT[:, k, t * P:(t + 1) * P], wr[:, k, :],
                                     start=(k == 0), stop=(k == KT - 1))
                last.then_inc(s_lg, 1)

            def turn_hidden(S, g, b):
                hold(pe, S["hb"], g + 1)
                for f in range(FT):
                    last = pe.transpose(PS[:, 6, f * P:(f + 1) * P], hb[:, b, f * P:(f + 1) * P], ident[:, :])
                last.then_inc(S["hT"], 1)

            def up(S, g, b, lhs, w):
                for k in range(KT):
                    last = pe.matmul(PS[:, 2 + b, :], lhs(k), w(k), start=(k == 0), stop=(k == KT - 1))
                last.then_inc(S["up"], 1)

            def down(S, g, b, w):
                hold(pe, S["he"], g + 1)
                for half in range(2):
                    for f in range(FT):
                        last = pe.matmul(PS[:, 4 + half, :], hbT[:, b, f, :], w(f, half),
                                         start=(f == 0), stop=(f == FT - 1))
                last.then_inc(S["dn"], 1)

            for j in range(4):
                pe.wait_ge(s_w_loaded[j], 16 * (U_SH // 4 - 1))
            def shared_up(t):
                if t >= 2:
                    pe.wait_ge(sh["hb"], t - 1)
                up(sh, t, t % 2, lambda k: hT[:, k, t * P:(t + 1) * P], lambda k: WT[:, :, k, :])

            for t in range(2):
                shared_up(t)
            pe.wait_ge(s_M, TT)
            for t in range(TT):
                for j in range(t + 1):
                    pe.matmul(PS[:, 0, t * NE:(t + 1) * NE], (tri if j == t else ones)[:, :], M[:, j, :],
                              start=(j == 0), stop=(j == t))
            for j in range(TT):
                last = pe.matmul(PS[:, 1, 0:NE], ones[:, :], M[:, j, :], start=(j == 0), stop=(j == TT - 1))
            last.then_inc(s_rk, 1)
            for t in range(TT):
                turn_hidden(sh, t, t % 2)
                if 1 <= t < TT - 1:
                    shared_up(t + 1)
                if t >= 1:
                    pe.wait_ge(sh["ya"], t)
                    pe.wait_ge(sh["yd"], t)
                down(sh, t, t % 2, lambda f, half: W2s[:, f, half * HALF:(half + 1) * HALF])
            pe.wait_ge(s_table_loaded, 16)
            pe.wait_ge(s_blocks_ready, 1)
            for c in range(2):
                pe.transpose(PS[:, c, 0:P], tab[:, :, c], ident[:, :]).then_inc(s_table_turned, 1)
            pe.wait_ge(s_table_copied, 2)
            pe.wait_ge(s_blocks_loaded, 16)
            np_ = pe.value_load(pendi[0:1, NE:NE + 1], min_val=1, max_val=NBLK // 2 - 1)

            def turn_rows(g, b, xg_round):
                hold(pe, s_rows_gathered[b], xg_round)
                for k in range(KT):
                    last = pe.transpose(PS[:, k // 4, (k % 4) * P:(k % 4 + 1) * P], xg[:, b, k * P:(k + 1) * P],
                                        ident[:, :])
                last.then_inc(s_rows_turned, 1)

            def turn_block(g):
                hold(pe, ro["hb"], g + 1)
                for f in range(FT):
                    last = pe.transpose(PS[:, 6, f * P:(f + 1) * P], hbr[:, f * P:(f + 1) * P], ident[:, :])
                last.then_inc(ro["hT"], 1)

            def block_up(g, b):
                hold(pe, s_xl, 2 * g + 2)
                for k in range(KT):
                    if k % 2 == 0:
                        hold(pe, s_wl, 4 * g + k // 2 + 1)
                    last = split(PS[:, 2 + b, :], xTh[:, k, :], xTl[:, k, :], W13h[:, b, k, :], W13l[:, b, k, :],
                                 k == 0, k == KT - 1)
                last.then_inc(ro["up"], 1)

            def block_down(g):
                hold(pe, s_hl, g + 1)
                hold(pe, s_w2l, g + 1)
                hold(pe, s_w2lp, g + 1)
                hold(pe, ro["ya"], g + 1)
                for half in range(2):
                    n0 = half * HALF
                    for f in range(FT):
                        last = split(PS[:, 4 + half, :], hTh[:, f, :], hTl[:, f, :], W2h[:, f, n0:n0 + HALF],
                                     W2l[f][:, n0:n0 + HALF], f == 0, f == FT - 1)
                last.then_inc(ro["dn"], 1)

            turn_rows(0, 0, 16)
            block_up(0, 0)
            turn_rows(1, 1, 16)
            with pe.Fori(0, np_) as i:
                for j in range(2):
                    g = 2 * i + j + 1
                    turn_block(g - 1)
                    block_up(g, 1 - j)
                    turn_rows(g + 1, j, 16 * i + 32)
                    block_down(g - 1)
            turn_block(2 * np_)
            block_down(2 * np_)

        @block.scalar
        def _(act):
            for p in range(2):
                act.sem_inc(s_bank_emptied[p], 1)
            act.sem_inc(s_x_copied, 2)
            act.sem_inc(s_i_ready, 1)
            act.sem_inc(s_a_ready, 1)
            act.sem_inc(s_probs_copied, 2)
            act.sem_inc(s_outs_copied, 2)
            act.sem_inc(s_o_copied, 2)
            act.sem_inc(s_h2_copied, 2)
            for dst, r0, src in vector_rows():
                if dst is vr0:
                    act.dma_start(dst[r0:r0 + src.shape[0], :], src).then_inc(s_vectors_loaded, 16)

            def rms_of(src, q, s_in, s_sq, s_rt, n):
                for t in (2 * q, 2 * q + 1):
                    if s_in is not None:
                        act.wait_ge(s_in, t + 1)
                    act.activation(junk[:, :], src[:, t, :], ACT.Square, accum_out=ss[:, t:t + 1]).then_inc(s_sq, 1)
                    act.wait_ge(s_sq, n + t % 2 + 1)
                act.activation(rms[:, 2 * q:2 * q + 2], ss[:, 2 * q:2 * q + 2], ACT.Sqrt, scale=1.0 / D,
                               bias=eps[:, 0:1]).then_inc(s_rt, 1)

            act.wait_ge(s_const_ready, 1)
            act.wait_ge(s_act_input, 1)
            for q in range(TT // 2):
                act.wait_ge(s_x_loaded[q], 16)
                rms_of(XS, q, None, s_x_squared, s_x_rms, 2 * q)
            act.wait_ge(s_vectors_turned, 1)
            act.activation(vc0[:, :], PS[:, 4, 0:P], ACT.Copy).then_inc(s_columns_copied, 1)
            act.activation(vc1[:, :], PS[:, 5, 0:3 * KT + 1], ACT.Copy).then_inc(s_columns_copied, 1)
            act.wait_ge(s_columns_copied, 1)
            act.activation(cond[:, :], ccol[:, :], ACT.Silu).then_inc(s_cond_ready, 1)
            for t in range(TT):
                act.wait_ge(s_x_turned, t + 1)
                act.activation(hT[:, :, t * P:(t + 1) * P], pair3(t % 2), ACT.Copy).then_inc(s_x_copied, 1)
            act.wait_ge(s_act_input, 2)
            act.activation(spt[:, 0:KT], spt[:, KT:2 * KT], ACT.Exp).then_inc(s_exps_done, 1)
            act.wait_ge(s_act_input, 4)
            act.activation(ls[:, 2:4], ls[:, 0:2], ACT.Exp).then_inc(s_exps_done, 1)
            with act.Fori(0, 2) as i:
                for j in range(4):
                    n = 4 * i + j
                    act.wait_ge(s_units_mul, U_XR + n + 1)
                    hold(act, s_conv_done, n + 1)
                    act.activation(xpad[:, j % 2, 4:4 + T], pair(j % 2), ACT.Copy).then_inc(s_bank_emptied[j % 2], 1)
            act.wait_ge(s_lam_spread, 1)
            act.activation(nlam[:, :], PS[:, 6, 0:1], ACT.Copy, scale=-1.0).then_inc(s_nlam_ready, 1)
            with act.Fori(0, 2) as i:
                for j in range(4):
                    n = 4 * i + j
                    act.wait_ge(s_gates_mul, n + 5)
                    hold(act, s_a_ready, n + 1)
                    act.activation(rT[:, :], pair(2), ACT.Sigmoid, bias=ba[:, ds(n, 1)]).then_inc(s_r_ready, 1)
                    hold(act, s_r_ready, n + 1)
                    act.activation(tT[:, :], rT[:, :], ACT.Tanh, scale=sp8[:, ds(n, 1)]).then_inc(s_tanh_ready, 1)
                    hold(act, s_yr_ready, n + 1)
                    act.activation(iT[:, :], pair(3), ACT.Sigmoid, bias=bx[:, ds(n, 1)]).then_inc(s_i_ready, 1)
                    act.activation(aT[:, :], rT[:, :], ACT.Exp, scale=nsp8[:, ds(n, 1)]).then_inc(s_a_ready, 1)
                    hold(act, s_units_mul, U_GR + n + 1)
                    act.activation(geT[:, :], pair(j % 2), ACT.Gelu_apprx_tanh).then_inc(s_bank_emptied[j % 2], 1)
                    hold(act, s_m2_ready, n + 1)
                    act.activation(mT[:, :], mT[:, :], ACT.Sqrt).then_inc(s_m_ready, 1)
            with act.Fori(0, 2) as i:
                for j in range(4):
                    n = 4 * i + j
                    hold(act, s_units_mul, U_GA + n + 1)
                    act.activation(gT[:, ds(n, 1), :].rearrange("p o n -> p (o n)"), pair(j % 2), ACT.Sigmoid)\
                        .then_inc(s_bank_emptied[j % 2], 1)
            act.wait_ge(s_ada_used, 2 + 12)
            for k in range(KT):
                act.activation(hTexact[:, k, :], hT[:, k, :], ACT.Copy).then_inc(s_vh, 1)
            act.wait_ge(s_mod_summed, 12)
            act.wait_ge(s_half_loaded, 64)
            for j in range(4):
                act.activation(VWh[0][:, j, :, :], WV[:, j, :, :], ACT.Copy).then_inc(s_vh, 1)
            for j in range(4):
                act.wait_ge(s_w_loaded[j], 16 * (1 + U_V // 4))
                act.activation(VWh[1][:, j, :, :], WT[:, j, :, :], ACT.Copy).then_inc(s_vh, 1)
            with act.Fori(0, 2) as i:
                for q in range(4):
                    hold(act, s_units_mul, U_V + 4 * i + q + 1)
                    act.activation(V[:, 2 * q:2 * q + 2, ds(i * HALF, HALF)], PS[:, 2 * (q % 2):2 * (q % 2) + 2, :],
                                   ACT.Copy).then_inc(s_bank_emptied[q % 2], 1)
            act.wait_ge(s_units_mul, U_QK + 1)
            act.activation(qT[:, 0, :], pair(0), ACT.Copy).then_inc(s_bank_emptied[0], 1)
            with act.Fori(0, NH // 2) as i:
                for b in range(2):
                    h = 2 * i + b
                    hold(act, s_units_mul, U_QK + 2 * h + 2)
                    act.activation(kT[:, b, :], pair(1), ACT.Copy).then_inc(s_bank_emptied[1], 1)

                    def exps(qt):
                        L = (qt + 1) * P
                        for c in range(2):
                            hold(act, s_bank_emptied[c], EV_ATT + EV_PER_HEAD * h + 1 + qt + 1)
                            s = SM[:, qt % 2, c, 0:L]
                            m = 2 * (qt % 2) + c
                            act.activation(s, s, ACT.Exp, scale=-1.0, bias=mn[:, m:m + 1],
                                           accum_out=lsum[:, m:m + 1]).then_inc(s_exps_ready, 1)

                    def turned(qt):
                        hold(act, s_values_mul, 8 * h + qt + 1)
                        for g in range(qt // 4 + 1):
                            G = group(qt) + g
                            nb = min(4, qt + 1 - 4 * g)
                            hold(act, s_probs_turned, 12 * h + G + 1)
                            act.activation(PT[:, qt % 2, 4 * g:4 * g + nb, :].rearrange("p k n -> p (k n)"),
                                           PS[:, 6 + G % 2, 0:nb * P], ACT.Copy).then_inc(s_probs_copied, 1)

                    def outs(qt):
                        hold(act, s_values_mul, 8 * h + qt + 3)
                        scale = rl[:, 2 * (qt % 2):2 * (qt % 2) + 1]
                        act.activation(ON[:, qt, ds(h * P, P)], PS[:, 4 + qt % 2, 0:P], ACT.Copy, scale=scale)
                        act.activation(osq[:, qt % 2, :], PS[:, 4 + qt % 2, 0:P], ACT.Square, scale=scale,
                                       accum_out=ssn[:, ds(qt * NH + h, 1)]).then_inc(s_outs_copied, 1)

                    exps(0)
                    for qt in range(TT):
                        if qt + 1 < TT:
                            exps(qt + 1)
                        else:
                            hold(act, s_units_mul, U_QK + 2 * h + 3)
                            act.activation(qT[:, 1 - b, :], pair(0), ACT.Copy).then_inc(s_bank_emptied[0], 1)
                        turned(qt)
                        if qt >= 1:
                            outs(qt - 1)
                    outs(TT - 1)
            act.wait_ge(s_outs_copied, 8 * NH + 2)
            act.wait_ge(s_bank_emptied[0], EV_ATT + NH * EV_PER_HEAD + 1)
            act.activation(sg[:, 0, :], qT[:, 0, :], ACT.Sigmoid)
            act.activation(ssn[:, :], ssn[:, :], ACT.Sqrt, scale=1.0 / P, bias=eps[:, 0:1]).then_inc(s_head_rms, 1)

            def gate_b(i, j):
                n = 2 * i + j
                act.wait_ge(s_units_mul, U_GB + 2 * n + 1)
                hold(act, s_merged, n + 1)
                act.activation(sg[:, j, :], pair(0), ACT.Sigmoid).then_inc(s_bank_emptied[0], 1)

            with act.Fori(0, TT // 2) as i:
                for b in range(2):
                    t = 2 * i + b
                    hold(act, s_o_turned, t + 1)
                    act.activation(tcols(oT, t), pair3(2 + b), ACT.Copy, scale=gsub8[:, 0:1]).then_inc(s_o_copied, 1)
            gate_b(0, 1)
            with act.Fori(1, 4) as i:
                for j in range(2):
                    gate_b(i, j)
            for r in range(4):
                act.wait_ge(s_row_spread, r + 1)
                act.activation(ROWS[:, r, :], pair(2 + r % 2), ACT.Copy).then_inc(s_rows_ready, 1)

            def out_rows(i, q):
                act.wait_ge(s_units_mul, U_O + 4 * i + q + 1)
                act.activation(Y[:, 2 * q:2 * q + 2, i * HALF:(i + 1) * HALF],
                               PS[:, 2 * (q % 2):2 * (q % 2) + 2, :], ACT.Copy).then_inc(s_bank_emptied[q % 2], 1)

            def h2_turned(q):
                for t in (2 * q, 2 * q + 1):
                    act.wait_ge(s_h2_turned, t + 1)
                    act.activation(hT[:, :, t * P:(t + 1) * P], pair3(2 + t % 2), ACT.Copy).then_inc(s_h2_copied, 1)

            for q in range(4):
                out_rows(0, q)
            E1 = EV_ATT + NH * EV_PER_HEAD + (U_O - U_GB) // 2
            for q in range(4):
                out_rows(1, q)
                act.wait_ge(s_bank_emptied[q % 2], E1 + 2 + q // 2 + 1)
                rms_of(Y, q, None, s_y_squared, s_y_rms, 4 * q - 2 * min(q, 1))
                if q >= 1:
                    rms_of(Y, q - 1, s_x1_ready, s_y_squared, s_y_rms, 4 * q)
                if q >= 2:
                    h2_turned(q - 2)
            rms_of(Y, 3, s_x1_ready, s_y_squared, s_y_rms, 14)
            h2_turned(2)
            h2_turned(3)
            act.sem_inc(ro["ya"], 1)

            def hidden_act(S, g, b):
                hold(act, S["up"], g + 1)
                act.activation(sgm[:, b, :], PS[:, 2 + b, 0:FE], ACT.Sigmoid).then_inc(S["sg"], 1)

            def hidden_turned(S, g, b):
                hold(act, S["hT"], g + 1)
                act.activation(hbT[:, b, :, :].rearrange("p f n -> p (f n)"), PS[:, 6, 0:FE], ACT.Copy)\
                    .then_inc(S["he"], 1)

            act.wait_ge(s_lg, TT)
            act.activation(sco[:, :, :].rearrange("p t e -> p (t e)"), PS[:, 7, :], ACT.Sigmoid).then_inc(s_sco, 1)
            for t in range(2):
                hidden_act(sh, t, t)
            for t in range(TT):
                hidden_turned(sh, t, t % 2)
                if 1 <= t < TT - 1:
                    hidden_act(sh, t + 1, (t + 1) % 2)
                act.wait_ge(sh["dn"], t + 1)
                if t >= 2:
                    act.wait_ge(s_shared_stored[t % 2], 16 * (t // 2))
                act.activation(yo[:, t % 2, 0:HALF], PS[:, 4, :], ACT.Copy).then_inc(sh["ya"], 1)
            act.wait_ge(s_table_turned, 2)
            act.activation(tokT[:, 0:P], PS[:, 0, 0:P], ACT.Copy).then_inc(s_table_copied, 1)
            act.activation(wtT[:, :], PS[:, 1, 0:P], ACT.Copy).then_inc(s_table_copied, 1)
            act.wait_ge(s_table_copied, 2)
            act.wait_ge(s_blocks_ready, 2)
            for b in range(2):
                act.wait_ge(s_shared_stored[b], 16 * TT // 2)
            np1 = act.value_load(pendi[0:1, NE + 1:NE + 2], min_val=1, max_val=NBLK // 2 - 2)

            act.wait_ge(s_blocks_loaded, 16)

            def regs(g):
                return expert_raw(act, g), expert_loads(act, g)

            def loaded(sems, loads, per):
                for q, n in enumerate(loads):
                    hold(act, sems[q], per * n)

            def up_exact(e, b, cs, free=None):
                par, loads = e
                if 0 in cs:
                    loaded(s_up_loaded, loads, 32)
                if free is not None:
                    hold(act, ro["up"], free)
                for c in cs:
                    act.activation(W13h[:, b, 2 * c:2 * c + 2, :],
                                   W13[:, ds(par, 1), 2 * c:2 * c + 2, :].rearrange("p o k n -> p (o k) n"), ACT.Copy)\
                        .then_inc(s_wh, 1)

            def down_exact(e, g):
                par, loads = e
                loaded(s_down_loaded, loads, 16)
                hold(act, ro["dn"], g + 1)
                for f in range(FT):
                    act.activation(W2h[:, f, :], W2[:, ds(par, 1), f, :].rearrange("p o n -> p (o n)"), ACT.Copy)\
                        .then_inc(s_w2h, 1)

            def rows_exact(g):
                hold(act, s_rows_turned, g + 1)
                for half in range(2):
                    act.activation(xTh[:, 4 * half:4 * half + 4, :].rearrange("p k n -> p (k n)"), PS[:, half, :],
                                   ACT.Copy).then_inc(s_xh, 1)

            def gate_block(g, b):
                hold(act, ro["up"], g + 1)
                act.activation(sgr[:, :], PS[:, 2 + b, 0:FE], ACT.Sigmoid).then_inc(ro["sg"], 1)

            def hidden_exact(g):
                hold(act, ro["hT"], g + 1)
                act.activation(hTh[:, :, :].rearrange("p f n -> p (f n)"), PS[:, 6, 0:FE], ACT.Copy).then_inc(s_hh, 1)

            def outputs(g, b, done):
                hold(act, ro["dn"], g + 2)
                hold(act, ro["st"], done)
                act.activation(yo[:, b, :], pair(2), ACT.Copy, scale=wtT[:, ds(g, 1)]).then_inc(ro["ya"], 1)

            up_exact(regs(0), 0, range(4))
            rows_exact(0)
            gate_block(0, 0)
            up_exact(regs(1), 1, range(3))

            def tail(g, b, more=True):
                down, here = regs(g), expert_raw(act, g + 1)
                up_ = regs(g + 2) if more else None
                gate_block(g, b)
                rows_exact(g + 1)
                up_exact((here, None), 1 - b, [3])
                hidden_exact(g)
                down_exact(down, g)
                if more:
                    up_exact(up_, b, [0], g + 1)
                outputs(g - 1, 1 - b, 16 * g)
                if more:
                    up_exact(up_, b, [1, 2])

            rows_exact(1)
            up_exact((expert_raw(act, 1), None), 1, [3])
            hidden_exact(0)
            down_exact(regs(0), 0)
            up_exact(regs(2), 0, range(3), 1)
            with act.Fori(0, np1) as i:
                for j in range(2):
                    tail(2 * i + j + 1, 1 - j)
            tail(2 * np1 + 1, 1)
            tail(2 * np1 + 2, 0, more=False)
            outputs(2 * np1 + 2, 0, 32 * np1 + 48)
            for t in range(TT):
                act.wait_ge(s_sum_loaded[t], 16)
                act.activation(junk[:, :], FS[:, t, :], ACT.Square, accum_out=ss[:, t:t + 1]).then_inc(s_sum_squared, 1)
                act.wait_ge(s_sum_squared, t + 1)
                if t % 2:
                    act.activation(rms[:, t - 1:t + 1], ss[:, t - 1:t + 1], ACT.Sqrt, scale=1.0 / D,
                                   bias=eps[:, 0:1]).then_inc(s_sum_rms, 1)

        @block.vector
        def _(dve):
            stt = dve.scalar_tensor_tensor
            dve.sem_inc(s_conv_done, 2)
            dve.sem_inc(s_yr_ready, 1)
            dve.sem_inc(s_merged, 2)
            dve.sem_inc(s_ada_used, 2)
            link = Link(dve, s_dve_step)
            dve.memset(eps[:, :], EPS).then_inc(s_act_input, 1)
            for q in range(TT // 2):
                dve.wait_ge(s_x_rms, q + 1)
                link(dve.reciprocal(rstd[:, 2 * q:2 * q + 2], rms[:, 2 * q:2 * q + 2]))
                for t in (2 * q, 2 * q + 1):
                    dve.tensor_scalar(XS[:, t, :], XS[:, t, :], rstd[:, t:t + 1], None, ALU.mult)\
                        .then_inc(s_x_normed, 1)

            def ada(i, bufs, ready, into):
                for k in range(KT):
                    for b in range(2):
                        acc_ = AA[:, ds(into + b, 1), :].rearrange("p o n -> p (o n)")
                        w = AW[:, bufs[b], k, :]
                        if k == 0:
                            dve.wait_ge(s_ada_loaded[bufs[b]], ready)
                            ins = dve.tensor_scalar(acc_, w, cond[:, 0:1], None, ALU.mult)
                        else:
                            hold(dve, s_ada_partial, 2 * (KT - 1) * i + 2 * (k - 1) + b + 1)
                            ins = stt(out=acc_, in0=w, scalar=cond[:, k:k + 1], in1=acc_, op0=ALU.mult, op1=ALU.add)
                        ins.then_inc(s_ada_partial if k < KT - 1 else s_ada_summed, 1)
                for b in range(2):
                    dve.wait_ge(s_ada_summed, 2 * i + b + 1)
                    dve.sem_inc(s_ada_used, 1)

            dve.wait_ge(s_cond_ready, 1)
            for i in range(2):
                ada(i, (2 * i, 2 * i + 1), 16, 2 * i)
            dve.wait_ge(s_mod_summed, 4)
            dve.tensor_tensor(mod[:, 0:16], PS[:, MODB, 0:16], bada[:, 0:16], ALU.add).then_inc(s_mod1_ready, 1)
            dve.wait_ge(s_mod1_ready, 1)
            link(stt(out=a1[:, :], in0=mod[:, KT:2 * KT], scalar=1.0, in1=gpm[:, :], op0=ALU.add, op1=ALU.mult))
            dve.wait_ge(s_x_copied, TT + 2)
            for k in range(KT):
                dve.tensor_scalar(hT[:, k, :], hT[:, k, :], a1[:, k:k + 1], mod[:, k:k + 1], ALU.mult, ALU.add)\
                    .then_inc(s_h_ready, 1)
            dve.wait_ge(s_vectors_loaded, 16 * N_SMALL)
            dve.wait_ge(s_columns_copied, 2)
            link(dve.tensor_scalar(spt[:, KT:2 * KT], lamc[:, :], -1.0, None, ALU.mult), wait=True)
            dve.tensor_tensor(spt[:, KT:2 * KT], spt[:, KT:2 * KT], lamc[:, :], ALU.min).then_inc(s_act_input, 1)
            for j in range(2):
                dve.tensor_tensor_reduce(out=lpr[:, :], in0=lqk[:, 2 * j * HD:(2 * j + 1) * HD],
                                         in1=lqk[:, (2 * j + 1) * HD:(2 * j + 2) * HD], scale=1.0, scalar=0.0,
                                         op0=ALU.mult, op1=ALU.add, accum_out=ls[:, j:j + 1]).then_inc(s_act_input, 1)
                dve.wait_ge(s_act_input, 3 + j)
            dve.wait_ge(s_exps_done, 1)
            e, w, w2, poly = (spt[:, j * KT:(j + 1) * KT] for j in range(4))
            link(dve.tensor_scalar(w, e, 2.0, None, ALU.add))
            link(dve.reciprocal(w, w))
            link(dve.tensor_tensor(w, w, e, ALU.mult))
            link(dve.tensor_tensor(w2, w, w, ALU.mult))
            link(dve.memset(poly, 1.0 / 19))
            for m in range(8, -1, -1):
                link(dve.tensor_tensor(poly, poly, w2, ALU.mult))
                link(dve.tensor_scalar(poly, poly, 1.0 / (2 * m + 1), None, ALU.add))
            link(stt(out=poly, in0=poly, scalar=2.0, in1=w, op0=ALU.mult, op1=ALU.mult))
            link(dve.tensor_scalar(w2, lamc[:, :], -1.0, 0.0, ALU.mult, ALU.max))
            link(dve.tensor_tensor(w2, w2, poly, ALU.add))
            link(dve.tensor_scalar(sp8[:, :], w2, LRU_C, None, ALU.mult), wait=False)
            link(dve.tensor_scalar(nsp8[:, :], w2, -LRU_C, None, ALU.mult), wait=False)
            link(dve.tensor_scalar(gsub8[:, :], gsub[:, :], 1.0 - LAM_INIT, None, ALU.mult), wait=False)
            dve.wait_ge(s_exps_done, 2)
            link(dve.tensor_tensor(ls[:, 5:6], ls[:, 2:3], ls[:, 3:4], ALU.subtract))
            dve.tensor_scalar(ls[:, 4:5], ls[:, 5:6], LAM_INIT, None, ALU.add).then_inc(s_lam_ready, 1)

            for b in range(2):
                link(dve.memset(xpad[:, b, 0:4], 0.0), wait=(b == 1))
            lc = Link(dve, s_conv_step, 0, 4 * 3)
            with dve.Fori(0, 2) as i:
                lc.at(i)
                for j in range(4):
                    n = 4 * i + j
                    hold(dve, s_bank_emptied[j % 2], U_XR // 2 + 2 * i + j // 2 + 2)
                    y = xcT[:, ds(n, 1), :].rearrange("p o n -> p (o n)")
                    lc(dve.tensor_scalar(y, xpad[:, j % 2, 4:4 + T], cw[:, ds(3 * KT + n, 1)], cb[:, ds(n, 1)],
                                         ALU.mult, ALU.add))
                    for tap in (2, 1, 0):
                        ins = stt(out=y, in0=xpad[:, j % 2, 1 + tap:1 + tap + T], scalar=cw[:, ds(tap * KT + n, 1)],
                                  in1=y, op0=ALU.mult, op1=ALU.add)
                        if tap:
                            lc(ins)
                        else:
                            ins.then_inc(s_conv_done, 1)
            lg = Link(dve, s_lru_step, 0, 4 * 6)
            with dve.Fori(0, 2) as i:
                lg.at(i)
                for j in range(4):
                    n = 4 * i + j
                    y = xcT[:, ds(n, 1), :].rearrange("p o n -> p (o n)")
                    hold(dve, s_tanh_ready, n + 1)
                    hold(dve, s_yr_ready, n + 1)
                    lg(dve.tensor_scalar(hsT[:, :], tT[:, :], 1.0, None, ALU.add))
                    lg(dve.reciprocal(hsT[:, :], hsT[:, :]))
                    stt(out=mT[:, :], in0=tT[:, :], scalar=2.0, in1=hsT[:, :], op0=ALU.mult, op1=ALU.mult)\
                        .then_inc(s_m2_ready, 1)
                    hold(dve, s_i_ready, n + 2)
                    lg(dve.tensor_tensor(ixT[:, :], iT[:, :], y, ALU.mult), wait=False)
                    hold(dve, s_m_ready, n + 1)
                    lg(dve.memset(mT[:, 0:1], 1.0))
                    lg(dve.tensor_tensor(ixT[:, :], ixT[:, :], mT[:, :], ALU.mult))
                    hold(dve, s_a_ready, n + 2)
                    lg(dve.tensor_tensor_scan(out=hsT[:, :], data0=aT[:, :], data1=ixT[:, :], initial=0.0,
                                              op0=ALU.mult, op1=ALU.add))
                    hold(dve, s_bank_emptied[j % 2], U_GR // 2 + 2 * i + j // 2 + 2)
                    dve.tensor_tensor(y, hsT[:, :], geT[:, :], ALU.mult).then_inc(s_yr_ready, 1)
            with dve.Fori(2, 6) as i:
                ada(i, (0, 1), 16 * i, 2 * i - 4)
            def rest(out_, whole, exact, s):
                dve.tensor_tensor(out_, whole, exact.bitcast(fp32), ALU.subtract).then_inc(s, 1)

            dve.wait_ge(s_units_mul, U_YA)
            for k in range(KT):
                dve.wait_ge(s_vh, k + 1)
                rest(hTrest[:, k, :], hT[:, k, :], hTexact[:, k, :], s_vl)
            for j in range(4):
                dve.wait_ge(s_vh, KT + j + 1)
                rest(VWl[0][:, j, :, :], WV[:, j, :, :], VWh[0][:, j, :, :], s_vl)
            with dve.Fori(0, 2) as i:
                for j in range(4):
                    n = 4 * i + j
                    g = gT[:, ds(n, 1), :].rearrange("p o n -> p (o n)")
                    hold(dve, s_units_mul, U_YA + n + 1)
                    dve.tensor_tensor(g, g, pair(j % 2), ALU.mult).then_inc(s_bank_emptied[j % 2], 1)

            dve.wait_ge(s_mod_summed, 12)
            dve.tensor_tensor(mod[:, 16:48], PS[:, MODB, 16:48], bada[:, 16:48], ALU.add).then_inc(s_mod2_ready, 1)
            dve.wait_ge(s_mod2_ready, 1)
            link(dve.tensor_tensor(rows_c[:, 0:8], mod[:, 16:24], gpo[:, :], ALU.mult), wait=False)
            link(stt(out=rows_c[:, 8:16], in0=mod[:, 32:40], scalar=1.0, in1=gpf[:, :], op0=ALU.add, op1=ALU.mult),
                 wait=False)
            link(dve.tensor_copy(rows_c[:, 16:24], mod[:, 24:32]), wait=False)
            link(dve.tensor_tensor(rows_c[:, 24:32], mod[:, 40:48], gpo2[:, :], ALU.mult))

            for j in range(4):
                dve.wait_ge(s_vh, KT + 4 + j + 1)
                rest(VWl[1][:, j, :, :], WT[:, j, :, :], VWh[1][:, j, :, :], s_vl)
            dve.wait_ge(s_units_mul, U_QK)
            for k in range(KT):
                dve.tensor_tensor(hT[:, k, :], hTrest[:, k, :].bitcast(fp32), hTexact[:, k, :].bitcast(fp32), ALU.add)\
                    .then_inc(s_h_ready, 1)

            la = Link(dve, s_att_step, 0, 2 * (2 + 16))
            with dve.Fori(0, NH // 2) as i:
                la.at(i)
                for b in range(2):
                    h = 2 * i + b
                    la(dve.tensor_scalar(B8[:, :], R[:, :], SL[:, ds(h, 1)], None, ALU.mult))
                    la(dve.tensor_tensor(B8[:, T - P:T], B8[:, T - P:T], MASK[:, :], ALU.add))

                    def soft(qt):
                        L = (qt + 1) * P
                        for c in range(2):
                            m = 2 * (qt % 2) + c
                            hold(dve, s_scores_ready, 16 * h + 2 * qt + c + 1)
                            if qt >= 2:
                                hold(dve, s_probs_turned, 12 * h + group(qt - 1))
                            dve.tensor_tensor_reduce(out=SM[:, qt % 2, c, 0:L], in0=pair(c)[:, 0:L],
                                                     in1=B8[:, T - L:T], scale=-HD ** -0.5, scalar=3e38,
                                                     op0=ALU.add, op1=ALU.min,
                                                     accum_out=mn[:, m:m + 1]).then_inc(s_bank_emptied[c], 1)

                    def merge(qt):
                        L = (qt + 1) * P
                        q = 2 * (qt % 2)
                        dve.wait_ge(s_exps_ready, 16 * h + 2 * qt + 2)
                        hold(dve, s_outs_copied, 8 * h + qt + 1)
                        la(dve.reciprocal(rl[:, q:q + 2], lsum[:, q:q + 2]))
                        la(dve.tensor_scalar(c1[:, qt % 2:qt % 2 + 1], rl[:, q + 1:q + 2], nlam[:, 0:1],
                                             lsum[:, q:q + 1], ALU.mult, ALU.mult))
                        stt(out=SM[:, qt % 2, 0, 0:L], in0=SM[:, qt % 2, 1, 0:L], scalar=c1[:, qt % 2:qt % 2 + 1],
                            in1=SM[:, qt % 2, 0, 0:L], op0=ALU.mult, op1=ALU.add).then_inc(s_probs_ready, 1)

                    soft(0)
                    for qt in range(TT):
                        merge(qt)
                        if qt + 1 < TT:
                            soft(qt + 1)

            dve.wait_ge(s_head_rms, 1)
            link(dve.reciprocal(ssn[:, :], ssn[:, :]))
            with dve.Fori(0, TT // 2) as i:
                for b in range(2):
                    t = 2 * i + b
                    hold(dve, s_o_copied, t + 1)
                    dve.tensor_tensor(on2[:, b, :].rearrange("p (h n) -> p h n", h=NH),
                                      ON[:, ds(t, 1), :].rearrange("p o (h n) -> p (o h) n", h=NH),
                                      ssn[:, ds(t * NH, NH)].rearrange("p (h o) -> p h o", o=1)
                                      .broadcast_to([P, NH, P]), ALU.mult).then_inc(s_o_normed, 1)

            def diagonals(r):
                if r >= 2:
                    dve.wait_ge(s_row_spread, r - 1)
                for k in range(KT):
                    dve.tensor_scalar(dg[:, r % 2, k, :], ident[:, :], rows_c[:, r * KT + k:r * KT + k + 1], None,
                                      ALU.mult).then_inc(s_diag_ready, 1)

            diagonals(0)
            diagonals(1)
            lm = Link(dve, s_merge_step, 0, 2)
            with dve.Fori(0, 4) as i:
                lm.at(i)
                for j in range(2):
                    n = 2 * i + j
                    g = gT[:, ds(n, 1), :].rearrange("p o n -> p (o n)")
                    dve.wait_ge(s_units_mul, U_GB + 2 * n + 2)
                    dve.wait_ge(s_merged, n + 2)
                    hold(dve, s_bank_emptied[0], EV_ATT + NH * EV_PER_HEAD + n + 1)
                    dve.tensor_tensor(ty[:, :], sg[:, j, :], pair(1), ALU.mult).then_inc(s_bank_emptied[1], 1)
                    hold(dve, s_bank_emptied[1], EV_ATT + NH * EV_PER_HEAD + n + 1)
                    dve.tensor_tensor(g, g, ty[:, :], ALU.add).then_inc(s_merged, 1)
            diagonals(2)
            diagonals(3)
            dve.wait_ge(s_rows_ready, 4)
            for q in range(TT // 2):
                dve.wait_ge(s_x_loaded[q], 32)

            def residual(q, turn):
                dve.wait_ge(s_y_rms, turn)
                link(dve.reciprocal(rstd[:, 2 * q:2 * q + 2], rms[:, 2 * q:2 * q + 2]))
                for t in (2 * q, 2 * q + 1):
                    link(stt(out=Y[:, t, :], in0=Y[:, t, :], scalar=rstd[:, t:t + 1], in1=ROWS[:, 0, :],
                           op0=ALU.mult, op1=ALU.mult))
                    dve.tensor_tensor(Y[:, t, :], Y[:, t, :], XS[:, t, :], ALU.add).then_inc(s_x1_ready, 1)

            def modulated(q, turn):
                dve.wait_ge(s_y_rms, turn)
                link(dve.reciprocal(rstd[:, 2 * q:2 * q + 2], rms[:, 2 * q:2 * q + 2]))
                for t in (2 * q, 2 * q + 1):
                    link(stt(out=h2t[:, t, :], in0=Y[:, t, :], scalar=rstd[:, t:t + 1], in1=ROWS[:, 1, :],
                           op0=ALU.mult, op1=ALU.mult))
                    dve.tensor_tensor(h2t[:, t, :], h2t[:, t, :], ROWS[:, 2, :], ALU.add).then_inc(s_h2_ready, 1)

            residual(0, 1)
            for q in range(1, TT // 2):
                residual(q, 2 * q)
                modulated(q - 1, 2 * q + 1)
            modulated(TT // 2 - 1, 2 * (TT // 2))
            lr = Link(dve, s_route_step)
            dve.wait_ge(s_ld, 48)
            dve.wait_ge(s_c2, 13)

            def over(ap, n, last):
                m = ap.shape[1]
                if last:
                    return ap.rearrange("p (o m) -> p o m", o=1).broadcast_to([P, n, m])
                return ap.rearrange("p (m o) -> p m o", o=1).broadcast_to([P, m, n])

            tiles = range(TT)

            def each(op, ns=tiles):
                for n in ns:
                    lr(op(n), wait=False)
                lr.wait()

            def eight(buf, t):
                return buf[:, 8 * t:8 * t + 8]

            dve.wait_ge(s_sco, 1)
            each(lambda t: dve.tensor_tensor(cho[:, t, :], sco[:, t, :], ebias[:, :], ALU.add))
            each(lambda n: dve.max(g8[:, n, :], cho[:, n // NG, n % NG * 8:n % NG * 8 + 8]), range(TT * NG))
            lr(dve.tensor_tensor(gs[:, :], g8[:, :, 0], g8[:, :, 1], ALU.add))
            each(lambda t: dve.max(eight(gv, t), eight(gs, t)))
            each(lambda t: dve.max_index(eight(gi, t), eight(gv, t), eight(gs, t)))
            lr(dve.tensor_copy(gif[:, :], gi[:, :]))
            each(lambda t: dve.tensor_tensor(gm4[:, t, :, :], over(io64[:, 0:NG], TOPG, True),
                                             over(gif[:, 8 * t:8 * t + TOPG], NG, False), ALU.is_equal))
            each(lambda t: dve.tensor_reduce(eight(gmk, t), gm4[:, t, :, :].rearrange("p k g -> p g k"), AX.X, ALU.add))
            lr(dve.tensor_scalar(gmk[:, :], gmk[:, :], -1.0, -MASKED, ALU.add, ALU.mult))
            c3 = cho[:, :, :].rearrange("p t (g n) -> p (t g) n", g=NG)
            lr(dve.tensor_tensor(c3, c3, over(gmk[:, :], NE // NG, False), ALU.add))
            each(lambda t: dve.max(eight(v8, t), cho[:, t, :]))
            each(lambda t: dve.max_index(eight(i8, t), eight(v8, t), cho[:, t, :]))
            lr(dve.tensor_copy(idxf[:, :], i8[:, :]))

            def hot(t):
                return oh[:, TOP * t:TOP * (t + 1), :]

            def hot2(t):
                return oh2[:, TOP * t:TOP * (t + 1), :]

            for b in range(2):
                dve.wait_ge(s_h2_stored[b], 16 * (TT // 2))
            each(lambda t: dve.tensor_tensor(hot(t), over(io64[:, :], TOP, True), over(eight(idxf, t), NE, False),
                                             ALU.is_equal))
            for t in tiles:
                dve.tensor_reduce(M[:, t, :], hot(t).rearrange("p k e -> p e k"), AX.X, ALU.add).then_inc(s_M, 1)
            def hidden(S, g, b):
                hold(dve, S["sg"], g + 1)
                dve.tensor_tensor(sgm[:, b, :], sgm[:, b, :], PS[:, 2 + b, 0:FE], ALU.mult).then_inc(S["t"], 1)
                hold(dve, S["t"], g + 1)
                dve.tensor_tensor(hb[:, b, :], sgm[:, b, :], PS[:, 2 + b, FE:2 * FE], ALU.mult).then_inc(S["hb"], 1)

            each(lambda t: dve.tensor_tensor(hot2(t), hot(t), over(sco[:, t, :], TOP, True), ALU.mult))
            each(lambda t: dve.tensor_reduce(eight(w8, t), hot2(t), AX.X, ALU.add))
            lr(dve.tensor_reduce(wsm[:, :], w8[:, :].rearrange("p (t k) -> p t k", k=TOP), AX.X, ALU.add))
            lr(dve.tensor_scalar(wsm[:, :], wsm[:, :], 1e-20, None, ALU.add))
            lr(dve.reciprocal(wsm[:, :], wsm[:, :]))
            pw = pairs[:, :].rearrange("p (t k c) -> p t k c", t=TT, k=TOP)
            each(lambda t: dve.tensor_scalar(pw[:, t, :, 1], eight(w8, t), wsm[:, t:t + 1], ROUTED_SCALE,
                                             ALU.mult, ALU.mult))
            for t in range(2):
                hidden(sh, t, t)
            dve.wait_ge(s_rk, 1)
            cmp = oh2[:, 0:8, :].rearrange("p k e -> p (k e)").rearrange("p (e k) -> p e k", k=8)
            lr(dve.tensor_copy(nbk[:, :], PS[:, 1, 0:NE]))
            lr(dve.tensor_tensor(cmp, over(nbk[:, :], 8, False), over(thr[:, :], NE, True), ALU.is_gt))
            lr(dve.tensor_reduce(nbk[:, :], cmp, AX.X, ALU.add))
            lr(dve.tensor_scalar(nbk[:, :], nbk[:, :], 1.0, None, ALU.add))
            lr(dve.tensor_tensor_scan(out=pend[:, :], data0=ones[:, 0:NE], data1=nbk[:, :], initial=0.0,
                                      op0=ALU.mult, op1=ALU.add))
            lr(dve.tensor_tensor(pst[:, :], pend[:, :], nbk[:, :], ALU.subtract))
            lr(dve.tensor_scalar(pst[:, :], pst[:, :], float(P), None, ALU.mult))
            each(lambda t: dve.tensor_tensor(pos[:, t, :], PS[:, 0, t * NE:(t + 1) * NE], pst[:, :], ALU.add))
            each(lambda t: dve.tensor_tensor(hot2(t), hot(t), over(pos[:, t, :], TOP, True), ALU.mult))
            each(lambda t: dve.tensor_reduce(eight(slotf, t), hot2(t), AX.X, ALU.add))
            dve.tensor_copy(slots[:, :], slotf[:, :]).then_inc(s_slot, 1)
            lr(dve.tensor_scalar(posab[:, :], pend[:, :], ioP[:, 0:1], None, ALU.is_le))
            lr(dve.tensor_reduce(eidf[:, :], posab[:, :], AX.X, ALU.add))
            lr(dve.tensor_scalar(eidf[:, :], eidf[:, :], float(NE - 1), None, ALU.min))
            lr(dve.tensor_scalar(ehi[:, :], eidf[:, :], 0.5, -0.25, ALU.mult, ALU.add))
            lr(dve.tensor_copy(ehf[:, :], ehi[:, :]))
            lr(stt(out=tbf[:, 0:1], in0=ehf[:, :], scalar=-2.0, in1=eidf[:, :], op0=ALU.mult, op1=ALU.add))
            lr(dve.tensor_scalar(tbf[:, 1:2], ehf[:, :], 1.0, None, ALU.add))
            lr(dve.tensor_tensor(tbf[:, 2:3], ehf[:, :], tbf[:, 0:1], ALU.add))
            lr(dve.tensor_scalar(tbf[:, 2:3], tbf[:, 2:3], 1.0, None, ALU.max))
            lr(dve.tensor_copy(tbf[:, 3:4], eidf[:, :]))
            lr(dve.tensor_scalar(npf[:, :], pend[:, NE - 1:NE], -0.5, 0.5, ALU.add, ALU.mult))
            lr(dve.tensor_copy(pendi[:, 0:NE], pend[:, :]))
            lr(dve.tensor_copy(pendi[:, NE:NE + 1], npf[:, :]))
            lr(dve.tensor_scalar(npf[:, :], npf[:, :], -1.0, None, ALU.add))
            lr(dve.tensor_copy(pendi[:, NE + 1:NE + 2], npf[:, :]))
            dve.tensor_copy(tbi[:, :], tbf[:, :]).then_inc(s_blocks_ready, 2)
            for t in range(TT):
                if 1 <= t < TT - 1:
                    hidden(sh, t + 1, (t + 1) % 2)
                dve.wait_ge(sh["dn"], t + 1)
                if t >= 2:
                    dve.wait_ge(s_shared_stored[t % 2], 16 * (t // 2))
                dve.tensor_copy(yo[:, t % 2, HALF:D], PS[:, 5, :]).then_inc(sh["yd"], 1)

            for b in range(2):
                dve.wait_ge(s_shared_stored[b], 16 * TT // 2)
            dve.wait_ge(s_blocks_ready, 2)
            np_ = dve.value_load(pendi[0:1, NE:NE + 1], min_val=1, max_val=NBLK // 2 - 1)

            dve.wait_ge(s_table_copied, 2)

            dve.wait_ge(s_blocks_loaded, 16)

            def up_rest(par, g, b, cs):
                for c in cs:
                    hold(dve, s_wh, 4 * g + c + 1)
                    k = slice(2 * c, 2 * c + 2)
                    rest(W13l[:, b, k, :], W13[:, ds(par, 1), k, :].rearrange("p o k n -> p (o k) n"), W13h[:, b, k, :],
                         s_wl)

            def down_rest(par, g):
                hold(dve, s_w2h, 2 * g + 1)
                rest(W2l[0][:, :], W2[:, ds(par, 1), 0, :].rearrange("p o n -> p (o n)"), W2h[:, 0, :], s_w2l)

            def rows_rest(g):
                for half in range(2):
                    hold(dve, s_xh, 2 * g + half + 1)
                    rest(xTl[:, 4 * half:4 * half + 4, :].rearrange("p k n -> p (k n)"), PS[:, half, :],
                         xTh[:, 4 * half:4 * half + 4, :].rearrange("p k n -> p (k n)"), s_xl)

            def hidden_block(g, b):
                hold(dve, ro["sg"], g + 1)
                dve.tensor_tensor(sgr[:, :], sgr[:, :], PS[:, 2 + b, 0:FE], ALU.mult).then_inc(ro["t"], 1)
                hold(dve, ro["t"], g + 1)
                dve.tensor_tensor(hbr[:, :], sgr[:, :], PS[:, 2 + b, FE:2 * FE], ALU.mult).then_inc(ro["hb"], 1)

            def hidden_rest(g):
                hold(dve, s_hh, g + 1)
                rest(hTl[:, :, :].rearrange("p f n -> p (f n)"), PS[:, 6, 0:FE],
                     hTh[:, :, :].rearrange("p f n -> p (f n)"), s_hl)

            up_rest(expert_raw(dve, 0), 0, 0, range(4))
            rows_rest(0)
            hidden_block(0, 0)
            up_rest(expert_raw(dve, 1), 1, 1, range(4))
            rows_rest(1)
            with dve.Fori(0, np_) as i:
                for j in range(2):
                    g = 2 * i + j + 1
                    down, up_ = expert_raw(dve, g - 1), expert_raw(dve, g + 1)
                    hidden_rest(g - 1)
                    down_rest(down, g - 1)
                    up_rest(up_, g + 1, j, range(2))
                    hidden_block(g, 1 - j)
                    rows_rest(g + 1)
                    up_rest(up_, g + 1, j, range(2, 4))
            hidden_rest(2 * np_)
            down_rest(expert_raw(dve, 2 * np_), 2 * np_)
            for t in range(TT):
                if t % 2 == 0:
                    dve.wait_ge(s_sum_rms, t // 2 + 1)
                    link(dve.reciprocal(rstd[:, t:t + 2], rms[:, t:t + 2]))
                link(stt(out=FS[:, t, :], in0=FS[:, t, :], scalar=rstd[:, t:t + 1], in1=ROWS[:, 3, :],
                       op0=ALU.mult, op1=ALU.mult))
                dve.tensor_tensor(FS[:, t, :], FS[:, t, :], Y[:, t, :], ALU.add).then_inc(s_out_ready, 1)


_INS = ["x", "c", "w_ada", "b_ada", "g_pre_mix", "w_in", "conv_w", "conv_b", "lru_wa", "lru_ba", "lru_wx", "lru_bx",
        "lru_lambda", "lam_q1", "lam_k1", "lam_q2", "lam_k2", "g_subln", "w_proj_rnn", "w_proj_att", "w_out",
        "g_post_mix", "g_pre_ffn", "w_router", "e_bias", "w1_e", "w3_e", "w2_e", "w1_s", "w3_s", "w2_s", "g_post_ffn"]


def kernel(**inputs):
    import numpy as _np
    import concourse.bacc as _bacc
    from concourse import mybir as _mybir
    from concourse.bass_utils import run_bass_kernel_spmd as _run

    nc = _bacc.Bacc("TRN2", target_bir_lowering=False, num_devices=1)
    arrays, args = {}, {}
    for name in _INS:
        v = _np.ascontiguousarray(inputs[name])
        arrays[f"in_{name}_dram"] = v
        args[name] = nc.dram_tensor(f"in_{name}_dram", v.shape, _mybir.dt.from_np(v.dtype), kind="ExternalInput").ap()
    out = nc.dram_tensor("out_0_dram", (1, T, D), _mybir.dt.from_np(_np.dtype("float32")), kind="ExternalOutput").ap()
    layer(nc, args, out)
    r = _run(nc, [arrays], core_ids=[0])
    return r.results[0]["out_0_dram"]
```
